# Optimizing a Trainium2 kernel written in Bass

```python
import math
import jax, jax.numpy as jnp
from jax import lax
import numpy as np

D_MODEL = 1024
BATCH = 1
SEQ = 256
DEPTH = 1

MIX_WIDTH = D_MODEL
DIFF_WIDTH = MIX_WIDTH // 2
RET_WIDTH = MIX_WIDTH - DIFF_WIDTH
N_DIFF_HEADS = 4
DIFF_V_DIM = DIFF_WIDTH // N_DIFF_HEADS
DIFF_QK_DIM = DIFF_V_DIM // 2
N_RET_HEADS = 4
RET_V_DIM = RET_WIDTH // N_RET_HEADS
RET_QK_DIM = RET_V_DIM // 2
DIFF_QK_COLS = N_DIFF_HEADS * 2 * DIFF_QK_DIM
RET_QK_COLS = N_RET_HEADS * RET_QK_DIM
SPLIT_SIZES = (DIFF_QK_COLS, DIFF_QK_COLS, DIFF_WIDTH, RET_QK_COLS, RET_QK_COLS, RET_WIDTH, RET_WIDTH)
SPLIT_POINTS = (512, 1024, 1536, 1792, 2048, 2560)
IN_COLS = 3072

ROPE_THETA = 500000.0
ROPE_FRACTION = 4
RET_THETA = 10000.0
Q_BLOCK = 128
RET_CHUNK = 128

N_KEYS = 128
N_EXPERTS = N_KEYS * N_KEYS
PEER_HEADS = 8
PEER_TOPK = 16
PEER_KEY_DIM = 256
PEER_TOKEN_BLOCK = 128

EPS = 1e-6


def rmsnorm(x, g):
    x32 = x.astype(jnp.float32)
    y = x32 * lax.rsqrt(jnp.mean(x32 * x32, axis=-1, keepdims=True) + EPS)
    return (y * g.astype(jnp.float32)).astype(x.dtype)

def group_norm(o, g):
    mu = jnp.mean(o, axis=-1, keepdims=True)
    c = o - mu
    var = jnp.mean(c * c, axis=-1, keepdims=True)
    return c * lax.rsqrt(var + EPS) * g.astype(jnp.float32)

def rotate_prefix(x, pos, inv_freq):
    half = inv_freq.shape[0]
    rot = 2 * half
    ang = pos[:, None] * inv_freq[None, :]
    shape = (1, pos.shape[0]) + (1,) * (x.ndim - 3) + (half,)
    cos = jnp.cos(ang).reshape(shape)
    sin = jnp.sin(ang).reshape(shape)
    xf = x.astype(jnp.float32)
    x1 = xf[..., :half]
    x2 = xf[..., half:rot]
    out = jnp.concatenate([x1 * cos - x2 * sin, x2 * cos + x1 * sin, xf[..., rot:]], axis=-1)
    return out.astype(x.dtype)

def diff_attention(q, k, v, lam):
    B, S, H, _, d = q.shape
    nb = S // Q_BLOCK
    scale = d ** -0.5
    q_blocks = q.reshape(B, nb, Q_BLOCK, H, 2, d).transpose(1, 0, 2, 3, 4, 5)

    def one_block(qb):
        s = jnp.einsum('bqhmd,bkhmd->bhmqk', qb, k).astype(jnp.float32) * scale
        p = jax.nn.softmax(s, axis=-1)
        a = p[:, :, 0] - lam * p[:, :, 1]
        return jnp.einsum('bhqk,bkhe->bqhe', a.astype(v.dtype), v)

    o = lax.map(one_block, q_blocks)
    return o.transpose(1, 0, 2, 3, 4).reshape(B, S, H, v.shape[-1])

def retention_direction(q, k, v, log_gamma, strict):
    B, S, H, dk = q.shape
    dv = v.shape[-1]
    C = RET_CHUNK
    nc = S // C
    qc = q.reshape(B, nc, C, H, dk).transpose(1, 0, 3, 2, 4)
    kc = k.reshape(B, nc, C, H, dk).transpose(1, 0, 3, 2, 4)
    vc = v.reshape(B, nc, C, H, dv).transpose(1, 0, 3, 2, 4)
    idx = jnp.arange(C, dtype=jnp.float32)
    dist = idx[:, None] - idx[None, :]
    mask = (dist > 0) if strict else (dist >= 0)
    lg = log_gamma[:, None, None]
    decay_in = jnp.where(mask[None], jnp.exp(lg * jnp.maximum(dist, 0.0)[None]), 0.0)
    q_decay = jnp.exp(log_gamma[:, None] * (idx + 1.0)[None])[None, :, :, None]
    k_decay = jnp.exp(log_gamma[:, None] * (C - 1.0 - idx)[None])[None, :, :, None]
    chunk_decay = jnp.exp(log_gamma * C)[None, :, None, None]

    def step(state, inp):
        qi, ki, vi = inp
        inner = jnp.einsum('bhid,bhjd->bhij', qi, ki) * decay_in[None]
        o = jnp.einsum('bhij,bhjv->bhiv', inner, vi) + jnp.einsum('bhid,bhdv->bhiv', qi * q_decay, state)
        state = state * chunk_decay + jnp.einsum('bhjd,bhjv->bhdv', ki * k_decay, vi)
        return state, o

    state0 = jnp.zeros((B, H, dk, dv), jnp.float32)
    _, o = lax.scan(step, state0, (qc, kc, vc))
    return o.transpose(1, 0, 3, 2, 4).reshape(B, S, H, dv)

def peer_ffn(xn, w_query, sub_keys, expert_down, expert_up):
    B, S, D = xn.shape
    T = B * S
    nb = T // PEER_TOKEN_BLOCK
    x_blocks = xn.reshape(nb, PEER_TOKEN_BLOCK, D)

    def one_block(xb):
        tb = xb.shape[0]
        q = (xb @ w_query).reshape(tb, PEER_HEADS, 2, PEER_KEY_DIM // 2)
        s = jnp.einsum('thpd,hpnd->thpn', q, sub_keys).astype(jnp.float32)
        top_s, top_i = lax.top_k(s, PEER_TOPK)
        cand_s = (top_s[:, :, 0, :, None] + top_s[:, :, 1, None, :]).reshape(tb, PEER_HEADS, PEER_TOPK * PEER_TOPK)
        cand_i = (top_i[:, :, 0, :, None] * N_KEYS + top_i[:, :, 1, None, :]).reshape(tb, PEER_HEADS, PEER_TOPK * PEER_TOPK)
        best_s, pos = lax.top_k(cand_s, PEER_TOPK)
        eid = jnp.take_along_axis(cand_i, pos, axis=-1)
        gate = jax.nn.softmax(best_s, axis=-1)
        u = jnp.take(expert_down, eid, axis=0)
        act = jax.nn.gelu(jnp.einsum('thkd,td->thk', u, xb).astype(jnp.float32), approximate=False)
        v = jnp.take(expert_up, eid, axis=0)
        return jnp.einsum('thk,thkd->td', (gate * act).astype(v.dtype), v)

    out = lax.map(one_block, x_blocks)
    return out.reshape(B, S, D).astype(xn.dtype)

def first_inputs(seed: int = 0) -> dict:
    key = jax.random.key(seed)
    ks = jax.random.split(key, 16)
    f32 = jnp.float32
    nrm = jax.random.normal
    x = nrm(ks[0], (BATCH, SEQ, D_MODEL), f32)
    attn_norm_g = 1.0 + 0.02 * nrm(ks[1], (DEPTH, D_MODEL), f32)
    w_in = nrm(ks[2], (DEPTH, D_MODEL, IN_COLS), f32) * D_MODEL ** -0.5
    diff_lambda = 0.1 * nrm(ks[3], (DEPTH, 4, DIFF_QK_DIM), f32)
    diff_norm_g = 1.0 + 0.02 * nrm(ks[4], (DEPTH, DIFF_V_DIM), f32)
    gammas = 1.0 - jnp.exp2(-5.0 - jnp.arange(N_RET_HEADS, dtype=f32))
    base = jnp.log(-jnp.log(gammas))
    ret_log_decay = base[None, None, :] + 0.05 * nrm(ks[5], (DEPTH, 2, N_RET_HEADS), f32)
    ret_norm_g = 1.0 + 0.02 * nrm(ks[6], (DEPTH, N_RET_HEADS, RET_V_DIM), f32)
    w_out = nrm(ks[7], (DEPTH, MIX_WIDTH, D_MODEL), f32) * MIX_WIDTH ** -0.5
    ffn_norm_g = 1.0 + 0.02 * nrm(ks[8], (DEPTH, D_MODEL), f32)
    peer_w_query = nrm(ks[9], (DEPTH, D_MODEL, PEER_HEADS * PEER_KEY_DIM), f32) * D_MODEL ** -0.5
    peer_sub_keys = nrm(ks[10], (DEPTH, PEER_HEADS, 2, N_KEYS, PEER_KEY_DIM // 2), f32) * (PEER_KEY_DIM // 2) ** -0.5
    peer_u = nrm(ks[11], (DEPTH, N_EXPERTS, D_MODEL), f32) * D_MODEL ** -0.5
    peer_v = nrm(ks[12], (DEPTH, N_EXPERTS, D_MODEL), f32) * PEER_HEADS ** -0.5
    final_norm_g = 1.0 + 0.02 * nrm(ks[13], (D_MODEL,), f32)
    return {'x': x, 'attn_norm_g': attn_norm_g, 'w_in': w_in, 'diff_lambda': diff_lambda,
            'diff_norm_g': diff_norm_g, 'ret_log_decay': ret_log_decay, 'ret_norm_g': ret_norm_g,
            'w_out': w_out, 'ffn_norm_g': ffn_norm_g, 'peer_w_query': peer_w_query,
            'peer_sub_keys': peer_sub_keys, 'peer_u': peer_u, 'peer_v': peer_v,
            'final_norm_g': final_norm_g}

def first_block(x, attn_norm_g, w_in, diff_lambda, diff_norm_g, ret_log_decay, ret_norm_g,
              w_out, ffn_norm_g, peer_w_query, peer_sub_keys, peer_u, peer_v, final_norm_g):
    B, S, _ = x.shape
    pos = jnp.arange(S, dtype=jnp.float32)
    rot_dim = DIFF_QK_DIM // ROPE_FRACTION
    rope_inv = jnp.power(jnp.float32(ROPE_THETA), -jnp.arange(rot_dim // 2, dtype=jnp.float32) * 2.0 / rot_dim)
    ret_inv = 1.0 / jnp.power(jnp.float32(RET_THETA), jnp.linspace(0.0, 1.0, RET_QK_DIM // 2, dtype=jnp.float32))

    for l in range(DEPTH):
        lambda_init = 0.8 - 0.6 * math.exp(-0.3 * l)
        h = rmsnorm(x, attn_norm_g[l])
        proj = h @ w_in[l]
        dq, dk, dv, rq, rk, rv, rg = jnp.split(proj, SPLIT_POINTS, axis=-1)

        dq = rotate_prefix(dq.reshape(B, S, N_DIFF_HEADS, 2, DIFF_QK_DIM), pos, rope_inv)
        dk = rotate_prefix(dk.reshape(B, S, N_DIFF_HEADS, 2, DIFF_QK_DIM), pos, rope_inv)
        dv = dv.reshape(B, S, N_DIFF_HEADS, DIFF_V_DIM)
        lam_p = diff_lambda[l].astype(jnp.float32)
        lam = jnp.exp(jnp.sum(lam_p[0] * lam_p[1])) - jnp.exp(jnp.sum(lam_p[2] * lam_p[3])) + lambda_init
        a = diff_attention(dq, dk, dv, lam)
        a = rmsnorm(a, diff_norm_g[l]).astype(jnp.float32) * (1.0 - lambda_init)
        a = a.reshape(B, S, DIFF_WIDTH)

        rq = rotate_prefix(rq.reshape(B, S, N_RET_HEADS, RET_QK_DIM), pos, ret_inv).astype(jnp.float32)
        rk = rotate_prefix(rk.reshape(B, S, N_RET_HEADS, RET_QK_DIM), pos, ret_inv).astype(jnp.float32) * RET_QK_DIM ** -0.5
        rv = rv.reshape(B, S, N_RET_HEADS, RET_V_DIM).astype(jnp.float32)
        log_gamma = -jnp.exp(ret_log_decay[l].astype(jnp.float32))
        r_fwd = retention_direction(rq, rk, rv, log_gamma[0], False)
        r_bwd = retention_direction(rq[:, ::-1], rk[:, ::-1], rv[:, ::-1], log_gamma[1], True)[:, ::-1]
        r = group_norm(r_fwd + r_bwd, ret_norm_g[l]).reshape(B, S, RET_WIDTH)
        r = jax.nn.silu(rg.astype(jnp.float32)) * r

        mix = jnp.concatenate([a, r], axis=-1).astype(x.dtype)
        x = x + mix @ w_out[l]

        x = x + peer_ffn(rmsnorm(x, ffn_norm_g[l]), peer_w_query[l], peer_sub_keys[l], peer_u[l], peer_v[l])

    return rmsnorm(x, final_norm_g)


CHUNK = 64
N_MEM = 256

SSD_HEADS = 16
SSD_HEAD_DIM = 64
SSD_D_INNER = SSD_HEADS * SSD_HEAD_DIM
SSD_GROUPS = 4
SSD_STATE = 128
SSD_CONV = 4
SSD_XBC = SSD_D_INNER + 2 * SSD_GROUPS * SSD_STATE

MLA_HEADS = 16
MLA_Q_RANK = 384
MLA_KV_RANK = 256
MLA_NOPE = 64
MLA_ROPE = 32
MLA_V = 64
ROPE_THETA_2 = 10000.0

MIX_WIDTH_2 = SSD_D_INNER + MLA_HEADS * MLA_V
IN_SSD = SSD_D_INNER + SSD_XBC + SSD_HEADS
IN_MLA = MLA_Q_RANK + MLA_KV_RANK + MLA_ROPE
IN_WIDTH = IN_SSD + IN_MLA

MEM_HEADS = 4
MEM_HEAD_DIM = D_MODEL // MEM_HEADS

D_FF = 2816
FFN_CONV = 3


def rmsnorm_2(x, w):
    xf = x.astype(jnp.float32)
    y = xf * lax.rsqrt(jnp.mean(xf * xf, axis=-1, keepdims=True) + EPS)
    return (y * w.astype(jnp.float32)).astype(x.dtype)

def causal_depthwise_conv(x, w, b):
    k = w.shape[0]
    y = lax.conv_general_dilated(
        x, w[:, None, :].astype(x.dtype), window_strides=(1,), padding=[(k - 1, 0)],
        dimension_numbers=("NWC", "WIO", "NWC"), feature_group_count=x.shape[-1])
    return y + b.astype(x.dtype)

def segsum_exp(a_cum):
    l = a_cum.shape[-1]
    diff = a_cum[..., :, None] - a_cum[..., None, :]
    mask = jnp.tril(jnp.ones((l, l), dtype=bool))
    return jnp.where(mask, jnp.exp(jnp.where(mask, diff, 0.0)), 0.0)

def rope_cos_sin(positions, dim):
    inv_freq = 1.0 / (ROPE_THETA_2 ** (jnp.arange(0, dim, 2, dtype=jnp.float32) / dim))
    ang = positions.astype(jnp.float32)[..., None] * inv_freq
    return jnp.cos(ang), jnp.sin(ang)

def apply_rope(t, cos, sin):
    t1, t2 = jnp.split(t.astype(jnp.float32), 2, axis=-1)
    return jnp.concatenate([t1 * cos - t2 * sin, t1 * sin + t2 * cos], axis=-1).astype(t.dtype)

def ssd_mixer(u, conv_w, conv_b, dt_bias, a_log, d_skip, norm_w):
    b, s, _ = u.shape
    nc = s // CHUNK
    e = SSD_HEADS // SSD_GROUPS
    z, xbc, dt = jnp.split(u, [SSD_D_INNER, SSD_D_INNER + SSD_XBC], axis=-1)
    xbc = jax.nn.silu(causal_depthwise_conv(xbc, conv_w, conv_b))
    xs, bm, cm = jnp.split(xbc, [SSD_D_INNER, SSD_D_INNER + SSD_GROUPS * SSD_STATE], axis=-1)
    xs = xs.reshape(b, nc, CHUNK, SSD_GROUPS, e, SSD_HEAD_DIM)
    bm = bm.reshape(b, nc, CHUNK, SSD_GROUPS, SSD_STATE)
    cm = cm.reshape(b, nc, CHUNK, SSD_GROUPS, SSD_STATE)
    dt = jax.nn.softplus(dt.astype(jnp.float32) + dt_bias.astype(jnp.float32))
    a = -jnp.exp(a_log.astype(jnp.float32))
    dt_c = dt.reshape(b, nc, CHUNK, SSD_GROUPS, e)
    a_dt = jnp.transpose(dt_c * a.reshape(SSD_GROUPS, e), (0, 3, 4, 1, 2))
    a_cum = jnp.cumsum(a_dt, axis=-1)
    x_dt = xs * dt_c[..., None]
    decay_in = segsum_exp(a_cum)
    cb = jnp.einsum("bclgn,bcsgn->bcgls", cm, bm)
    y_diag = jnp.einsum("bcgls,bgecls,bcsgep->bclgep", cb, decay_in, x_dt)
    decay_states = jnp.exp(a_cum[..., -1:] - a_cum)
    states = jnp.einsum("bclgn,bgecl,bclgep->bcgepn", bm, decay_states, x_dt)
    chunk_decay = jnp.exp(a_cum[..., -1])

    def step(h, inp):
        st, dec = inp
        return h * dec[..., None, None] + st, h

    h0 = jnp.zeros_like(states[:, 0])
    _, prev = lax.scan(step, h0, (jnp.moveaxis(states, 1, 0), jnp.moveaxis(chunk_decay, 3, 0)))
    prev = jnp.moveaxis(prev, 0, 1)
    y_off = jnp.einsum("bclgn,bcgepn,bgecl->bclgep", cm, prev, jnp.exp(a_cum))
    y = (y_diag + y_off).reshape(b, s, SSD_HEADS, SSD_HEAD_DIM)
    y = y + xs.reshape(b, s, SSD_HEADS, SSD_HEAD_DIM) * d_skip[:, None]
    y = y.reshape(b, s, SSD_D_INNER) * jax.nn.silu(z)
    y = rmsnorm_2(y.reshape(b, s, SSD_GROUPS, SSD_D_INNER // SSD_GROUPS),
                norm_w.reshape(SSD_GROUPS, SSD_D_INNER // SSD_GROUPS))
    return y.reshape(b, s, SSD_D_INNER).astype(u.dtype)

def mla_mixer(u, positions, q_norm_w, w_q_up, kv_norm_w, w_kv_up):
    b, s, _ = u.shape
    q_lat, kv_lat, k_rope = jnp.split(u, [MLA_Q_RANK, MLA_Q_RANK + MLA_KV_RANK], axis=-1)
    q = (rmsnorm_2(q_lat, q_norm_w) @ w_q_up).reshape(b, s, MLA_HEADS, MLA_NOPE + MLA_ROPE)
    q_nope, q_rope = jnp.split(q, [MLA_NOPE], axis=-1)
    kv = (rmsnorm_2(kv_lat, kv_norm_w) @ w_kv_up).reshape(b, s, MLA_HEADS, MLA_NOPE + MLA_V)
    k_nope, v = jnp.split(kv, [MLA_NOPE], axis=-1)
    cos, sin = rope_cos_sin(positions, MLA_ROPE)
    q_rope = apply_rope(q_rope, cos[:, :, None, :], sin[:, :, None, :])
    k_rope = apply_rope(k_rope, cos, sin)
    scale = (MLA_NOPE + MLA_ROPE) ** -0.5
    nb = s // Q_BLOCK
    k_chunk = jnp.arange(s) // CHUNK

    def blocks(t):
        return jnp.moveaxis(t.reshape(b, nb, Q_BLOCK, *t.shape[2:]), 1, 0)

    def attend(args):
        i, qn, qr = args
        sc = jnp.einsum("bqhd,bkhd->bhqk", qn, k_nope) + jnp.einsum("bqhr,bkr->bhqk", qr, k_rope)
        sc = sc.astype(jnp.float32) * scale
        q_chunk = (i * Q_BLOCK + jnp.arange(Q_BLOCK)) // CHUNK
        mask = k_chunk[None, :] <= q_chunk[:, None]
        sc = jnp.where(mask, sc, jnp.finfo(jnp.float32).min)
        p = jax.nn.softmax(sc, axis=-1).astype(v.dtype)
        return jnp.einsum("bhqk,bkhd->bqhd", p, v)

    o = lax.map(attend, (jnp.arange(nb), blocks(q_nope), blocks(q_rope)))
    return jnp.moveaxis(o, 0, 1).reshape(b, s, MLA_HEADS * MLA_V).astype(u.dtype)

def memory_attention(h, mem_h, wq, wk, wv, wo):
    b, s, _ = h.shape
    q = (h @ wq).reshape(b, s, MEM_HEADS, MEM_HEAD_DIM)
    k = (mem_h @ wk).reshape(b, -1, MEM_HEADS, MEM_HEAD_DIM)
    v = (mem_h @ wv).reshape(b, -1, MEM_HEADS, MEM_HEAD_DIM)
    sc = jnp.einsum("bqhd,bkhd->bhqk", q, k).astype(jnp.float32) * (MEM_HEAD_DIM ** -0.5)
    p = jax.nn.softmax(sc, axis=-1).astype(v.dtype)
    o = jnp.einsum("bhqk,bkhd->bqhd", p, v).reshape(b, s, D_MODEL)
    return o @ wo

def conv_ffn(h, w_up, conv_w, conv_b, w_down):
    u = causal_depthwise_conv(h @ w_up, conv_w, conv_b)
    g, val = jnp.split(u, 2, axis=-1)
    return (jax.nn.silu(g) * val) @ w_down

def second_inputs(seed: int = 0) -> dict:
    key = jax.random.key(seed)
    ks = iter(jax.random.split(key, 40))
    f32 = jnp.float32

    def dense(shape, fan_in):
        return jax.random.normal(next(ks), shape, f32) * (fan_in ** -0.5)

    def gain(shape):
        return 1.0 + 0.02 * jax.random.normal(next(ks), shape, f32)

    def small(shape):
        return 0.01 * jax.random.normal(next(ks), shape, f32)

    L = DEPTH
    x = jax.random.normal(next(ks), (BATCH, SEQ, D_MODEL), f32)
    mem = jax.random.normal(next(ks), (BATCH, N_MEM, D_MODEL), f32)
    offset = jax.random.randint(next(ks), (BATCH, 1), 0, 1024, dtype=jnp.int32)
    positions = offset + jnp.arange(SEQ, dtype=jnp.int32)[None, :]
    dt0 = jnp.exp(jax.random.uniform(next(ks), (L, SSD_HEADS), f32, np.log(1e-3), np.log(1e-1)))
    dt_bias = dt0 + jnp.log(-jnp.expm1(-dt0))
    a_log = jnp.log(jax.random.uniform(next(ks), (L, SSD_HEADS), f32, 1.0, 16.0))
    return {
        "x": x,
        "mem": mem,
        "positions": positions,
        "norm_mix_w": gain((L, D_MODEL)),
        "w_in": dense((L, D_MODEL, IN_WIDTH), D_MODEL),
        "ssd_conv_w": dense((L, SSD_CONV, SSD_XBC), SSD_CONV),
        "ssd_conv_b": small((L, SSD_XBC)),
        "ssd_dt_bias": dt_bias,
        "ssd_a_log": a_log,
        "ssd_d": 1.0 + 0.1 * jax.random.normal(next(ks), (L, SSD_HEADS), f32),
        "ssd_norm_w": gain((L, SSD_D_INNER)),
        "mla_q_norm_w": gain((L, MLA_Q_RANK)),
        "mla_w_q_up": dense((L, MLA_Q_RANK, MLA_HEADS * (MLA_NOPE + MLA_ROPE)), MLA_Q_RANK),
        "mla_kv_norm_w": gain((L, MLA_KV_RANK)),
        "mla_w_kv_up": dense((L, MLA_KV_RANK, MLA_HEADS * (MLA_NOPE + MLA_V)), MLA_KV_RANK),
        "w_out": dense((L, MIX_WIDTH_2, D_MODEL), MIX_WIDTH_2),
        "norm_memx_w": gain((L, D_MODEL)),
        "norm_mem_w": gain((L, D_MODEL)),
        "w_mem_q": dense((L, D_MODEL, D_MODEL), D_MODEL),
        "w_mem_k": dense((L, D_MODEL, D_MODEL), D_MODEL),
        "w_mem_v": dense((L, D_MODEL, D_MODEL), D_MODEL),
        "w_mem_o": dense((L, D_MODEL, D_MODEL), D_MODEL),
        "norm_ffn_w": gain((L, D_MODEL)),
        "w_ffn_up": dense((L, D_MODEL, 2 * D_FF), D_MODEL),
        "ffn_conv_w": dense((L, FFN_CONV, 2 * D_FF), FFN_CONV),
        "ffn_conv_b": small((L, 2 * D_FF)),
        "w_ffn_down": dense((L, D_FF, D_MODEL), D_FF),
        "norm_final_w": gain((D_MODEL,)),
    }

def second_block(x, mem, positions, norm_mix_w, w_in, ssd_conv_w, ssd_conv_b, ssd_dt_bias,
              ssd_a_log, ssd_d, ssd_norm_w, mla_q_norm_w, mla_w_q_up, mla_kv_norm_w,
              mla_w_kv_up, w_out, norm_memx_w, norm_mem_w, w_mem_q, w_mem_k, w_mem_v,
              w_mem_o, norm_ffn_w, w_ffn_up, ffn_conv_w, ffn_conv_b, w_ffn_down, norm_final_w):
    for l in range(DEPTH):
        h = rmsnorm_2(x, norm_mix_w[l])
        u = h @ w_in[l]
        u_ssd, u_mla = jnp.split(u, [IN_SSD], axis=-1)
        y_ssd = ssd_mixer(u_ssd, ssd_conv_w[l], ssd_conv_b[l], ssd_dt_bias[l], ssd_a_log[l],
                          ssd_d[l], ssd_norm_w[l])
        y_mla = mla_mixer(u_mla, positions, mla_q_norm_w[l], mla_w_q_up[l],
                          mla_kv_norm_w[l], mla_w_kv_up[l])
        x = x + jnp.concatenate([y_ssd, y_mla], axis=-1) @ w_out[l]
        x = x + memory_attention(rmsnorm_2(x, norm_memx_w[l]), rmsnorm_2(mem, norm_mem_w[l]),
                                 w_mem_q[l], w_mem_k[l], w_mem_v[l], w_mem_o[l])
        x = x + conv_ffn(rmsnorm_2(x, norm_ffn_w[l]), w_ffn_up[l], ffn_conv_w[l], ffn_conv_b[l],
                         w_ffn_down[l])
    return rmsnorm_2(x, norm_final_w)


def setup_inputs(seed=0):
    out = dict(first_inputs(seed))
    for name, value in second_inputs(seed + 1).items():
        if name != "x":
            out[name + "_2"] = value
    return out


def reference(
    x, attn_norm_g, w_in, diff_lambda, diff_norm_g, ret_log_decay, ret_norm_g, w_out,
    ffn_norm_g, peer_w_query, peer_sub_keys, peer_u, peer_v, final_norm_g, mem_2, positions_2,
    norm_mix_w_2, w_in_2, ssd_conv_w_2, ssd_conv_b_2, ssd_dt_bias_2, ssd_a_log_2, ssd_d_2,
    ssd_norm_w_2, mla_q_norm_w_2, mla_w_q_up_2, mla_kv_norm_w_2, mla_w_kv_up_2, w_out_2,
    norm_memx_w_2, norm_mem_w_2, w_mem_q_2, w_mem_k_2, w_mem_v_2, w_mem_o_2, norm_ffn_w_2,
    w_ffn_up_2, ffn_conv_w_2, ffn_conv_b_2, w_ffn_down_2, norm_final_w_2,
):
    x = first_block(
        x, attn_norm_g, w_in, diff_lambda, diff_norm_g, ret_log_decay, ret_norm_g, w_out,
        ffn_norm_g, peer_w_query, peer_sub_keys, peer_u, peer_v, final_norm_g,
    )
    return second_block(
        x, mem_2, positions_2, norm_mix_w_2, w_in_2, ssd_conv_w_2, ssd_conv_b_2, ssd_dt_bias_2,
        ssd_a_log_2, ssd_d_2, ssd_norm_w_2, mla_q_norm_w_2, mla_w_q_up_2, mla_kv_norm_w_2,
        mla_w_kv_up_2, w_out_2, norm_memx_w_2, norm_mem_w_2, w_mem_q_2, w_mem_k_2, w_mem_v_2,
        w_mem_o_2, norm_ffn_w_2, w_ffn_up_2, ffn_conv_w_2, ffn_conv_b_2, w_ffn_down_2,
        norm_final_w_2,
    )


_drawn_inputs = setup_inputs


def setup_inputs(seed=0):
    import zlib

    import numpy as np

    out = dict(_drawn_inputs(seed))
    spreads = {}
    factors = {'diff_lambda': 4.316,
     'ret_norm_g': 2.926,
     'norm_mix_w_2': 2.935,
     'ssd_conv_b_2': 6.301,
     'ssd_norm_w_2': 4.717,
     'mla_q_norm_w_2': 8.0,
     'mla_kv_norm_w_2': 8.0,
     'norm_memx_w_2': 8.0,
     'norm_mem_w_2': 8.0,
     'norm_ffn_w_2': 4.746,
     'ffn_conv_b_2': 22.305,
     'norm_final_w_2': 7.933,
     'ssd_d_2': 4.82}
    for name, (base, spread) in spreads.items():
        noise = np.random.default_rng([zlib.crc32(name.encode()), seed]).standard_normal(out[name].shape)
        drawn = base * np.exp(spread * noise) if base else spread * noise
        out[name] = __import__('jax').numpy.asarray(drawn.astype(out[name].dtype))
    for name, factor in factors.items():
        out[name] = (out[name] * factor).astype(out[name].dtype)
    return out
```

```python
from contextlib import ExitStack

import numpy as np

import concourse.bass as bass
from concourse import mybir

ALU = mybir.AluOpType
ACT = mybir.ActivationFunctionType
F32 = mybir.dt.float32
I32 = mybir.dt.int32
U32 = mybir.dt.uint32
AX = mybir.AxisListType.X

P = 128
T, D = 256, 1024
TT = T // P
KD = D // P
EPS = 1e-6

HD = 4
LAMBDA_INIT = 0.2
PH, TOPK, NK = 8, 16, 128
SH, SP_, SG = 16, 64, 4
MH, MNOPE, MROPE, MV = 16, 64, 32, 64
MQ = MNOPE + MROPE
DTQ, KVR = 16 + 384, 256 + 32
FF = 2816 // P
NEG = -1.0e30

NW = 6

STAGES = [("w_in", 24), ("w_out", 8), ("w_query", 16), ("sub_keys", 2), ("experts", 2 * NK),
          ("z", 8), ("dt_q", 4), ("kv_rope", 4), ("xbc", 16), ("q_up", 5), ("kv_up", 4),
          ("w_out_2", 16), ("mem_k", 8), ("mem_v", 8), ("mem_q", 8), ("mem_o", 8), ("ffn", 3 * FF)]
SLOT, _n = {}, 0
for _name, _k in STAGES:
    SLOT[_name] = _n
    _n += _k
N_SLOTS = _n

TURNS = [("attn_norm", 4), ("qk", 6), ("mix", 4), ("ffn_norm", 4), ("chosen", 2), ("norm_mix", 4),
         ("xs", 4), ("ssd", 4), ("latents", 3), ("mla_q", 8), ("mla_k", 8), ("mla_out", 4),
         ("norm_mem", 4), ("norm_memx", 4), ("norm_ffn", 4)]
COPIES = [("w_in", 6, 6), ("w_query", 8, 8), ("z", 2, 2), ("dt_q", 1, 1), ("kv_rope", 1, 1),
          ("q_up", 3, 3), ("kv_up", 4, 4), ("mem_k", 4, 4), ("mem_v", 2, 2), ("mem_q", 4, 4)]


def _bases():
    turn, at, av = {}, 0, 0
    b = 0
    for name, n in TURNS:
        turn[name] = (b, at, av, n)
        b, at, av = b + n, at + (n + 1) // 2, av + n // 2
    copy, ca, cv = {}, 0, 0
    for name, a, v in COPIES:
        copy[name] = (ca, cv)
        ca, cv = ca + a, cv + v
    return turn, copy


TURN, COPY = _bases()
NORMS = {"attn": 0, "ffn": 1, "final1": 2, "mix": 3, "mem": 4, "memx": 5, "ffn2": 6, "final2": 7}



def shape_constants():
    f = np.float32
    pos = np.arange(T, dtype=f)
    rot = 16
    inv = np.power(f(500000.0), -np.arange(rot // 2, dtype=f) * f(2.0) / f(rot)).astype(f)
    ret = (f(1.0) / np.power(f(10000.0), np.linspace(0.0, 1.0, 32, dtype=f))).astype(f)
    mla = (f(1.0) / np.power(f(10000.0), np.arange(0, 32, 2, dtype=f) / f(32))).astype(f)
    by_token = lambda a: a.reshape(TT, P, -1).transpose(1, 0, 2).reshape(P, -1)
    a1, a2 = pos[:, None] * inv[None], pos[:, None] * ret[None]
    i, j = np.arange(T)[None, :], np.arange(T)[:, None]
    parts = [
        ("ident", np.eye(P)),
        ("iota", np.broadcast_to(np.arange(P), (P, P))),
        ("cos_d", by_token(np.cos(a1))), ("sin_d", by_token(np.sin(a1))),
        ("cos_r", by_token(np.cos(a2))), ("sin_r", by_token(np.sin(a2))),
        ("later", by_token(np.maximum(i - j, 0))),
        ("earlier", by_token(np.maximum(j - i, 0))),
        ("tri", by_token((j <= i))),
        ("mask", by_token(np.where(i // 64 <= j // 64, 0.0, NEG))),
        ("inv_m", np.broadcast_to(mla, (P, 16))),
        ("ones", np.ones((P, P))),
    ]
    at, n = {}, 0
    for name, a in parts:
        at[name] = (n, n + a.shape[1])
        n += a.shape[1]
    return np.concatenate([np.asarray(a, f) for _, a in parts], axis=1), at


CONST, CAT = shape_constants()

COLS = [("attn_g", 8), ("ffn_g", 8), ("mix_g", 8), ("mem_g", 8), ("memx_g", 8), ("ffn2_g", 8),
        ("ssd_g", 8), ("q_g", 3), ("kv_g", 2), ("xw", 64), ("xb", 16), ("fw", 44 * 3), ("fb", 44)]
ROWS = [("diff_g", 128), ("ret_g", 512), ("lam", 256), ("decay", 8), ("final1_g", 1024), ("final2_g", 1024),
        ("dt_bias", 16), ("a_log", 16), ("d_skip", 16)]


def _places(parts):
    at, n = {}, 0
    for name, k in parts:
        at[name] = (n, n + k)
        n += k
    return at, n


COL, NCOLS = _places(COLS)
ROW, NROWS = _places(ROWS)

AREA = dict(
    x_scaled=(24576, 26624), squares=(26624, 27648),
    proj=(0, 6144), qk_t=(6144, 9216), decay=(9216, 11264), gate_r=(11264, 12288), e_diff=(12288, 13312),
    a_diff=(13312, 13824), at_diff=(13824, 14336), o_diff=(14336, 15360), p_ret=(15360, 17408),
    o_ret=(17408, 18432), mix=(18432, 20480), rot=(20480, 22528), stat=(22528, 22784),
    pq_t=(0, 4096), keys=(4096, 8192), spare=(8192, 8704), vals=(8704, 9216), idx=(9216, 9728), idxf=(9728, 10240),
    cand=(10240, 14336), best=(14336, 14592), pos=(14592, 14848), hi=(14848, 15104), lo=(15104, 15360),
    eq=(15360, 17408), chosen=(17408, 18176), gst=(18176, 18432),
    z=(0, 2048), lat=(2048, 4096), xc=(4096, 8192), xs=(8192, 10240), xdt=(10240, 12288), cb=(12288, 14336),
    seg=(14336, 15360), y=(15360, 17408), dts=(17408, 17920), mix_t=(17920, 22016), lat_t=(22016, 23296),
    rope=(23296, 24576),
    q=(4096, 7168), kv=(7168, 11264), kcat=(11264, 14336), q_t=(27648, 31744), k_t=(0, 4096),
    s_m=(14336, 14848), e_m=(14848, 15360), et_m=(15360, 15872), o_m=(15872, 17920),
    mem=(0, 2048), mem_t=(2048, 4096), mk_t=(4096, 6144), mv=(6144, 8192), mq_t=(8192, 10240),
    e_x=(10240, 10752), et_x=(10752, 11776),
    out=(0, 2048),
)


def two_blocks(nc, weights, consts, cols_in, rows_in, x_in, mem_in, pos_in, out):
    with ExitStack() as ctx:
        def sb(name, shape, dt=F32):
            return ctx.enter_context(nc.sbuf_tensor(name, shape, dt))

        arena = sb("arena", [P, NK * T])
        ring = sb("ring", [P, NW, 1024])
        xres = sb("xres", [P, TT, D])
        h_t = sb("h_t", [P, KD, T])
        cst = sb("cst", [P, CONST.shape[1]])
        cols = sb("cols", [P, NCOLS])
        rows = sb("rows", [P, NROWS])
        chosen_t = sb("chosen_t", [P, 3, T])
        work = sb("work", [P, 4, 512])
        ssq = sb("ssq", [P, 8])
        rstd = sb("rstd", [P, 8])
        lam = sb("lam", [P, 8])
        log_g = sb("log_g", [P, 8])
        sm = sb("sm", [P, 2, 16])
        pos_i = sb("pos_i", [P, TT], I32)
        bank = ctx.enter_context(nc.psum_tensor("bank", [P, 8, 512], F32))

        def area(name, pattern=None, **kw):
            a, b = AREA[name]
            v = arena[:, a:b]
            return v.rearrange(pattern, **kw) if pattern else v

        def const(name):
            return cst[:, CAT[name][0]:CAT[name][1]]

        def col(name, i, n=1):
            return cols[:, COL[name][0] + i:COL[name][0] + i + n]

        def row(name):
            return rows[:, ROW[name][0]:ROW[name][1]]

        ident = const("ident")
        x_scaled = area("x_scaled", "p (t d) -> p t d", t=TT)
        squares = area("squares")
        proj = area("proj", "p (t c) -> p t c", t=TT)
        qk_t = area("qk_t", "p (b t) -> p b t", t=T)
        decay = area("decay", "p (h j i) -> p h j i", h=HD, j=TT)
        gate_r = area("gate_r", "p (t c) -> p t c", t=TT)
        e_diff = area("e_diff", "p (b m k) -> p b m k", b=2, m=2)
        a_diff = area("a_diff", "p (b k) -> p b k", b=2)
        at_diff = area("at_diff", "p (b k q) -> p b k q", b=2, k=2)
        o_diff = area("o_diff", "p (t c) -> p t c", t=TT)
        p_ret = area("p_ret", "p (h j i) -> p h j i", h=HD, j=TT)
        o_ret = area("o_ret", "p (t c) -> p t c", t=TT)
        mix = area("mix", "p (t c) -> p t c", t=TT)
        pq_t = area("pq_t", "p (j t) -> p j t", t=T)
        keys = area("keys", "p (t b c) -> p t b c", t=TT, c=512)
        gates = arena[:, :].rearrange("p (i t) -> p i t", t=T)
        z = area("z", "p (t c) -> p t c", t=TT)
        lat = area("lat", "p (t c) -> p t c", t=TT)
        xc = area("xc", "p (b t) -> p b t", t=T)
        xs = area("xs", "p (t c) -> p t c", t=TT)
        xdt = area("xdt", "p (t c) -> p t c", t=TT)
        cb = area("cb", "p (g s l) -> p g s l", g=SG, s=TT)
        seg = area("seg", "p (b l) -> p b l", b=2)
        y = area("y", "p (t c) -> p t c", t=TT)
        mix_t = area("mix_t", "p (b t) -> p b t", t=T)
        lat_t = area("lat_t", "p (b t) -> p b t", t=T)
        q = area("q", "p (t c) -> p t c", t=TT)
        kv = area("kv", "p (t c) -> p t c", t=TT)
        kcat = area("kcat", "p (t c) -> p t c", t=TT)
        q_t = area("q_t", "p (h t) -> p h t", t=T)
        k_t = area("k_t", "p (h t) -> p h t", t=T)
        s_m = area("s_m", "p (b k) -> p b k", b=2)
        e_m = area("e_m", "p (b k) -> p b k", b=2)
        et_m = area("et_m", "p (b k q) -> p b k q", b=2, k=2)
        o_m = area("o_m", "p (t c) -> p t c", t=TT)
        mem = area("mem", "p (t c) -> p t c", t=TT)
        mem_t = area("mem_t", "p (b t) -> p b t", t=T)
        mk_t = area("mk_t", "p (b t) -> p b t", t=T)
        mv = area("mv", "p (t c) -> p t c", t=TT)
        mq_t = area("mq_t", "p (b t) -> p b t", t=T)
        e_x = area("e_x", "p (b k) -> p b k", b=2)
        et_x = area("et_x", "p (b k q) -> p b k q", b=2, k=2)
        out_sb = area("out", "p (t c) -> p t c", t=TT)

        loaded = [ctx.enter_context(nc.semaphore(f"slot_loaded_{i}")) for i in range(NW)]
        s = {name: ctx.enter_context(nc.semaphore(name)) for name in (
            "x_loaded", "params_loaded", "mem_loaded", "out_stored",
            "spent", "phase", "dve_done", "act_done",
            "norm_summed", "norm_mean", "norm_rooted", "norm_factor", "norm_scaled",
            "turned", "turned_out_act", "turned_out_dve", "copied_act", "copied_dve",
            "lambda_products", "lambda_exp", "decay_arg", "decay_exp",
            "diff_scores", "diff_shift", "diff_exp", "diff_mixed", "diff_turned", "diff_t_copied", "diff_out", "diff_out_copied",
            "ret_scores", "ret_decayed", "ret_out", "ret_out_copied",
            "head_mean", "head_root", "gate_shifted", "gate_exp",
            "one_hot_1", "one_hot_2", "one_hot_gated", "spread", "spread_copied",
            "gelu_done", "weighed",
            "conv_done", "filter_step", "latents_scaled", "choice_made", "residual_ready",
            "dt_arg", "dt_e", "dt_l", "dt_scaled", "cum_done", "cb_done", "cb_masked",
            "seg_sum", "seg_clipped", "seg_exp", "seg_weighed", "ssd_out",
            "group_mean", "group_root", "trig_arg", "trig_done",
            "mla_scores", "mla_shift", "mla_exp", "mla_turned", "mla_t_copied", "mla_out", "mla_out_copied",
            "mem_scores", "mem_shift", "mem_exp", "mem_scaled", "mem_turned", "mem_t_copied", "mem_out", "mem_out_copied",
            "ffn_conv_g", "ffn_conv_v", "ffn_silu", "ffn_act",
        )}

        def wait_slot(pe, n):
            pe.wait_ge(loaded[n % NW], 16 * (n // NW + 1))

        def begin(eng, n):
            if n:
                eng.wait_ge(s["phase"], 3 * n)

        def end(eng):
            eng.drain().then_inc(s["phase"], 1)

        block = ctx.enter_context(nc.Block())

        @block.sync
        def _(sp):
            def slot_load(n, k):
                src = weights[bass.ds(n, 1)].rearrange("a p f -> p (a f)")
                sp.dma_start(ring[:, k, :], src).then_inc(loaded[k], 16)

            total = N_SLOTS
            sp.dma_start(xres[:, :, :], x_in).then_inc(s["x_loaded"], 16)
            for n in range(NW):
                slot_load(n, n)
            full = (total - NW) // NW
            with sp.Fori(1, full + 1) as r:
                for k in range(NW):
                    sp.wait_ge(s["spent"], r * NW + (k + 1 - NW))
                    slot_load(r * NW + k, k)
            for n in range((full + 1) * NW, total):
                sp.wait_ge(s["spent"], n + 1 - NW)
                slot_load(n, n % NW)

        @block.gpsimd
        def _(pool):
            pool.dma_start(cst[:, :], consts).then_inc(s["params_loaded"], 16)
            pool.dma_start(cols[:, :], cols_in).then_inc(s["params_loaded"], 16)
            pool.dma_start(rows[:, :], rows_in).then_inc(s["params_loaded"], 16)
            pool.dma_start(pos_i[:, :], pos_in).then_inc(s["params_loaded"], 16)

            begin(pool, 14)
            one_hots = lambda b: work[:, b, :].rearrange("p (t k) -> p t k", t=4)

            def gated(g, u):
                pool.wait_ge(s["one_hot_1"], g + 1)
                g4 = chosen_t[:, 2, bass.ds(g * 4, 4)].unsqueeze(2).broadcast_to([P, 4, NK])
                nc.gpsimd.tensor_tensor(one_hots(u), one_hots(u), g4, ALU.mult).then_inc(s["one_hot_gated"], 1)

            with pool.Fori(0, T // 8) as r:
                for u in range(2):
                    gated(r * 2 + u, u)
            begin(pool, 31)
            pool.dma_start(mem[:, :, :], mem_in).then_inc(s["mem_loaded"], 16)

        @block.tensor
        def _(pe):
            def turn(name, source, blocks, width=P):
                first, act0, dve0, n = TURN[name]
                for b in range(blocks):
                    k = b // 2
                    if b % 2 == 0 and k >= 8:
                        if k % 2 == 0:
                            pe.wait_ge(s["turned_out_act"], act0 + (k - 8) // 2 + 1)
                        else:
                            pe.wait_ge(s["turned_out_dve"], dve0 + (k - 8) // 2 + 1)
                    for t in range(TT):
                        at = (b % 2) * T + t * P
                        mm = pe.transpose(bank[0:width, k % 8, at:at + P], source(b, t), ident)
                    if b % 2 == 1 or b == blocks - 1:
                        mm.then_inc(s["turned"], 1)

            def norm_turn(name, which):
                pe.wait_ge(s["norm_scaled"], 2 * which + 2)
                turn(name, lambda b, t: x_scaled[:, t, b * P:(b + 1) * P], KD)

            def by_tokens(name, src, depth, widths, copied=None):
                first, (act0, dve0) = SLOT[name], COPY[name]
                panels = len(widths) * depth
                for c, w in enumerate(widths):
                    if c >= 2:
                        pe.wait_ge(s["copied_act"], act0 + c - 1)
                        pe.wait_ge(s["copied_dve"], dve0 + c - 1)
                    for k in range(depth):
                        p = c * depth + k
                        n, half = first + p // 2, p % 2
                        if half == 0:
                            wait_slot(pe, n)
                        for t in range(TT):
                            mm = pe.matmul(bank[:, 2 * (c % 2) + t, 0:w], src[:, k, t * P:(t + 1) * P],
                                           ring[:, n % NW, half * 512:half * 512 + w],
                                           start=(k == 0), stop=(k == depth - 1))
                        if half == 1 or p == panels - 1:
                            mm.then_inc(s["spent"], 1)

            def by_channels(name, src, blocks, free):
                for j in range(blocks):
                    n = SLOT[name] + j
                    if j >= 4:
                        free(j)
                    wait_slot(pe, n)
                    for k in range(KD):
                        mm = pe.matmul(bank[:, j % 4, 0:T], ring[:, n % NW, k * P:(k + 1) * P], src[:, k, :],
                                       start=(k == 0), stop=(k == KD - 1))
                    mm.then_inc(s["spent"], 1)

            def free_by(name):
                act0, dve0 = COPY[name]

                def free(j):
                    if j % 2 == 0:
                        pe.wait_ge(s["copied_act"], act0 + (j - 4) // 2 + 1)
                    else:
                        pe.wait_ge(s["copied_dve"], dve0 + (j - 4) // 2 + 1)
                return free

            def into_residual(name, src, depth):
                for k in range(depth):
                    n = SLOT[name] + k
                    wait_slot(pe, n)
                    for t in range(TT):
                        for h in range(2):
                            mm = pe.matmul(bank[:, 2 * t + h, :], src[:, k, t * P:(t + 1) * P],
                                           ring[:, n % NW, h * 512:(h + 1) * 512],
                                           start=(k == 0), stop=(k == depth - 1))
                    mm.then_inc(s["spent"], 1)

            pe.wait_ge(s["params_loaded"], 64)
            norm_turn("attn_norm", NORMS["attn"])
            end(pe)
            begin(pe, 1)
            by_tokens("w_in", h_t, KD, [512] * 6)
            end(pe)
            begin(pe, 2)
            end(pe)
            begin(pe, 3)
            turn("qk", lambda b, t: proj[:, t, b * P:(b + 1) * P] if b < 8 else
                 proj[:, t, 1536 + (b - 8) * P:1536 + (b - 7) * P], 12)
            end(pe)
            begin(pe, 4)
            units = [(h, t) for h in range(HD) for t in range(TT)]

            def diff_scores(u):
                h, t = units[u]
                if u >= 2:
                    pe.wait_ge(s["diff_exp"], u - 1)
                for m in range(2):
                    r = slice(m * 64, m * 64 + 64)
                    mm = pe.matmul(bank[:, 2 * (u % 2) + m, 0:T], qk_t[r, h, t * P:(t + 1) * P],
                                   qk_t[r, 4 + h, :], start=True, stop=True)
                mm.then_inc(s["diff_scores"], 1)

            diff_scores(0)
            for u, (h, t) in enumerate(units):
                if u + 1 < len(units):
                    diff_scores(u + 1)
                pe.wait_ge(s["diff_mixed"], u + 1)
                if u >= 2:
                    pe.wait_ge(s["diff_t_copied"], u - 1)
                for k in range(2):
                    mm = pe.transpose(bank[:, 4 + u % 2, k * P:(k + 1) * P], a_diff[:, u % 2, k * P:(k + 1) * P], ident)
                mm.then_inc(s["diff_turned"], 1)
                pe.wait_ge(s["diff_t_copied"], u + 1)
                if u >= 2:
                    pe.wait_ge(s["diff_out_copied"], u - 1)
                for k in range(2):
                    mm = pe.matmul(bank[:, 6 + u % 2, 0:P], at_diff[:, u % 2, k, :],
                                   proj[:, k, 1024 + h * P:1024 + (h + 1) * P], start=(k == 0), stop=(k == 1))
                mm.then_inc(s["diff_out"], 1)
            end(pe)
            begin(pe, 5)

            def ret_scores(h):
                r = slice((h % 2) * 64, (h % 2) * 64 + 64)
                if h >= 2:
                    pe.wait_ge(s["ret_decayed"], h - 1)
                for j in range(TT):
                    mm = pe.matmul(bank[:, h % 2, j * T:(j + 1) * T], qk_t[r, 10 + h // 2, j * P:(j + 1) * P],
                                   qk_t[r, 8 + h // 2, :], start=True, stop=True)
                mm.then_inc(s["ret_scores"], 1)

            ret_scores(0)
            for h in range(HD):
                if h + 1 < HD:
                    ret_scores(h + 1)
                pe.wait_ge(s["ret_decayed"], h + 1)
                for t in range(TT):
                    for j in range(TT):
                        mm = pe.matmul(bank[:, 2 + t, h * P:(h + 1) * P], p_ret[:, h, j, t * P:(t + 1) * P],
                                       proj[:, j, 2048 + h * P:2048 + (h + 1) * P], start=(j == 0), stop=(j == 1))
                mm.then_inc(s["ret_out"], 1)
            end(pe)
            begin(pe, 6)
            end(pe)
            begin(pe, 7)
            turn("mix", lambda b, t: mix[:, t, b * P:(b + 1) * P], KD)
            end(pe)
            begin(pe, 8)
            into_residual("w_out", h_t, KD)
            end(pe)
            begin(pe, 9)
            norm_turn("ffn_norm", NORMS["ffn"])
            end(pe)
            begin(pe, 10)
            by_channels("w_query", h_t, 16, free_by("w_query"))
            end(pe)
            begin(pe, 11)
            for b in range(4):
                n = SLOT["sub_keys"] + b // 2
                if b % 2 == 0:
                    wait_slot(pe, n)
                for t in range(TT):
                    for i in range(4):
                        mm = pe.matmul(bank[:, 2 * b + t, i * P:(i + 1) * P], pq_t[:, 4 * b + i, t * P:(t + 1) * P],
                                       ring[:, n % NW, ((4 * b + i) % 8) * P:((4 * b + i) % 8 + 1) * P],
                                       start=True, stop=True)
                    if b % 2 == 1 and t == 1:
                        mm.then_inc(s["spent"], 1)
            end(pe)
            begin(pe, 12)
            turn_after_choice = area("chosen", "p (f c) -> p f c", f=6)
            pe.wait_ge(s["choice_made"], 1)
            turn("chosen", lambda b, t: turn_after_choice[:, b * 2 + t, :], 3)
            end(pe)
            begin(pe, 13)
            end(pe)
            begin(pe, 14)
            one_hots = lambda b: work[:, b, :].rearrange("p (t k) -> p t k", t=4)

            def spread(g, u):
                pe.wait_ge(s["one_hot_gated"], g + 1)
                pe.wait_ge(s["one_hot_2"], g + 1)
                for i in range(4):
                    mm = pe.matmul(bank[:, u, i * P:(i + 1) * P], one_hots(2 + u)[:, i, :], one_hots(u)[:, i, :],
                                   start=True, stop=True)
                mm.then_inc(s["spread"], 1)

            spread(0, 0)
            spread(1, 1)
            with pe.Fori(1, T // 8) as r:
                for u in range(2):
                    pe.wait_ge(s["spread_copied"], r * 2 + (u - 1))
                    spread(r * 2 + u, u)
            end(pe)
            begin(pe, 15)
            X = SLOT["experts"]
            U3 = NW // 2

            def down(k, n0, rounds, u, first=False):
                pe.wait_ge(loaded[n0 % NW], rounds * 16 + 16 * (n0 // NW + 1))
                for c in range(KD):
                    mm = pe.matmul(bank[:, 4 + u, 0:T], ring[:, n0 % NW, c * P:(c + 1) * P], h_t[:, c, :],
                                   start=(c == 0), stop=(c == KD - 1))
                mm.then_inc(s["spent"], 1)

            def up(k, n0, rounds, u, start=False, stop=False):
                pe.wait_ge(loaded[n0 % NW], rounds * 16 + 16 * (n0 // NW + 1))
                pe.wait_ge(s["weighed"], k + 1)
                for t in range(TT):
                    for h in range(2):
                        mm = pe.matmul(bank[:, 2 * t + h, :], work[:, u, T + t * P:T + (t + 1) * P],
                                       ring[:, n0 % NW, h * 512:(h + 1) * 512], start=start, stop=stop,
                                       skip_group_check=True)
                mm.then_inc(s["spent"], 1)

            down(0, X, 0, 0)
            down(1, X + 1, 0, 1)
            up(0, X + 2, 0, 0, start=True)
            with pe.Fori(0, (NK - 2) // U3) as r:
                for u in range(U3):
                    k = r * U3 + (1 + u)
                    pe.wait_ge(s["gelu_done"], r * U3 + (u + 1))
                    down(k + 1, X + 3 + 2 * u, r, (2 + u) % U3)
                    up(k, X + 4 + 2 * u, r, (1 + u) % U3)
            up(NK - 1, X + 2 * NK - 1, 0, (NK - 1) % U3, stop=True)
            end(pe)
            begin(pe, 16)
            end(pe)
            begin(pe, 17)
            norm_turn("norm_mix", NORMS["mix"])
            end(pe)
            begin(pe, 18)
            by_tokens("z", h_t, KD, [512, 512])
            pe.wait_ge(s["copied_act"], COPY["z"][0] + 1)
            pe.wait_ge(s["copied_dve"], COPY["z"][1] + 1)
            by_tokens("dt_q", h_t, KD, [DTQ])
            end(pe)
            begin(pe, 19)
            by_tokens("kv_rope", h_t, KD, [KVR])
            end(pe)
            begin(pe, 20)
            by_channels("xbc", h_t, 16, lambda j: pe.wait_ge(s["conv_done"], 4 * (j - 3)))
            end(pe)
            begin(pe, 21)
            for t in range(TT):
                for b in range(2):
                    for i in range(4):
                        mm = pe.transpose(bank[:, 2 * t + b, i * P:(i + 1) * P], xc[:, 4 * b + i, t * P:(t + 1) * P], ident)
                    mm.then_inc(s["turned"], 1)
            for g in range(SG):
                for j in range(TT):
                    mm = pe.matmul(bank[:, 4 + g % 2, j * T:(j + 1) * T],
                                   xc[:, 8 + g, j * P:(j + 1) * P], xc[:, 12 + g, :], start=True, stop=True)
                mm.then_inc(s["cb_done"], 1)
                if g >= 1 and g + 1 < SG:
                    pe.wait_ge(s["cb_masked"], g)
            pe.wait_ge(s["dt_scaled"], 1)
            adt = area("dts")[:, 0:32].rearrange("p (t h) -> p t h", t=TT)
            tri = const("tri").rearrange("p (j l) -> p j l", j=TT)
            for t in range(TT):
                for j in range(t + 1):
                    mm = pe.matmul(bank[:, 6, t * 16:(t + 1) * 16], tri[:, j, t * P:(t + 1) * P], adt[:, j, :],
                                   start=(j == 0), stop=(j == t))
            mm.then_inc(s["cum_done"], 1)
            end(pe)
            begin(pe, 22)

            def seg_sum(h):
                if h >= 2:
                    pe.wait_ge(s["seg_clipped"], 2 * (h - 1))
                for j in range(TT):
                    mm = pe.matmul(bank[:, h % 2, 0:T], adt[:, j, h:h + 1].to_broadcast([P, P]), tri[:, j, :],
                                   start=(j == 0), stop=(j == 1))
                mm.then_inc(s["seg_sum"], 1)

            seg_sum(0)
            for h in range(SH):
                if h + 1 < SH:
                    seg_sum(h + 1)
                pe.wait_ge(s["seg_weighed"], 2 * (h + 1))
                lo = (h % 8) * 64
                pe.matmul(bank[:, 4 + h // 8, lo:lo + 64], seg[:, h % 2, 0:P], xdt[:, 0, h * 64:(h + 1) * 64],
                          start=True, stop=True)
                pe.matmul(bank[:, 6 + h // 8, lo:lo + 64], seg[:, h % 2, P:2 * P], xdt[:, 0, h * 64:(h + 1) * 64],
                          start=True, stop=False)
                pe.matmul(bank[:, 6 + h // 8, lo:lo + 64], seg[:, h % 2, 2 * P:3 * P], xdt[:, 1, h * 64:(h + 1) * 64],
                          start=False, stop=True).then_inc(s["ssd_out"], 1)
            end(pe)
            begin(pe, 23)
            end(pe)
            begin(pe, 24)
            turn("ssd", lambda b, t: y[:, t, b * P:(b + 1) * P], KD)
            end(pe)
            begin(pe, 25)
            pe.wait_ge(s["latents_scaled"], 1)
            turn("latents", lambda b, t: lat[:, t, 16 + b * P:16 + (b + 1) * P] if b < 3 else
                 lat[:, t, 512 + (b - 3) * P:512 + (b - 2) * P], 5)
            end(pe)
            begin(pe, 26)
            by_tokens("q_up", lat_t, 3, [512] * 3)
            pe.wait_ge(s["copied_act"], COPY["q_up"][0] + 3)
            pe.wait_ge(s["copied_dve"], COPY["q_up"][1] + 3)
            by_tokens("kv_up", lat_t[:, 3:5, :], 2, [512] * 4)
            end(pe)
            begin(pe, 27)
            end(pe)
            begin(pe, 28)
            turn("mla_q", lambda b, t: q[:, t, b * MQ:(b + 1) * MQ], MH, MQ)
            end(pe)
            begin(pe, 29)
            turn("mla_k", lambda b, t: kcat[:, t, b * MQ:(b + 1) * MQ], MH, MQ)
            end(pe)
            begin(pe, 30)
            munits = [(h, t) for h in range(MH) for t in range(TT)]

            def mla_scores(u):
                h, t = munits[u]
                if u >= 2:
                    pe.wait_ge(s["mla_shift"], u - 1)
                pe.matmul(bank[:, u % 2, 0:(t + 1) * P], q_t[0:MQ, h, t * P:(t + 1) * P], k_t[0:MQ, h, 0:(t + 1) * P],
                          start=True, stop=True).then_inc(s["mla_scores"], 1)

            mla_scores(0)
            for u, (h, t) in enumerate(munits):
                if u + 1 < len(munits):
                    mla_scores(u + 1)
                pe.wait_ge(s["mla_exp"], u + 1)
                if u >= 2:
                    pe.wait_ge(s["mla_t_copied"], u - 1)
                for k in range(t + 1):
                    mm = pe.transpose(bank[:, 2 + u % 2, k * P:(k + 1) * P], e_m[:, u % 2, k * P:(k + 1) * P], ident)
                mm.then_inc(s["mla_turned"], 1)
                pe.wait_ge(s["mla_t_copied"], u + 1)
                if u >= 2:
                    pe.wait_ge(s["mla_out_copied"], u - 1)
                for k in range(t + 1):
                    mm = pe.matmul(bank[:, 4 + u % 2, 0:MV], et_m[:, u % 2, k, :],
                                   kv[:, k, h * 128 + MNOPE:(h + 1) * 128], start=(k == 0), stop=(k == t))
                mm.then_inc(s["mla_out"], 1)
            end(pe)
            begin(pe, 31)
            turn("mla_out", lambda b, t: o_m[:, t, b * P:(b + 1) * P], KD)
            end(pe)
            begin(pe, 32)
            into_residual("w_out_2", mix_t, 16)
            end(pe)
            begin(pe, 33)
            norm_turn("norm_mem", NORMS["mem"])
            end(pe)
            begin(pe, 34)
            norm_turn("norm_memx", NORMS["memx"])
            end(pe)
            begin(pe, 35)
            by_channels("mem_k", mem_t, 8, free_by("mem_k"))
            end(pe)
            begin(pe, 36)
            by_tokens("mem_v", mem_t, KD, [512, 512])
            end(pe)
            begin(pe, 37)
            by_channels("mem_q", h_t, 8, free_by("mem_q"))
            end(pe)
            begin(pe, 38)
            xunits = [(h, t) for h in range(4) for t in range(TT)]

            def mem_scores(u):
                h, t = xunits[u]
                if u >= 2:
                    pe.wait_ge(s["mem_exp"], u - 1)
                for k in range(2):
                    mm = pe.matmul(bank[:, u % 2, 0:T], mq_t[:, 2 * h + k, t * P:(t + 1) * P], mk_t[:, 2 * h + k, :],
                                   start=(k == 0), stop=(k == 1))
                mm.then_inc(s["mem_scores"], 1)

            mem_scores(0)
            for u, (h, t) in enumerate(xunits):
                if u + 1 < len(xunits):
                    mem_scores(u + 1)
                pe.wait_ge(s["mem_scaled"], u + 1)
                if u >= 2:
                    pe.wait_ge(s["mem_t_copied"], u - 1)
                for k in range(2):
                    mm = pe.transpose(bank[:, 2 + u % 2, k * P:(k + 1) * P], e_x[:, u % 2, k * P:(k + 1) * P], ident)
                mm.then_inc(s["mem_turned"], 1)
                if t == 1:
                    pe.wait_ge(s["mem_t_copied"], u + 1)
                    if h >= 2:
                        pe.wait_ge(s["mem_out_copied"], h - 1)
                    for e in range(2):
                        for k in range(2):
                            mm = pe.matmul(bank[:, 4 + h % 2, e * T:(e + 1) * T],
                                           mv[:, k, h * T + e * P:h * T + (e + 1) * P], et_x[:, h % 2, k, :],
                                           start=(k == 0), stop=(k == 1))
                    mm.then_inc(s["mem_out"], 1)
            end(pe)
            begin(pe, 39)
            into_residual("mem_o", h_t, KD)
            end(pe)
            begin(pe, 40)
            norm_turn("norm_ffn", NORMS["ffn2"])
            end(pe)
            begin(pe, 41)
            F = SLOT["ffn"]
            U2 = NW // 3

            def ffn_up(n0, rounds, u):
                for half in range(2):
                    nn = n0 + half
                    pe.wait_ge(loaded[nn % NW], rounds * 16 + 16 * (nn // NW + 1))
                    for c in range(KD):
                        mm = pe.matmul(bank[:, 4 + 2 * u + half, 0:T], ring[:, nn % NW, c * P:(c + 1) * P], h_t[:, c, :],
                                       start=(c == 0), stop=(c == KD - 1))
                    mm.then_inc(s["spent"], 1)

            def ffn_down(k, n0, rounds, u, start=False, stop=False):
                pe.wait_ge(loaded[n0 % NW], rounds * 16 + 16 * (n0 // NW + 1))
                pe.wait_ge(s["ffn_act"], k + 1)
                for t in range(TT):
                    for h in range(2):
                        mm = pe.matmul(bank[:, 2 * t + h, :], work[:, 2, u * T + t * P:u * T + (t + 1) * P],
                                       ring[:, n0 % NW, h * 512:(h + 1) * 512], start=start, stop=stop,
                                       skip_group_check=True)
                mm.then_inc(s["spent"], 1)

            ffn_up(F, 0, 0)
            ffn_up(F + 2, 0, 1)
            ffn_down(0, F + 4, 0, 0, start=True)
            with pe.Fori(0, (FF - 2) // U2) as r:
                for u in range(U2):
                    k = r * U2 + (1 + u)
                    pe.wait_ge(s["ffn_conv_v"], r * U2 + (1 + u))
                    ffn_up(F + 5 + 3 * u, r, u % 2)
                    ffn_down(k, F + 7 + 3 * u, r, (1 + u) % 2)
            ffn_down(FF - 1, F + 3 * FF - 1, 0, (FF - 1) % 2, stop=True)
            end(pe)

        @block.scalar
        def _(act):
            done = [0]

            def link(ins):
                done[0] += 1
                ins.then_inc(s["act_done"], 1)
                act.wait_ge(s["act_done"], done[0])

            def turned_out(name, dst, blocks, gain=None, rows_=P):
                first, act0, dve0, n = TURN[name]
                for k in range(0, n, 2):
                    act.wait_ge(s["turned"], first + k + 1)
                    width = min(2, blocks - 2 * k)
                    if gain is None:
                        ins = nc.scalar.copy(dst[0:rows_, 2 * k:2 * k + width, :],
                                             bank[0:rows_, k % 8, 0:width * T].rearrange("p (b t) -> p b t", t=T))
                    else:
                        for i in range(width):
                            ins = nc.scalar.mul(dst[:, 2 * k + i, :], bank[:, k % 8, i * T:(i + 1) * T], gain(2 * k + i))
                    ins.then_inc(s["turned_out_act"], 1)

            def norm(which, src):
                for t in range(TT):
                    nc.scalar.activation(squares, src[:, t, :], ACT.Square, accum_out=ssq[:, t:t + 1]).then_inc(s["norm_summed"], 1)
                    act.wait_ge(s["norm_summed"], 2 * which + t + 1)
                act.wait_ge(s["norm_mean"], which + 1)
                nc.scalar.activation(rstd[:, 0:2], ssq[:, 2:4], ACT.Sqrt).then_inc(s["norm_rooted"], 1)
                act.wait_ge(s["norm_factor"], which + 1)
                nc.scalar.mul(x_scaled[:, 0, :], src[:, 0, :], rstd[:, 2:3]).then_inc(s["norm_scaled"], 1)

            def by_tokens(name, depth, widths, dst):
                for c, w in enumerate(widths):
                    p = (c + 1) * depth
                    act.wait_ge(s["spent"], SLOT[name] + (p + 1) // 2)
                    nc.scalar.copy(dst[:, 0, c * 512:c * 512 + w], bank[:, 2 * (c % 2), 0:w]).then_inc(s["copied_act"], 1)

            def by_channels(name, blocks, dst):
                for j in range(0, blocks, 2):
                    act.wait_ge(s["spent"], SLOT[name] + j + 1)
                    nc.scalar.copy(dst[:, j, :], bank[:, j % 4, 0:T]).then_inc(s["copied_act"], 1)

            act.wait_ge(s["params_loaded"], 64)
            act.wait_ge(s["x_loaded"], 16)
            norm(NORMS["attn"], xres)
            turned_out("attn_norm", h_t, KD, lambda b: col("attn_g", b))
            end(act)
            begin(act, 1)
            by_tokens("w_in", KD, [512] * 6, proj)
            end(act)
            begin(act, 2)
            nc.scalar.activation(gate_r[:, :, :], proj[:, :, 2560:3072], ACT.Silu)
            act.wait_ge(s["lambda_products"], 1)
            nc.scalar.activation(lam[:, 2:4], lam[:, 0:2], ACT.Exp).then_inc(s["lambda_exp"], 1)
            nc.scalar.activation(log_g[:, :], row("decay"), ACT.Exp).then_inc(s["lambda_exp"], 1)
            for h in range(HD):
                act.wait_ge(s["decay_arg"], h + 1)
                nc.scalar.activation(decay[:, h, :, :], decay[:, h, :, :], ACT.Exp)
            end(act)
            begin(act, 3)
            turned_out("qk", qk_t, 12)
            end(act)
            begin(act, 4)
            for u in range(8):
                act.wait_ge(s["diff_shift"], u + 1)
                if u >= 2:
                    act.wait_ge(s["diff_mixed"], u - 1)
                for m in range(2):
                    ins = nc.scalar.activation(e_diff[:, u % 2, m, :], bank[:, 2 * (u % 2) + m, 0:T], ACT.Exp,
                                               bias=sm[:, u % 2, m:m + 1], scale=0.125,
                                               accum_out=sm[:, u % 2, 2 + m:3 + m])
                ins.then_inc(s["diff_exp"], 1)
                act.wait_ge(s["diff_turned"], u + 1)
                if u >= 2:
                    act.wait_ge(s["diff_out"], u - 1)
                nc.scalar.copy(at_diff[:, u % 2, :, :], bank[:, 4 + u % 2, 0:T].rearrange("p (k q) -> p k q", k=2))\
                    .then_inc(s["diff_t_copied"], 1)
            end(act)
            begin(act, 5)
            end(act)
            begin(act, 6)
            for i in range(2):
                act.wait_ge(s["head_mean"], i + 1)
                nc.scalar.activation(area("stat")[:, 32 * i + 16:32 * i + 24], area("stat")[:, 32 * i + 8:32 * i + 16], ACT.Sqrt)\
                    .then_inc(s["head_root"], 1)
            end(act)
            begin(act, 7)
            turned_out("mix", h_t, KD)
            end(act)
            begin(act, 8)
            end(act)
            begin(act, 9)
            norm(NORMS["ffn"], xres)
            turned_out("ffn_norm", h_t, KD, lambda b: col("ffn_g", b))
            end(act)
            begin(act, 10)
            by_channels("w_query", 16, pq_t)
            end(act)
            begin(act, 11)
            for b in range(4):
                act.wait_ge(s["spent"], SLOT["sub_keys"] + b // 2 + 1)
                nc.scalar.copy(keys[:, 0, b, :], bank[:, 2 * b, :])
            end(act)
            begin(act, 12)
            gst = area("gst")
            for t in range(TT):
                best = area("best", "p (t c) -> p t c", t=TT)[:, t, :]
                act.wait_ge(s["gate_shifted"], t + 1)
                nc.scalar.activation(best, best, ACT.Exp).then_inc(s["gate_exp"], 1)
            turned_out("chosen", chosen_t, 3)
            end(act)
            begin(act, 13)
            end(act)
            begin(act, 14)

            def table(g, u):
                act.wait_ge(s["spread"], g + 1)
                nc.scalar.copy(gates[:, :, bass.ds(g * 4, 4)], bank[:, u, :].rearrange("p (t i) -> p i t", t=4))\
                    .then_inc(s["spread_copied"], 1)

            with act.Fori(0, T // 8) as r:
                for u in range(2):
                    table(r * 2 + u, u)
            end(act)
            begin(act, 15)
            X = SLOT["experts"]
            U3 = NW // 2

            def gelu(k, spent, u):
                act.wait_ge(s["spent"], spent)
                nc.scalar.activation(work[:, u, 0:T], bank[:, 4 + u, 0:T], ACT.Gelu).then_inc(s["gelu_done"], 1)

            gelu(0, X + 1, 0)
            gelu(1, X + 2, 1)
            gelu(2, X + 4, 2)
            with act.Fori(1, NK // U3) as r:
                for u in range(U3):
                    act.wait_ge(s["weighed"], r * U3 + (u - 2))
                    gelu(0, r * (2 * U3) + (X + 2 * u), u)
            for k in range(NK // U3 * U3, NK):
                act.wait_ge(s["weighed"], k - 2)
                gelu(k, X + 2 * k, k % U3)
            end(act)
            begin(act, 16)
            act.wait_ge(s["residual_ready"], 1)
            norm(NORMS["final1"], xres)
            end(act)
            begin(act, 17)
            norm(NORMS["mix"], xres)
            turned_out("norm_mix", h_t, KD, lambda b: col("mix_g", b))
            end(act)
            begin(act, 18)
            by_tokens("z", KD, [512, 512], z)
            by_tokens("dt_q", KD, [DTQ], lat)
            end(act)
            begin(act, 19)
            act.wait_ge(s["spent"], SLOT["kv_rope"] + 4)
            nc.scalar.copy(lat[:, 0, 512:512 + KVR], bank[:, 0, 0:KVR]).then_inc(s["copied_act"], 1)
            nc.scalar.activation(z[:, 0, :], z[:, 0, :], ACT.Silu)
            nc.scalar.activation(z[:, 1, :], z[:, 1, :], ACT.Silu)
            end(act)
            begin(act, 20)
            for j in range(16):
                act.wait_ge(s["conv_done"], 4 * (j + 1))
                nc.scalar.activation(xc[:, j, :], xc[:, j, :], ACT.Silu)
            end(act)
            begin(act, 21)
            dts = area("dts")
            act.wait_ge(s["dt_arg"], 1)
            nc.scalar.activation(dts[:, 96:128], dts[:, 64:96], ACT.Exp, scale=-1.0).then_inc(s["dt_e"], 1)
            act.wait_ge(s["dt_e"], 1)
            nc.scalar.activation(dts[:, 128:160], dts[:, 96:128], ACT.Ln, bias=1.0).then_inc(s["dt_l"], 1)
            nc.scalar.activation(dts[:, 160:176], row("a_log"), ACT.Exp).then_inc(s["dt_l"], 1)
            for k in range(0, 4, 2):
                act.wait_ge(s["turned"], TURN["xs"][0] + k + 1)
                t, b = k // 2, k % 2
                nc.scalar.copy(xs[:, t, b * 512:(b + 1) * 512], bank[:, k, :]).then_inc(s["turned_out_act"], 1)
            end(act)
            begin(act, 22)
            for h in range(SH):
                act.wait_ge(s["seg_clipped"], 2 * (h + 1))
                nc.scalar.activation(seg[:, h % 2, 0:3 * P], seg[:, h % 2, 0:3 * P], ACT.Exp).then_inc(s["seg_exp"], 1)
            end(act)
            begin(act, 23)
            act.wait_ge(s["group_mean"], 1)
            nc.scalar.activation(dts[:, 208:216], dts[:, 200:208], ACT.Sqrt).then_inc(s["group_root"], 1)
            end(act)
            begin(act, 24)
            turned_out("ssd", mix_t, KD, lambda b: col("ssd_g", b))
            end(act)
            begin(act, 25)
            act.wait_ge(s["group_mean"], 2)
            nc.scalar.activation(dts[:, 208:212], dts[:, 200:204], ACT.Sqrt).then_inc(s["group_root"], 1)
            turned_out("latents", lat_t, 5, lambda b: col("q_g", b) if b < 3 else col("kv_g", b - 3))
            rope = area("rope")
            act.wait_ge(s["trig_arg"], 1)
            nc.scalar.activation(rope[:, 192:256], rope[:, 128:192], ACT.Sin).then_inc(s["trig_done"], 1)
            end(act)
            begin(act, 26)
            by_tokens("q_up", 3, [512] * 3, q)
            by_tokens("kv_up", 2, [512] * 4, kv)
            end(act)
            begin(act, 27)
            end(act)
            begin(act, 28)
            turned_out("mla_q", q_t, MH, rows_=MQ)
            end(act)
            begin(act, 29)
            turned_out("mla_k", k_t, MH, rows_=MQ)
            end(act)
            begin(act, 30)
            for u in range(2 * MH):
                h, t = u // 2, u % 2
                w = (t + 1) * P
                act.wait_ge(s["mla_shift"], u + 1)
                if u >= 2:
                    act.wait_ge(s["mla_turned"], u - 1)
                nc.scalar.activation(e_m[:, u % 2, 0:w], s_m[:, u % 2, 0:w], ACT.Exp, bias=sm[:, u % 2, 0:1],
                                     accum_out=sm[:, u % 2, 1:2]).then_inc(s["mla_exp"], 1)
                act.wait_ge(s["mla_turned"], u + 1)
                if u >= 2:
                    act.wait_ge(s["mla_out"], u - 1)
                nc.scalar.copy(et_m[:, u % 2, 0:t + 1, :], bank[:, 2 + u % 2, 0:w].rearrange("p (k q) -> p k q", q=P))\
                    .then_inc(s["mla_t_copied"], 1)
            end(act)
            begin(act, 31)
            turned_out("mla_out", mix_t[:, 8:16, :], KD)
            end(act)
            begin(act, 32)
            end(act)
            begin(act, 33)
            act.wait_ge(s["mem_loaded"], 16)
            norm(NORMS["mem"], mem)
            turned_out("norm_mem", mem_t, KD, lambda b: col("mem_g", b))
            end(act)
            begin(act, 34)
            norm(NORMS["memx"], xres)
            turned_out("norm_memx", h_t, KD, lambda b: col("memx_g", b))
            end(act)
            begin(act, 35)
            by_channels("mem_k", 8, mk_t)
            end(act)
            begin(act, 36)
            by_tokens("mem_v", KD, [512, 512], mv)
            end(act)
            begin(act, 37)
            by_channels("mem_q", 8, mq_t)
            end(act)
            begin(act, 38)
            for u in range(8):
                h, t = u // 2, u % 2
                act.wait_ge(s["mem_shift"], u + 1)
                if u >= 2:
                    act.wait_ge(s["mem_turned"], u - 1)
                nc.scalar.activation(e_x[:, u % 2, :], bank[:, u % 2, 0:T], ACT.Exp, bias=sm[:, u % 2, 0:1],
                                     scale=0.0625, accum_out=sm[:, u % 2, 1:2]).then_inc(s["mem_exp"], 1)
                act.wait_ge(s["mem_turned"], u + 1)
                if h >= 2:
                    act.wait_ge(s["mem_out"], h - 1)
                nc.scalar.copy(et_x[:, h % 2, :, t * P:(t + 1) * P],
                               bank[:, 2 + u % 2, 0:T].rearrange("p (k q) -> p k q", q=P)).then_inc(s["mem_t_copied"], 1)
            end(act)
            begin(act, 39)
            end(act)
            begin(act, 40)
            norm(NORMS["ffn2"], xres)
            turned_out("norm_ffn", h_t, KD, lambda b: col("ffn2_g", b))
            end(act)
            begin(act, 41)
            with act.Fori(0, FF // 2) as r:
                for u in range(2):
                    act.wait_ge(s["ffn_conv_g"], r * 2 + (u + 1))
                    nc.scalar.activation(work[:, 0, u * T:(u + 1) * T], work[:, 0, u * T:(u + 1) * T], ACT.Silu)\
                        .then_inc(s["ffn_silu"], 1)
            end(act)
            begin(act, 42)
            act.wait_ge(s["residual_ready"], 2)
            norm(NORMS["final2"], xres)
            act.wait_ge(s["norm_scaled"], 2 * NORMS["final2"] + 2 + 2)
            act.dma_start(out, out_sb[:, :, :]).then_inc(s["out_stored"], 16)
            act.wait_ge(s["out_stored"], 16)

        @block.vector
        def _(dve):
            v = nc.vector
            done = [0]

            def link(ins):
                done[0] += 1
                ins.then_inc(s["dve_done"], 1)
                dve.wait_ge(s["dve_done"], done[0])

            def signal(name):
                dve.drain().then_inc(s[name], 1)

            def turned_out(name, dst, blocks, gain=None, rows_=P):
                first, act0, dve0, n = TURN[name]
                for k in range(1, n, 2):
                    dve.wait_ge(s["turned"], first + k + 1)
                    width = min(2, blocks - 2 * k)
                    if gain is None:
                        ins = v.tensor_copy(dst[0:rows_, 2 * k:2 * k + width, :],
                                            bank[0:rows_, k % 8, 0:width * T].rearrange("p (b t) -> p b t", t=T))
                    else:
                        for i in range(width):
                            ins = v.tensor_scalar(dst[:, 2 * k + i, :], bank[:, k % 8, i * T:(i + 1) * T],
                                                  gain(2 * k + i), None, ALU.mult)
                    ins.then_inc(s["turned_out_dve"], 1)

            def norm(which, src):
                dve.wait_ge(s["norm_summed"], 2 * which + 2)
                v.tensor_scalar(ssq[:, 2:4], ssq[:, 0:2], 1.0 / D, EPS, ALU.mult, ALU.add).then_inc(s["norm_mean"], 1)
                dve.wait_ge(s["norm_rooted"], which + 1)
                v.reciprocal(rstd[:, 2:4], rstd[:, 0:2]).then_inc(s["norm_factor"], 1)
                dve.wait_ge(s["norm_factor"], which + 1)
                v.tensor_scalar(x_scaled[:, 1, :], src[:, 1, :], rstd[:, 3:4], None, ALU.mult).then_inc(s["norm_scaled"], 1)

            def by_tokens(name, depth, widths, dst):
                for c, w in enumerate(widths):
                    p = (c + 1) * depth
                    dve.wait_ge(s["spent"], SLOT[name] + (p + 1) // 2)
                    v.tensor_copy(dst[:, 1, c * 512:c * 512 + w], bank[:, 2 * (c % 2) + 1, 0:w]).then_inc(s["copied_dve"], 1)

            def by_channels(name, blocks, dst):
                for j in range(1, blocks, 2):
                    dve.wait_ge(s["spent"], SLOT[name] + j + 1)
                    v.tensor_copy(dst[:, j, :], bank[:, j % 4, 0:T]).then_inc(s["copied_dve"], 1)

            def into_residual(spent):
                dve.wait_ge(s["spent"], spent)
                for t in range(TT):
                    for h in range(2):
                        link(v.tensor_tensor(xres[:, t, h * 512:(h + 1) * 512], xres[:, t, h * 512:(h + 1) * 512],
                                             bank[:, 2 * t + h, :], ALU.add))

            def rotate(x1, x2, cos, sin, tmp):
                v.tensor_tensor(tmp(0), x1, cos, ALU.mult)
                v.tensor_tensor(tmp(1), x2, sin, ALU.mult)
                v.tensor_tensor(tmp(2), x2, cos, ALU.mult)
                link(v.tensor_tensor(tmp(3), x1, sin, ALU.mult))
                v.tensor_tensor(x1, tmp(0), tmp(1), ALU.subtract)
                link(v.tensor_tensor(x2, tmp(2), tmp(3), ALU.add))

            dve.wait_ge(s["params_loaded"], 64)
            dve.wait_ge(s["x_loaded"], 16)
            norm(NORMS["attn"], xres)
            turned_out("attn_norm", h_t, KD, lambda b: col("attn_g", b))
            end(dve)
            begin(dve, 1)
            by_tokens("w_in", KD, [512] * 6, proj)
            end(dve)
            begin(dve, 2)
            lp = row("lam").rearrange("p (a b d) -> p a b d", a=2, b=2)
            lt = area("rot")[:, 0:128].rearrange("p (a d) -> p a d", a=2)
            link(v.tensor_tensor(lt, lp[:, :, 0, :], lp[:, :, 1, :], ALU.mult))
            v.tensor_reduce(lam[:, 0:2], lt, AX, ALU.add).then_inc(s["lambda_products"], 1)
            dve.wait_ge(s["lambda_exp"], 2)
            link(v.tensor_tensor(lam[:, 4:5], lam[:, 3:4], lam[:, 2:3], ALU.subtract))
            link(v.tensor_scalar(lam[:, 5:6], lam[:, 4:5], -LAMBDA_INIT, None, ALU.add))
            later, earlier = const("later"), const("earlier")
            for h in range(HD):
                dh = decay[:, h, :, :].rearrange("p j i -> p (j i)")
                link(v.tensor_scalar(dh, earlier, log_g[:, 4 + h:5 + h], -1.0, ALU.mult, ALU.mult))
                link(v.tensor_scalar(area("p_ret")[:, 0:512], later, log_g[:, h:h + 1], -1.0, ALU.mult, ALU.mult))
                v.tensor_tensor(dh, dh, area("p_ret")[:, 0:512], ALU.add).then_inc(s["decay_arg"], 1)
                dve.wait_ge(s["decay_arg"], h + 1)
            rot = area("rot")
            for t in range(TT):
                dqk = proj[:, t, 0:1024].rearrange("p (g d) -> p g d", d=64)
                cd = const("cos_d")[:, t * 8:(t + 1) * 8].unsqueeze(1).broadcast_to([P, 16, 8])
                sd = const("sin_d")[:, t * 8:(t + 1) * 8].unsqueeze(1).broadcast_to([P, 16, 8])
                rotate(dqk[:, :, 0:8], dqk[:, :, 8:16], cd, sd,
                       lambda i: rot[:, i * 128:(i + 1) * 128].rearrange("p (g d) -> p g d", d=8))
                rqk = proj[:, t, 1536:2048].rearrange("p (g d) -> p g d", d=64)
                cr = const("cos_r")[:, t * 32:(t + 1) * 32].unsqueeze(1).broadcast_to([P, 8, 32])
                sr = const("sin_r")[:, t * 32:(t + 1) * 32].unsqueeze(1).broadcast_to([P, 8, 32])
                rotate(rqk[:, :, 0:32], rqk[:, :, 32:64], cr, sr,
                       lambda i: rot[:, 1024 + i * 256:1024 + (i + 1) * 256].rearrange("p (g d) -> p g d", d=32))
            end(dve)
            begin(dve, 3)
            turned_out("qk", qk_t, 12)
            end(dve)
            begin(dve, 4)

            def diff_shift(u):
                dve.wait_ge(s["diff_scores"], u + 1)
                if u >= 2:
                    dve.wait_ge(s["diff_exp"], u - 1)
                link(v.tensor_reduce(sm[:, u % 2, 4:6], bank[:, 2 * (u % 2):2 * (u % 2) + 2, 0:T], AX, ALU.max))
                v.tensor_scalar(sm[:, u % 2, 0:2], sm[:, u % 2, 4:6], -0.125, None, ALU.mult).then_inc(s["diff_shift"], 1)

            diff_shift(0)
            for u in range(8):
                h, t = u // 2, u % 2
                if u + 1 < 8:
                    diff_shift(u + 1)
                dve.wait_ge(s["diff_exp"], u + 1)
                if u >= 2:
                    dve.wait_ge(s["diff_turned"], u - 1)
                link(v.reciprocal(sm[:, u % 2, 6:8], sm[:, u % 2, 2:4]))
                link(v.tensor_scalar(sm[:, u % 2, 8:9], sm[:, u % 2, 7:8], lam[:, 5:6], None, ALU.mult))
                link(v.tensor_scalar(e_diff[:, u % 2, 1, :], e_diff[:, u % 2, 1, :], sm[:, u % 2, 8:9], None, ALU.mult))
                v.scalar_tensor_tensor(out=a_diff[:, u % 2, :], in0=e_diff[:, u % 2, 0, :], scalar=sm[:, u % 2, 6:7],
                                       in1=e_diff[:, u % 2, 1, :], op0=ALU.mult, op1=ALU.add).then_inc(s["diff_mixed"], 1)
                dve.wait_ge(s["diff_out"], u + 1)
                v.tensor_copy(o_diff[:, t, h * P:(h + 1) * P], bank[:, 6 + u % 2, 0:P]).then_inc(s["diff_out_copied"], 1)
            end(dve)
            begin(dve, 5)
            for h in range(HD):
                dve.wait_ge(s["ret_scores"], h + 1)
                v.scalar_tensor_tensor(out=p_ret[:, h, :, :].rearrange("p j i -> p (j i)"), in0=bank[:, h % 2, :],
                                       scalar=0.125, in1=decay[:, h, :, :].rearrange("p j i -> p (j i)"),
                                       op0=ALU.mult, op1=ALU.mult).then_inc(s["ret_decayed"], 1)
            dve.wait_ge(s["ret_out"], HD)
            for t in range(TT):
                v.tensor_copy(o_ret[:, t, :], bank[:, 2 + t, :])
            end(dve)
            begin(dve, 6)
            stat = area("stat")
            by_head = lambda a: a.rearrange("p t (h c) -> p (t h) c", c=P)
            sq = area("rot", "p (g c) -> p g c", c=P)[:, 0:8, :]
            od, orr = by_head(o_diff), by_head(o_ret)
            link(v.tensor_tensor(sq, od, od, ALU.mult))
            link(v.tensor_reduce(stat[:, 0:8], sq, AX, ALU.add))
            v.tensor_scalar(stat[:, 8:16], stat[:, 0:8], 1.0 / P, EPS, ALU.mult, ALU.add).then_inc(s["head_mean"], 1)
            link(v.tensor_reduce(stat[:, 64:72], orr, AX, ALU.add))
            link(v.tensor_scalar(stat[:, 72:80], stat[:, 64:72], 1.0 / P, None, ALU.mult))
            link(v.tensor_tensor(orr, orr, stat[:, 72:80].unsqueeze(2).broadcast_to([P, 8, P]), ALU.subtract))
            link(v.tensor_tensor(sq, orr, orr, ALU.mult))
            link(v.tensor_reduce(stat[:, 32:40], sq, AX, ALU.add))
            v.tensor_scalar(stat[:, 40:48], stat[:, 32:40], 1.0 / P, EPS, ALU.mult, ALU.add).then_inc(s["head_mean"], 1)
            dve.wait_ge(s["head_root"], 1)
            link(v.reciprocal(stat[:, 24:32], stat[:, 16:24]))
            link(v.tensor_scalar(stat[:, 24:32], stat[:, 24:32], 1.0 - LAMBDA_INIT, None, ALU.mult))
            link(v.tensor_tensor(od, od, stat[:, 24:32].unsqueeze(2).broadcast_to([P, 8, P]), ALU.mult))
            for t in range(TT):
                v.tensor_tensor(mix[:, t, 0:512].rearrange("p (h c) -> p h c", c=P), od[:, 4 * t:4 * t + 4, :],
                                row("diff_g").unsqueeze(1).broadcast_to([P, HD, P]), ALU.mult)
            dve.wait_ge(s["head_root"], 2)
            link(v.reciprocal(stat[:, 56:64], stat[:, 48:56]))
            link(v.tensor_tensor(orr, orr, stat[:, 56:64].unsqueeze(2).broadcast_to([P, 8, P]), ALU.mult))
            for t in range(TT):
                link(v.tensor_tensor(o_ret[:, t, :], o_ret[:, t, :], row("ret_g"), ALU.mult))
                v.tensor_tensor(mix[:, t, 512:1024], o_ret[:, t, :], gate_r[:, t, :], ALU.mult)
            end(dve)
            begin(dve, 7)
            turned_out("mix", h_t, KD)
            end(dve)
            begin(dve, 8)
            into_residual(SLOT["w_out"] + 8)
            end(dve)
            begin(dve, 9)
            norm(NORMS["ffn"], xres)
            turned_out("ffn_norm", h_t, KD, lambda b: col("ffn_g", b))
            end(dve)
            begin(dve, 10)
            by_channels("w_query", 16, pq_t)
            end(dve)
            begin(dve, 11)
            for b in range(4):
                dve.wait_ge(s["spent"], SLOT["sub_keys"] + b // 2 + 1)
                v.tensor_copy(keys[:, 1, b, :], bank[:, 2 * b + 1, :])
            end(dve)
            begin(dve, 12)
            vals = area("vals", "p (g c) -> p g c", c=TOPK)
            idx = area("idx", "p (g c) -> p g c", c=TOPK).bitcast(U32)
            spare = area("spare")
            sets = keys.rearrange("p t b (i c) -> p (t b i) c", c=NK)

            def top16(values, top, index, rest):
                link(v.max(top[:, 0:8], values))
                v.max_index(index[:, 0:8], top[:, 0:8], values)
                link(v.match_replace(rest, top[:, 0:8], values, -3.0e38))
                link(v.max(top[:, 8:16], rest))
                v.max_index(index[:, 8:16], top[:, 8:16], rest)

            for g in range(2 * 2 * PH):
                top16(sets[:, g, :], vals[:, g, :], idx[:, g, :], spare[:, (g % 2) * NK:(g % 2 + 1) * NK])
            cand = area("cand", "p (g i j) -> p g i j", i=TOPK, j=TOPK)
            pairs = vals.rearrange("p (g s) c -> p g s c", s=2)
            best = area("best", "p (g c) -> p g c", c=TOPK)
            pos = area("pos", "p (g c) -> p g c", c=TOPK).bitcast(U32)
            dve.wait_ge(s["dve_done"], done[0])
            for g in range(2 * PH):
                link(v.tensor_tensor(cand[:, g, :, :], pairs[:, g, 0, :].unsqueeze(2).broadcast_to([P, TOPK, TOPK]),
                                     pairs[:, g, 1, :].unsqueeze(1).broadcast_to([P, TOPK, TOPK]), ALU.add))
                top16(cand[:, g, :, :].rearrange("p i j -> p (i j)"), best[:, g, :], pos[:, g, :],
                      spare[:, (g % 2) * 256:(g % 2 + 1) * 256])
            link(v.tensor_copy(area("idxf"), area("idx").bitcast(U32)))
            hi_i, lo_i = area("hi").bitcast(U32), area("lo").bitcast(U32)
            posv = area("pos").bitcast(U32)
            link(v.tensor_scalar(hi_i, posv, 4, None, ALU.logical_shift_right))
            link(v.tensor_scalar(lo_i, posv, 15, None, ALU.bitwise_and))
            link(v.tensor_copy(area("hi"), hi_i))
            link(v.tensor_copy(area("lo"), lo_i))
            chosen = area("chosen", "p (f c) -> p f c", f=6)
            eq = area("eq", "p (k a) -> p k a", a=TOPK)
            idxf = area("idxf", "p (t h s a) -> p t h s a", t=TT, s=2, a=TOPK)
            iota16 = const("iota")[:, 0:TOPK].unsqueeze(1).broadcast_to([P, P, TOPK])
            for t in range(TT):
                for f, ch in enumerate(("hi", "lo")):
                    pick = area(ch)[:, t * P:(t + 1) * P].unsqueeze(2).broadcast_to([P, P, TOPK])
                    link(v.tensor_tensor(eq, pick, iota16, ALU.is_equal))
                    e4 = eq.rearrange("p (h k) a -> p h k a", h=PH)
                    link(v.tensor_tensor(e4, e4, idxf[:, t, :, f, :].unsqueeze(2).broadcast_to([P, PH, TOPK, TOPK]), ALU.mult))
                    link(v.tensor_reduce(chosen[:, 2 * f + t, :], eq, AX, ALU.add))
            gst = area("gst")
            for t in range(TT):
                bt = best[:, 8 * t:8 * t + 8, :]
                link(v.tensor_copy(gst[:, t * 8:t * 8 + 8], bt[:, :, 0:1].rearrange("p h o -> p (h o)")))
                v.tensor_tensor(bt, bt, gst[:, t * 8:t * 8 + 8].unsqueeze(2).broadcast_to([P, PH, TOPK]), ALU.subtract)\
                    .then_inc(s["gate_shifted"], 1)
            for t in range(TT):
                bt = best[:, 8 * t:8 * t + 8, :]
                dve.wait_ge(s["gate_exp"], t + 1)
                link(v.tensor_reduce(gst[:, 16 + t * 8:24 + t * 8], bt, AX, ALU.add))
                link(v.reciprocal(gst[:, 32 + t * 8:40 + t * 8], gst[:, 16 + t * 8:24 + t * 8]))
                link(v.tensor_tensor(chosen[:, 4 + t, :].rearrange("p (h k) -> p h k", h=PH), bt,
                                     gst[:, 32 + t * 8:40 + t * 8].unsqueeze(2).broadcast_to([P, PH, TOPK]), ALU.mult))
            signal("choice_made")
            turned_out("chosen", chosen_t, 3)
            end(dve)
            begin(dve, 13)
            end(dve)
            begin(dve, 14)
            iota4 = const("iota").unsqueeze(1).broadcast_to([P, 4, NK])
            one_hots = lambda b: work[:, b, :].rearrange("p (t k) -> p t k", t=4)

            def compared(g, u):
                keys4 = lambda f: chosen_t[:, f, bass.ds(g * 4, 4)].unsqueeze(2).broadcast_to([P, 4, NK])
                v.tensor_tensor(one_hots(u), iota4, keys4(0), ALU.is_equal).then_inc(s["one_hot_1"], 1)
                v.tensor_tensor(one_hots(2 + u), iota4, keys4(1), ALU.is_equal).then_inc(s["one_hot_2"], 1)

            compared(0, 0)
            compared(1, 1)
            with dve.Fori(1, T // 8) as r:
                for u in range(2):
                    dve.wait_ge(s["spread"], r * 2 + (u - 1))
                    compared(r * 2 + u, u)
            end(dve)
            begin(dve, 15)
            X = SLOT["experts"]
            U3 = NW // 2

            def weigh(k, u):
                dve.wait_ge(s["gelu_done"], k + 1)
                g = gates[:, bass.ds(k, 1), :].rearrange("p a t -> p (a t)")
                v.tensor_tensor(work[:, u, T:2 * T], work[:, u, 0:T], g, ALU.mult).then_inc(s["weighed"], 1)

            for k in range(3):
                weigh(k, k)
            with dve.Fori(1, NK // U3) as r:
                for u in range(U3):
                    dve.wait_ge(s["spent"], r * (2 * U3) + (X + 2 * u - 3))
                    weigh(r * U3 + u, u)
            for k in range(NK // U3 * U3, NK):
                dve.wait_ge(s["spent"], X + 2 * k - 3)
                weigh(k, k % U3)
            end(dve)
            begin(dve, 16)
            into_residual(X + 2 * NK)
            signal("residual_ready")
            norm(NORMS["final1"], xres)
            dve.wait_ge(s["norm_scaled"], 2 * NORMS["final1"] + 2)
            for t in range(TT):
                v.tensor_tensor(xres[:, t, :], x_scaled[:, t, :], row("final1_g"), ALU.mult)
            end(dve)
            begin(dve, 17)
            norm(NORMS["mix"], xres)
            turned_out("norm_mix", h_t, KD, lambda b: col("mix_g", b))
            end(dve)
            begin(dve, 18)
            by_tokens("z", KD, [512, 512], z)
            by_tokens("dt_q", KD, [DTQ], lat)
            end(dve)
            begin(dve, 19)
            dve.wait_ge(s["spent"], SLOT["kv_rope"] + 4)
            v.tensor_copy(lat[:, 1, 512:512 + KVR], bank[:, 1, 0:KVR]).then_inc(s["copied_dve"], 1)
            end(dve)
            begin(dve, 20)
            for j in range(16):
                dve.wait_ge(s["spent"], SLOT["xbc"] + j + 1)
                b = bank[:, j % 4, :]
                v.tensor_scalar(xc[:, j, :], b[:, 0:T], col("xw", 4 * j + 3), col("xb", j), ALU.mult, ALU.add)\
                    .then_inc(s["conv_done"], 1)
                for d in range(1, 4):
                    dve.wait_ge(s["conv_done"], 4 * j + d)
                    v.scalar_tensor_tensor(out=xc[:, j, d:T], in0=b[:, 0:T - d], scalar=col("xw", 4 * j + 3 - d),
                                           in1=xc[:, j, d:T], op0=ALU.mult, op1=ALU.add).then_inc(s["conv_done"], 1)
            end(dve)
            begin(dve, 21)
            dts = area("dts")
            t2 = lambda a: dts[:, a:a + 32].rearrange("p (t h) -> p t h", t=TT)
            wide = lambda r_: row(r_).unsqueeze(1).broadcast_to([P, TT, 16])
            link(v.tensor_tensor(t2(32), lat[:, :, 0:16], wide("dt_bias"), ALU.add))
            link(v.scalar_tensor_tensor(out=dts[:, 64:96], in0=dts[:, 32:64], scalar=-1.0, in1=dts[:, 32:64],
                                        op0=ALU.mult, op1=ALU.max))
            signal("dt_arg")
            dve.wait_ge(s["dt_l"], 2)
            link(v.scalar_tensor_tensor(out=dts[:, 32:64], in0=dts[:, 32:64], scalar=0.0, in1=dts[:, 128:160],
                                        op0=ALU.max, op1=ALU.add))
            link(v.tensor_scalar(dts[:, 160:176], dts[:, 160:176], -1.0, None, ALU.mult))
            v.tensor_tensor(t2(0), t2(32), dts[:, 160:176].unsqueeze(1).broadcast_to([P, TT, 16]), ALU.mult)\
                .then_inc(s["dt_scaled"], 1)
            for k in range(1, 4, 2):
                dve.wait_ge(s["turned"], TURN["xs"][0] + k + 1)
                t, b = k // 2, k % 2
                v.tensor_copy(xs[:, t, b * 512:(b + 1) * 512], bank[:, k, :]).then_inc(s["turned_out_dve"], 1)
            dve.wait_ge(s["turned_out_act"], TURN["xs"][1] + 2)
            dve.wait_ge(s["turned_out_dve"], TURN["xs"][2] + 2)
            for t in range(TT):
                v.tensor_tensor(xdt[:, t, :].rearrange("p (h c) -> p h c", c=64),
                                xs[:, t, :].rearrange("p (h c) -> p h c", c=64),
                                t2(32)[:, t, :].unsqueeze(2).broadcast_to([P, SH, 64]), ALU.mult)
            for g in range(SG):
                dve.wait_ge(s["cb_done"], g + 1)
                v.tensor_tensor(cb[:, g, :, :].rearrange("p j l -> p (j l)"), bank[:, 4 + g % 2, :], const("tri"), ALU.mult)\
                    .then_inc(s["cb_masked"], 1)
            dve.wait_ge(s["cum_done"], 1)
            v.tensor_copy(dts[:, 64:96], bank[:, 6, 0:32])
            end(dve)
            begin(dve, 22)

            def clip(h):
                dve.wait_ge(s["seg_sum"], h + 1)
                if h >= 2:
                    dve.wait_ge(s["ssd_out"], h - 1)
                for st in range(TT):
                    v.tensor_scalar(seg[:, h % 2, 2 * P * st:2 * P * st + (2 - st) * P], bank[:, h % 2, st * P:T],
                                    dts[:, 64 + st * 16 + h:65 + st * 16 + h], 0.0, ALU.subtract, ALU.min)\
                        .then_inc(s["seg_clipped"], 1)

            clip(0)
            for h in range(SH):
                if h + 1 < SH:
                    clip(h + 1)
                dve.wait_ge(s["seg_exp"], h + 1)
                g = h // 4
                for st in range(TT):
                    sl = seg[:, h % 2, 2 * P * st:2 * P * st + (2 - st) * P]
                    v.tensor_tensor(sl, sl, cb[:, g, st, st * P:T], ALU.mult).then_inc(s["seg_weighed"], 1)
            end(dve)
            begin(dve, 23)
            for t in range(TT):
                link(v.tensor_tensor(xs[:, t, :].rearrange("p (h c) -> p h c", c=64),
                                     xs[:, t, :].rearrange("p (h c) -> p h c", c=64),
                                     row("d_skip").unsqueeze(2).broadcast_to([P, SH, 64]), ALU.mult))
                link(v.tensor_tensor(y[:, t, 0:512], xs[:, t, 0:512], bank[:, 4 + 2 * t, :], ALU.add))
                link(v.tensor_tensor(y[:, t, 512:1024], xs[:, t, 512:1024], bank[:, 5 + 2 * t, :], ALU.add))
                link(v.tensor_tensor(y[:, t, :], y[:, t, :], z[:, t, :], ALU.mult))
                link(v.tensor_tensor(xs[:, t, :], y[:, t, :], y[:, t, :], ALU.mult))
                link(v.tensor_reduce(dts[:, 192 + 4 * t:196 + 4 * t], xs[:, t, :].rearrange("p (g c) -> p g c", c=256), AX, ALU.add))
            v.tensor_scalar(dts[:, 200:208], dts[:, 192:200], 1.0 / 256, EPS, ALU.mult, ALU.add).then_inc(s["group_mean"], 1)
            dve.wait_ge(s["group_root"], 1)
            link(v.reciprocal(dts[:, 192:200], dts[:, 208:216]))
            for t in range(TT):
                yg = y[:, t, :].rearrange("p (g c) -> p g c", c=256)
                v.tensor_tensor(yg, yg, dts[:, 192 + 4 * t:196 + 4 * t].unsqueeze(2).broadcast_to([P, SG, 256]), ALU.mult)
            end(dve)
            begin(dve, 24)
            turned_out("ssd", mix_t, KD, lambda b: col("ssd_g", b))
            end(dve)
            begin(dve, 25)
            ql, kl = lat[:, :, 16:400], lat[:, :, 512:768]
            sq1 = area("squares")[:, 0:768].rearrange("p (t c) -> p t c", t=TT)
            sq2 = area("x_scaled")[:, 0:512].rearrange("p (t c) -> p t c", t=TT)
            v.tensor_tensor(sq1, ql, ql, ALU.mult)
            link(v.tensor_tensor(sq2, kl, kl, ALU.mult))
            v.tensor_reduce(dts[:, 192:194], sq1, AX, ALU.add)
            link(v.tensor_reduce(dts[:, 194:196], sq2, AX, ALU.add))
            link(v.tensor_scalar(dts[:, 200:202], dts[:, 192:194], 1.0 / 384, EPS, ALU.mult, ALU.add))
            v.tensor_scalar(dts[:, 202:204], dts[:, 194:196], 1.0 / 256, EPS, ALU.mult, ALU.add).then_inc(s["group_mean"], 1)
            dve.wait_ge(s["group_root"], 2)
            link(v.reciprocal(dts[:, 192:196], dts[:, 208:212]))
            for t in range(TT):
                link(v.tensor_scalar(ql[:, t, :], ql[:, t, :], dts[:, 192 + t:193 + t], None, ALU.mult))
                link(v.tensor_scalar(kl[:, t, :], kl[:, t, :], dts[:, 194 + t:195 + t], None, ALU.mult))
            signal("latents_scaled")
            rope = area("rope")
            link(v.tensor_copy(rope[:, 0:2], pos_i[:, :]))
            for t in range(TT):
                link(v.tensor_scalar(rope[:, 32 + t * 16:48 + t * 16], const("inv_m"), rope[:, t:t + 1], None, ALU.mult))
            ang = rope[:, 32:64]
            BIG = 12582912.0
            for i, shift in enumerate((0.0, 0.25)):
                turns = rope[:, 64 + 32 * i:96 + 32 * i]
                r_ = rope[:, 128 + 32 * i:160 + 32 * i]
                link(v.tensor_scalar(turns, ang, 0.15915494309189535, shift, ALU.mult, ALU.add))
                link(v.tensor_scalar(turns, turns, BIG, None, ALU.add))
                link(v.tensor_scalar(turns, turns, BIG, None, ALU.subtract))
                link(v.scalar_tensor_tensor(out=r_, in0=turns, scalar=-6.28125, in1=ang, op0=ALU.mult, op1=ALU.add))
                link(v.scalar_tensor_tensor(out=r_, in0=turns, scalar=-0.0019340515136718750, in1=r_, op0=ALU.mult, op1=ALU.add))
                link(v.scalar_tensor_tensor(out=r_, in0=turns, scalar=-1.2556659146e-06, in1=r_, op0=ALU.mult, op1=ALU.add))
                if i:
                    link(v.tensor_scalar(r_, r_, 1.5707963267948966, None, ALU.add))
                link(v.tensor_scalar(r_, r_, 3.1415925, -3.1415925, ALU.min, ALU.max))
            signal("trig_arg")
            turned_out("latents", lat_t, 5, lambda b: col("q_g", b) if b < 3 else col("kv_g", b - 3))
            end(dve)
            begin(dve, 26)
            by_tokens("q_up", 3, [512] * 3, q)
            by_tokens("kv_up", 2, [512] * 4, kv)
            end(dve)
            begin(dve, 27)
            xsc = area("x_scaled")
            for t in range(TT):
                sin = rope[:, 192 + t * 16:208 + t * 16]
                cos = rope[:, 224 + t * 16:240 + t * 16]
                qh = q[:, t, :].rearrange("p (h c) -> p h c", c=MQ)
                w16 = lambda a: a.unsqueeze(1).broadcast_to([P, MH, 16])
                rotate(qh[:, :, 64:80], qh[:, :, 80:96], w16(cos), w16(sin),
                       lambda i: xsc[:, i * 256:(i + 1) * 256].rearrange("p (h c) -> p h c", c=16))
                rotate(lat[:, t, 768:784], lat[:, t, 784:800], cos, sin, lambda i: xsc[:, 1024 + i * 16:1040 + i * 16])
                kc = kcat[:, t, :].rearrange("p (h c) -> p h c", c=MQ)
                v.tensor_copy(kc[:, :, 0:64], kv[:, t, :].rearrange("p (h c) -> p h c", c=128)[:, :, 0:64])
                v.tensor_copy(kc[:, :, 64:96], lat[:, t, 768:800].unsqueeze(1).broadcast_to([P, MH, 32]))
            end(dve)
            begin(dve, 28)
            turned_out("mla_q", q_t, MH, rows_=MQ)
            end(dve)
            begin(dve, 29)
            turned_out("mla_k", k_t, MH, rows_=MQ)
            end(dve)
            begin(dve, 30)
            mask = const("mask").rearrange("p (t k) -> p t k", t=TT)

            def mla_shift(u):
                t = u % 2
                w = (t + 1) * P
                dve.wait_ge(s["mla_scores"], u + 1)
                if u >= 2:
                    dve.wait_ge(s["mla_exp"], u - 1)
                link(v.scalar_tensor_tensor(out=s_m[:, u % 2, 0:w], in0=bank[:, u % 2, 0:w], scalar=float(MQ) ** -0.5,
                                            in1=mask[:, t, 0:w], op0=ALU.mult, op1=ALU.add))
                v.tensor_reduce(sm[:, u % 2, 0:1], s_m[:, u % 2, 0:w], AX, ALU.max, negate=True).then_inc(s["mla_shift"], 1)

            mla_shift(0)
            for u in range(2 * MH):
                h, t = u // 2, u % 2
                dve.wait_ge(s["mla_exp"], u + 1)
                link(v.reciprocal(sm[:, u % 2, 2:3], sm[:, u % 2, 1:2]))
                if u + 1 < 2 * MH:
                    mla_shift(u + 1)
                dve.wait_ge(s["mla_out"], u + 1)
                v.tensor_scalar(o_m[:, t, h * 64:(h + 1) * 64], bank[:, 4 + u % 2, 0:MV], sm[:, u % 2, 2:3], None, ALU.mult)\
                    .then_inc(s["mla_out_copied"], 1)
            end(dve)
            begin(dve, 31)
            turned_out("mla_out", mix_t[:, 8:16, :], KD)
            end(dve)
            begin(dve, 32)
            into_residual(SLOT["w_out_2"] + 16)
            end(dve)
            begin(dve, 33)
            norm(NORMS["mem"], mem)
            turned_out("norm_mem", mem_t, KD, lambda b: col("mem_g", b))
            end(dve)
            begin(dve, 34)
            norm(NORMS["memx"], xres)
            turned_out("norm_memx", h_t, KD, lambda b: col("memx_g", b))
            end(dve)
            begin(dve, 35)
            by_channels("mem_k", 8, mk_t)
            end(dve)
            begin(dve, 36)
            by_tokens("mem_v", KD, [512, 512], mv)
            end(dve)
            begin(dve, 37)
            by_channels("mem_q", 8, mq_t)
            end(dve)
            begin(dve, 38)

            def mem_shift(u):
                dve.wait_ge(s["mem_scores"], u + 1)
                if u >= 2:
                    dve.wait_ge(s["mem_exp"], u - 1)
                link(v.tensor_reduce(sm[:, u % 2, 3:4], bank[:, u % 2, 0:T], AX, ALU.max))
                v.tensor_scalar(sm[:, u % 2, 0:1], sm[:, u % 2, 3:4], -0.0625, None, ALU.mult).then_inc(s["mem_shift"], 1)

            mem_shift(0)
            for u in range(8):
                h, t = u // 2, u % 2
                if u + 1 < 8:
                    mem_shift(u + 1)
                dve.wait_ge(s["mem_exp"], u + 1)
                link(v.reciprocal(sm[:, u % 2, 2:3], sm[:, u % 2, 1:2]))
                v.tensor_scalar(e_x[:, u % 2, :], e_x[:, u % 2, :], sm[:, u % 2, 2:3], None, ALU.mult).then_inc(s["mem_scaled"], 1)
                if t == 1:
                    dve.wait_ge(s["mem_out"], h + 1)
                    v.tensor_copy(h_t[:, 2 * h:2 * h + 2, :], bank[:, 4 + h % 2, :].rearrange("p (e t) -> p e t", e=2))\
                        .then_inc(s["mem_out_copied"], 1)
            end(dve)
            begin(dve, 39)
            into_residual(SLOT["mem_o"] + 8)
            end(dve)
            begin(dve, 40)
            norm(NORMS["ffn2"], xres)
            turned_out("norm_ffn", h_t, KD, lambda b: col("ffn2_g", b))
            end(dve)
            begin(dve, 41)
            F = SLOT["ffn"]

            def ffn_filter(k, u, half, dst, name, count):
                b = bank[:, 4 + 2 * u + half, :]
                c0 = COL["fw"][0] + half * 66
                w = lambda d: cols[:, bass.ds(k * 3 + (c0 + 2 - d), 1)]
                v.tensor_scalar(dst, b[:, 0:T], w(0), cols[:, bass.ds(k + (COL["fb"][0] + half * 22), 1)], ALU.mult, ALU.add)\
                    .then_inc(s["filter_step"], 1)
                dve.wait_ge(s["filter_step"], count)
                v.scalar_tensor_tensor(out=dst[:, 1:T], in0=b[:, 0:T - 1], scalar=w(1), in1=dst[:, 1:T],
                                       op0=ALU.mult, op1=ALU.add).then_inc(s["filter_step"], 1)
                dve.wait_ge(s["filter_step"], count + 1)
                v.scalar_tensor_tensor(out=dst[:, 2:T], in0=b[:, 0:T - 2], scalar=w(2), in1=dst[:, 2:T],
                                       op0=ALU.mult, op1=ALU.add).then_inc(s[name], 1)

            def ffn_block(k, u, spent, r4, down_spent):
                dve.wait_ge(s["spent"], spent)
                ffn_filter(k, u, 0, work[:, 0, u * T:(u + 1) * T], "ffn_conv_g", r4 + 1)
                dve.wait_ge(s["spent"], spent + 1)
                ffn_filter(k, u, 1, work[:, 1, u * T:(u + 1) * T], "ffn_conv_v", r4 + 3)
                dve.wait_ge(s["ffn_silu"], k + 1)
                dve.wait_ge(s["ffn_conv_v"], k + 1)
                if down_spent is not None:
                    dve.wait_ge(s["spent"], down_spent)
                v.tensor_tensor(work[:, 2, u * T:(u + 1) * T], work[:, 0, u * T:(u + 1) * T],
                                work[:, 1, u * T:(u + 1) * T], ALU.mult).then_inc(s["ffn_act"], 1)

            ffn_block(0, 0, F + 1, 0, None)
            ffn_block(1, 1, F + 3, 4, None)
            with dve.Fori(1, FF // 2) as r:
                for u in range(2):
                    k = r * 2 + u
                    ffn_block(k, u, r * 6 + (F + 3 * u), r * 8 + 4 * u, r * 6 + (F + 3 * u - 1))
            end(dve)
            begin(dve, 42)
            into_residual(F + 3 * FF)
            signal("residual_ready")
            norm(NORMS["final2"], xres)
            dve.wait_ge(s["norm_scaled"], 2 * NORMS["final2"] + 2)
            for t in range(TT):
                v.tensor_tensor(out_sb[:, t, :], x_scaled[:, t, :], row("final2_g"), ALU.mult).then_inc(s["norm_scaled"], 1)


def lay_out(i):
    a = {k: np.asarray(v) for k, v in i.items()}
    z = lambda *shape: np.zeros(shape, np.float32)

    def panels(w):
        K, C = w.shape
        wide = -(-C // 512) * 512
        if wide > C:
            w = np.concatenate([w, z(K, wide - C)], axis=1)
        p = w.reshape(K // P, P, wide // 512, 512).transpose(2, 0, 1, 3).reshape(-1, P, 512)
        if len(p) % 2:
            p = np.concatenate([p, z(1, P, 512)])
        return p.reshape(-1, 2, P, 512).transpose(0, 2, 1, 3).reshape(-1, P, 1024)

    def channels(w):
        return w.reshape(KD, P, -1, P).transpose(2, 1, 0, 3).reshape(-1, P, 1024)

    def deep(w):
        return w.reshape(-1, P, D)

    def interleave(ahead, *parts):
        n = len(parts[-1])
        out = [p[0:1] for p in parts[:-1]]
        for k in range(n):
            if k + 1 < n:
                out += [p[k + 1:k + 2] for p in parts[:-1]]
            out.append(parts[-1][k:k + 1])
        return np.concatenate(out)

    w2 = a["w_in_2"][0]
    sub = a["peer_sub_keys"][0].transpose(3, 0, 1, 2).reshape(P, 2, 1024).transpose(1, 0, 2)
    ffn = channels(a["w_ffn_up_2"][0])
    order = [panels(a["w_in"][0]), deep(a["w_out"][0]), channels(a["peer_w_query"][0]), sub,
             interleave(1, a["peer_u"][0].reshape(NK, NK, KD, P).transpose(0, 3, 2, 1).reshape(NK, P, 1024),
                        a["peer_v"][0].reshape(NK, P, D)),
             panels(w2[:, 0:1024]), panels(w2[:, 3072:3072 + DTQ]), panels(w2[:, 3072 + DTQ:]),
             channels(w2[:, 1024:3072]), panels(a["mla_w_q_up_2"][0]), panels(a["mla_w_kv_up_2"][0]),
             deep(a["w_out_2"][0]), channels(a["w_mem_k_2"][0]), panels(a["w_mem_v_2"][0]),
             channels(a["w_mem_q_2"][0]), deep(a["w_mem_o_2"][0]),
             interleave(1, ffn[:FF], ffn[FF:], deep(a["w_ffn_down_2"][0]))]
    assert [len(o) for o in order] == [n for _, n in STAGES]
    by_part = lambda v: v.reshape(-1, P).T
    taps = lambda v: v.reshape(v.shape[0], -1, P).transpose(2, 1, 0).reshape(P, -1)
    cols = [by_part(a[n].reshape(-1)) for n in ("attn_norm_g", "ffn_norm_g", "norm_mix_w_2", "norm_mem_w_2", "norm_memx_w_2",
                                                "norm_ffn_w_2", "ssd_norm_w_2", "mla_q_norm_w_2", "mla_kv_norm_w_2")]
    cols += [taps(a["ssd_conv_w_2"][0]), by_part(a["ssd_conv_b_2"].reshape(-1)),
             taps(a["ffn_conv_w_2"][0]), by_part(a["ffn_conv_b_2"].reshape(-1))]
    rows = np.concatenate([a[n].reshape(-1) for n in ("diff_norm_g", "ret_norm_g", "diff_lambda", "ret_log_decay", "final_norm_g",
                                                      "norm_final_w_2", "ssd_dt_bias_2", "ssd_a_log_2", "ssd_d_2")])
    by_token = lambda v: np.ascontiguousarray(v.reshape(TT, P, -1).transpose(1, 0, 2))
    return {
        "weights": np.concatenate(order),
        "consts": CONST,
        "cols": np.ascontiguousarray(np.concatenate(cols, axis=1)),
        "rows": np.ascontiguousarray(np.broadcast_to(rows, (P, len(rows)))),
        "x": by_token(a["x"]),
        "mem": by_token(a["mem_2"]),
        "positions": np.ascontiguousarray(a["positions_2"].reshape(TT, P).T),
    }


def kernel(**inputs):
    import concourse.bacc as bacc
    from concourse.bass_utils import run_bass_kernel_spmd

    arrays = lay_out(inputs)
    nc = bacc.Bacc("TRN2", target_bir_lowering=False, num_devices=1)
    args = [nc.dram_tensor(name + "_in", v.shape, mybir.dt.from_np(v.dtype), kind="ExternalInput").ap()
            for name, v in arrays.items()]
    out = nc.dram_tensor("out", (P, TT, D), F32, kind="ExternalOutput").ap()
    two_blocks(nc, *args, out)
    r = run_bass_kernel_spmd(nc, [{n + "_in": v for n, v in arrays.items()}], core_ids=[0])
    got = r.results[0]["out"]
    return got.transpose(1, 0, 2).reshape(1, T, D)
```

```python
from contextlib import ExitStack

import numpy as np

import concourse.bass as bass
from concourse import mybir

ALU = mybir.AluOpType
ACT = mybir.ActivationFunctionType
F32 = mybir.dt.float32
F32R = mybir.dt.float32r
I32 = mybir.dt.int32
U32 = mybir.dt.uint32
AX = mybir.AxisListType.X

P = 128
T, D = 256, 1024
TT = T // P
KD = D // P
EPS = 1e-6

HD = 4
LAMBDA_INIT = 0.2
PH, TOPK, NK = 8, 16, 128
SH, SP_, SG = 16, 64, 4
MH, MNOPE, MROPE, MV = 16, 64, 32, 64
MQ = MNOPE + MROPE
DTQ, KVR = 16 + 384, 256 + 32
FF = 2816 // P
NEG = -1.0e30

NR = 3
NS = 3

STAGES = [("w_in", 24), ("w_out", 8), ("w_query", 16), ("sub_keys", 2), ("experts", 2 * NK),
          ("z", 8), ("dt_q", 4), ("kv_rope", 4), ("xbc", 16), ("q_up", 5), ("kv_up", 4),
          ("w_out_2", 16), ("mem_k", 8), ("mem_v", 8), ("mem_q", 8), ("mem_o", 8), ("ffn", 3 * FF)]
SLOT, _n = {}, 0
for _name, _k in STAGES:
    SLOT[_name] = _n
    _n += _k
N_SLOTS = _n

TURNS = [("attn_norm", 4), ("qk", 6), ("mix", 4), ("ffn_norm", 4), ("chosen", 2), ("norm_mix", 4),
         ("xs", 4), ("ssd", 4), ("latents", 3), ("mla_q", 8), ("mla_k", 8), ("mla_out", 4),
         ("norm_mem", 4), ("norm_memx", 4), ("norm_ffn", 4)]
COPIES = [("w_in", 6, 6), ("z", 2, 2), ("dt_q", 1, 1), ("kv_rope", 1, 1),
          ("q_up", 3, 3), ("kv_up", 4, 4), ("mem_k", 4, 4), ("mem_v", 2, 2), ("mem_q", 4, 4)]


def _bases():
    turn, at, av = {}, 0, 0
    b = 0
    for name, n in TURNS:
        turn[name] = (b, at, av, n)
        b += n
        if name in ("qk", "chosen", "xs", "mla_q", "mla_k"):
            at, av = at + (n + 1) // 2, av + n // 2
    copy, ca, cv = {}, 0, 0
    for name, a, v in COPIES:
        copy[name] = (ca, cv)
        ca, cv = ca + a, cv + v
    return turn, copy


TURN, COPY = _bases()
SPLIT, _n = {}, 0
for _name, _k in [("attn_norm", 8), ("mix", 8), ("ffn_norm", 8), ("w_query", 16), ("norm_mix", 8), ("ssd", 8),
                  ("latents", 5), ("mla_out", 8), ("norm_mem", 8), ("norm_memx", 8), ("norm_ffn", 8)]:
    SPLIT[_name] = _n
    _n += _k
NORMS = {"attn": 0, "ffn": 1, "final1": 2, "mix": 3, "mem": 4, "memx": 5, "ffn2": 6, "final2": 7}



def shape_constants():
    f = np.float32
    pos = np.arange(T, dtype=f)
    rot = 16
    inv = np.power(f(500000.0), -np.arange(rot // 2, dtype=f) * f(2.0) / f(rot)).astype(f)
    ret = (f(1.0) / np.power(f(10000.0), np.linspace(0.0, 1.0, 32, dtype=f))).astype(f)
    mla = (f(1.0) / np.power(f(10000.0), np.arange(0, 32, 2, dtype=f) / f(32))).astype(f)
    by_token = lambda a: a.reshape(TT, P, -1).transpose(1, 0, 2).reshape(P, -1)
    a1, a2 = pos[:, None] * inv[None], pos[:, None] * ret[None]
    i, j = np.arange(T)[None, :], np.arange(T)[:, None]
    parts = [
        ("ident", np.eye(P)),
        ("iota", np.broadcast_to(np.arange(P), (P, P))),
        ("cos_d", by_token(np.cos(a1))), ("sin_d", by_token(np.sin(a1))),
        ("cos_r", by_token(np.cos(a2))), ("sin_r", by_token(np.sin(a2))),
        ("inv_m", np.broadcast_to(mla, (P, 16))),
        ("later", by_token(np.maximum(i - j, 0))),
        ("earlier", by_token(np.maximum(j - i, 0))),
        ("tri", by_token((j <= i))),
        ("mask", by_token(np.where(i // 64 <= j // 64, 0.0, NEG))),
    ]
    at, n = {}, 0
    for name, a in parts:
        at[name] = (n, n + a.shape[1])
        n += a.shape[1]
    return np.concatenate([np.asarray(a, f) for _, a in parts], axis=1), at


CONST, CAT = shape_constants()
NCONST = CAT["later"][0]

COLS = [("attn_g", 8), ("ffn_g", 8), ("mix_g", 8), ("mem_g", 8), ("memx_g", 8), ("ffn2_g", 8),
        ("ssd_g", 8), ("q_g", 3), ("kv_g", 2), ("xw", 64), ("xb", 16), ("fw", 44 * 3), ("fb", 44)]
ROWS = [("diff_g", 128), ("ret_g", 512), ("lam", 256), ("decay", 8), ("dt_bias", 16), ("a_log", 16), ("d_skip", 16),
        ("final1_g", 1024), ("final2_g", 1024)]


def _places(parts):
    at, n = {}, 0
    for name, k in parts:
        at[name] = (n, n + k)
        n += k
    return at, n


COL, NCOLS = _places(COLS)
ROW, _ = _places(ROWS)
NROWS = ROW["final1_g"][0]

AREA = dict(
    x_scaled=(24576, 26624), squares=(26624, 27648),
    proj=(0, 6144), qk_t=(6144, 9216), decay=(9216, 11264), gate_r=(11264, 12288), e_diff=(12288, 13312),
    a_diff=(13312, 13824), at_diff=(13824, 14336), o_diff=(14336, 15360), p_ret=(15360, 17408),
    later_earlier=(27648, 28672), final_g=(31744, 32768), tri=(22016, 22528), mask=(27136, 27648),
    o_ret=(17408, 18432), mix=(18432, 20480), rot=(20480, 22528), stat=(22528, 22784),
    pq_hi=(18432, 22528), pq_lo=(22528, 26624), keys=(4096, 8192), spare=(8192, 8704), vals=(8704, 9216), idx=(9216, 9728), idxf=(9728, 10240),
    cand=(10240, 14336), best=(14336, 14592), pos=(14592, 14848), hi=(14848, 15104), lo=(15104, 15360),
    eq=(15360, 17408), chosen=(17408, 18176), gst=(18176, 18432),
    z=(0, 2048), lat=(2048, 4096), xc=(4096, 8192), xs=(8192, 10240), xdt=(10240, 12288), cb=(12288, 14336),
    seg=(14336, 15360), y=(15360, 17408), dts=(17408, 17920), m_hi=(17920, 19968), m_lo=(19968, 22016), lat_hi=(22016, 23296), lat_lo=(24576, 25856),
    rope=(23296, 24576),
    q=(4096, 7168), kv=(7168, 11264), kcat=(11264, 14336), q_t=(27648, 31744), k_t=(0, 4096),
    s_m=(14336, 14848), e_m=(14848, 15360), et_m=(15360, 15872), o_m=(15872, 17920),
    mem=(0, 2048), mem_hi=(2048, 4096), mem_lo=(12288, 14336), mk_t=(4096, 6144), mv=(6144, 8192), mq_t=(8192, 10240),
    e_x=(10240, 10752), et_x=(10752, 11776),
    gate_f=(0, 512), value_f=(512, 1024), out=(0, 2048),
)


def two_blocks(nc, weights, consts, cols_in, rows_in, x_in, mem_in, pos_in, out):
    with ExitStack() as ctx:
        def sb(name, shape, dt=F32):
            return ctx.enter_context(nc.sbuf_tensor(name, shape, dt))

        base = (nc.sbuf_base + 31) // 32 * 32
        arena = sb("arena", [P, NK * T])
        work = sb("work", [P, 9 * T])
        ring = sb("ring", [P, NR, 1024])
        w_hi, w_lo = sb("w_hi", [P, NS, 1024], F32R), sb("w_lo", [P, NS, 1024], F32R)
        xres = sb("xres", [P, TT, D])
        h_t = sb("h_hi", [P, KD, T], F32R), sb("h_lo", [P, KD, T], F32R)
        cst = sb("cst", [P, NCONST])
        cols = sb("cols", [P, NCOLS])
        rows = sb("rows", [P, NROWS])
        chosen_t = sb("chosen_t", [P, 3, T])
        ssq = sb("ssq", [P, 8])
        rstd = sb("rstd", [P, 8])
        lam = sb("lam", [P, 8])
        log_g = sb("log_g", [P, 8])
        sm = sb("sm", [P, 2, 16])
        pos_i = sb("pos_i", [P, TT], I32)
        bank = ctx.enter_context(nc.psum_tensor("bank", [P, 8, 512], F32))

        def area(name, pattern=None, **kw):
            a, b = AREA[name]
            v = arena[:, a:b]
            return v.rearrange(pattern, **kw) if pattern else v

        def parts(name, column, blocks):
            return nc.alloc_sbuf_tensor_at(name, [P, blocks, T], F32R, offset=base + 4 * column)

        pq_t = parts("pq_hi", AREA["pq_hi"][0], 16), parts("pq_lo", AREA["pq_lo"][0], 16)
        m_t = parts("m_hi", AREA["m_hi"][0], KD), parts("m_lo", AREA["m_lo"][0], KD)
        lat_t = parts("lat_hi", AREA["lat_hi"][0], 5), parts("lat_lo", AREA["lat_lo"][0], 5)
        mem_t = parts("mem_hi", AREA["mem_hi"][0], KD), parts("mem_lo", AREA["mem_lo"][0], KD)
        act_t = parts("act_hi", NK * T + 3 * T, 3), parts("act_lo", NK * T + 6 * T, 3)

        def const(name):
            if name in ("later", "earlier"):
                k = 512 * (name == "earlier")
                return area("later_earlier")[:, k:k + 512]
            if name in ("tri", "mask"):
                return area(name)
            return cst[:, CAT[name][0]:CAT[name][1]]

        def col(name, i, n=1):
            return cols[:, COL[name][0] + i:COL[name][0] + i + n]

        def row(name):
            return rows[:, ROW[name][0]:ROW[name][1]]

        ident = const("ident")
        x_scaled = area("x_scaled", "p (t d) -> p t d", t=TT)
        squares = area("squares")
        proj = area("proj", "p (t c) -> p t c", t=TT)
        qk_t = area("qk_t", "p (b t) -> p b t", t=T)
        decay = area("decay", "p (h j i) -> p h j i", h=HD, j=TT)
        gate_r = area("gate_r", "p (t c) -> p t c", t=TT)
        e_diff = area("e_diff", "p (b m k) -> p b m k", b=2, m=2)
        a_diff = area("a_diff", "p (b k) -> p b k", b=2)
        at_diff = area("at_diff", "p (b k q) -> p b k q", b=2, k=2)
        o_diff = area("o_diff", "p (t c) -> p t c", t=TT)
        p_ret = area("p_ret", "p (h j i) -> p h j i", h=HD, j=TT)
        o_ret = area("o_ret", "p (t c) -> p t c", t=TT)
        mix = area("mix", "p (t c) -> p t c", t=TT)
        keys = area("keys", "p (t b c) -> p t b c", t=TT, c=512)
        gates = arena[:, :].rearrange("p (i t) -> p i t", t=T)
        z = area("z", "p (t c) -> p t c", t=TT)
        lat = area("lat", "p (t c) -> p t c", t=TT)
        xc = area("xc", "p (b t) -> p b t", t=T)
        xs = area("xs", "p (t c) -> p t c", t=TT)
        xdt = area("xdt", "p (t c) -> p t c", t=TT)
        cb = area("cb", "p (g s l) -> p g s l", g=SG, s=TT)
        seg = area("seg", "p (b l) -> p b l", b=2)
        y = area("y", "p (t c) -> p t c", t=TT)
        q = area("q", "p (t c) -> p t c", t=TT)
        kv = area("kv", "p (t c) -> p t c", t=TT)
        kcat = area("kcat", "p (t c) -> p t c", t=TT)
        q_t = area("q_t", "p (h t) -> p h t", t=T)
        k_t = area("k_t", "p (h t) -> p h t", t=T)
        s_m = area("s_m", "p (b k) -> p b k", b=2)
        e_m = area("e_m", "p (b k) -> p b k", b=2)
        et_m = area("et_m", "p (b k q) -> p b k q", b=2, k=2)
        o_m = area("o_m", "p (t c) -> p t c", t=TT)
        mem = area("mem", "p (t c) -> p t c", t=TT)
        mk_t = area("mk_t", "p (b t) -> p b t", t=T)
        mv = area("mv", "p (t c) -> p t c", t=TT)
        mq_t = area("mq_t", "p (b t) -> p b t", t=T)
        e_x = area("e_x", "p (b k) -> p b k", b=2)
        et_x = area("et_x", "p (b k q) -> p b k q", b=2, k=2)
        out_sb = area("out", "p (t c) -> p t c", t=TT)

        loaded = [ctx.enter_context(nc.semaphore(f"slot_loaded_{i}")) for i in range(NR)]
        s = {name: ctx.enter_context(nc.semaphore(name)) for name in (
            "x_loaded", "params_loaded", "mem_loaded", "out_stored",
            "mem_hi_made", "hi_made", "split", "spent", "phase", "split_act", "split_dve", "gain_loaded", "tri_loaded", "mask_loaded", "act_product", "act_hi_made", "dve_done", "act_done",
            "norm_summed", "norm_mean", "norm_rooted", "norm_factor", "norm_scaled",
            "turned", "turned_out_act", "turned_out_dve", "copied_act", "copied_dve",
            "lambda_products", "lambda_exp", "decay_arg", "decay_exp",
            "diff_scores", "diff_shift", "diff_exp", "diff_mixed", "diff_turned", "diff_t_copied", "diff_out", "diff_out_copied",
            "ret_scores", "ret_decayed", "ret_out", "ret_out_copied",
            "head_mean", "head_root", "gate_shifted", "gate_exp",
            "one_hot_1", "one_hot_2", "one_hot_gated", "spread", "spread_copied",
            "gelu_done", "weighed",
            "conv_done", "filter_step", "latents_scaled", "choice_made", "residual_ready",
            "dt_arg", "dt_e", "dt_l", "dt_scaled", "cum_done", "cb_done", "cb_masked",
            "seg_sum", "seg_clipped", "seg_exp", "seg_weighed", "ssd_out",
            "group_mean", "group_root", "trig_arg", "trig_done",
            "mla_scores", "mla_shift", "mla_exp", "mla_turned", "mla_t_copied", "mla_out", "mla_out_copied",
            "mem_scores", "mem_shift", "mem_exp", "mem_scaled", "mem_turned", "mem_t_copied", "mem_out", "mem_out_copied",
            "ffn_conv_g", "ffn_conv_v", "ffn_silu", "ffn_act",
        )}

        def wait_slot(pe, n):
            pe.wait_ge(s["split"], n + 1)

        def begin(eng, n):
            if n:
                eng.wait_ge(s["phase"], 3 * n)

        def end(eng):
            eng.drain().then_inc(s["phase"], 1)

        block = ctx.enter_context(nc.Block())

        @block.sync
        def _(sp):
            def slot_load(n, k):
                src = weights[bass.ds(n, 1)].rearrange("a p f -> p (a f)")
                sp.dma_start(ring[:, k, :], src).then_inc(loaded[k], 16)

            total = N_SLOTS
            sp.dma_start(xres[:, :, :], x_in).then_inc(s["x_loaded"], 16)
            for n in range(NR):
                slot_load(n, n)
            full = (total - NR) // NR
            with sp.Fori(1, full + 1) as r:
                for k in range(NR):
                    sp.wait_ge(s["split"], r * NR + (k + 1 - NR))
                    slot_load(r * NR + k, k)
            for n in range((full + 1) * NR, total):
                sp.wait_ge(s["split"], n + 1 - NR)
                slot_load(n, n % NR)

        @block.gpsimd
        def _(pool):
            def lo_part(n, k):
                pool.wait_ge(s["hi_made"], n + 1)
                nc.gpsimd.tensor_tensor(w_lo[:, k, :], ring[:, k, :], w_hi[:, k, :].bitcast(F32), ALU.subtract)\
                    .then_inc(s["split"], 1)

            def lo_parts(first, end_):
                n = first
                while n < end_ and n % NS:
                    lo_part(n, n % NS)
                    n += 1
                rounds = (end_ - n) // NS
                with pool.Fori(0, rounds) as r:
                    for k in range(NS):
                        lo_part(r * NS + (n + k), k)
                for m in range(n + rounds * NS, end_):
                    lo_part(m, m % NS)

            pool.dma_start(cols[:, :], cols_in).then_inc(s["params_loaded"], 16)
            pool.dma_start(cst[:, :], consts[:, 0:NCONST]).then_inc(s["params_loaded"], 16)
            pool.dma_start(rows[:, :], rows_in[:, 0:NROWS]).then_inc(s["params_loaded"], 16)
            pool.dma_start(pos_i[:, :], pos_in).then_inc(s["params_loaded"], 16)
            pool.dma_start(area("later_earlier"), consts[:, NCONST:NCONST + 1024]).then_inc(s["params_loaded"], 16)
            lo_parts(0, SLOT["experts"] + NS)
            begin(pool, 14)
            one_hots = lambda b: work[:, b * 512:(b + 1) * 512].rearrange("p (t k) -> p t k", t=4)

            def gated(g, u):
                pool.wait_ge(s["one_hot_1"], g + 1)
                g4 = chosen_t[:, 2, bass.ds(g * 4, 4)].unsqueeze(2).broadcast_to([P, 4, NK])
                nc.gpsimd.tensor_tensor(one_hots(u), one_hots(u), g4, ALU.mult).then_inc(s["one_hot_gated"], 1)

            with pool.Fori(0, T // 8) as r:
                for u in range(2):
                    gated(r * 2 + u, u)
            lo_parts(SLOT["experts"] + NS, N_SLOTS)

        @block.tensor
        def _(pe):
            def product(out_, a, b, start, stop, **kw):
                pe.matmul(out_, a[0], b[0], start=start, stop=False, **kw)
                pe.matmul(out_, a[0], b[1], start=False, stop=False, **kw)
                return pe.matmul(out_, a[1], b[0], start=False, stop=stop, **kw)

            def both(pair, *index):
                return [x[index] for x in pair]

            every = slice(0, P)
            w_parts = (w_hi, w_lo)

            def turn(name, source, blocks, width=P):
                first, act0, dve0, n = TURN[name]
                for b in range(blocks):
                    k = b // 2
                    if b % 2 == 0 and k >= 8:
                        if k % 2 == 0:
                            pe.wait_ge(s["turned_out_act"], act0 + (k - 8) // 2 + 1)
                        else:
                            pe.wait_ge(s["turned_out_dve"], dve0 + (k - 8) // 2 + 1)
                    for t in range(TT):
                        at = (b % 2) * T + t * P
                        mm = pe.transpose(bank[0:width, k % 8, at:at + P], source(b, t), ident)
                    if b % 2 == 1 or b == blocks - 1:
                        mm.then_inc(s["turned"], 1)

            def norm_turn(name, which):
                pe.wait_ge(s["norm_scaled"], 2 * which + 2)
                turn(name, lambda b, t: x_scaled[:, t, b * P:(b + 1) * P], KD)

            def by_tokens(name, src, depth, widths, first_block=0):
                first, (act0, dve0) = SLOT[name], COPY[name]
                panels = len(widths) * depth
                for c, w in enumerate(widths):
                    if c >= 2:
                        pe.wait_ge(s["copied_act"], act0 + c - 1)
                        pe.wait_ge(s["copied_dve"], dve0 + c - 1)
                    for k in range(depth):
                        p = c * depth + k
                        n, half = first + p // 2, p % 2
                        if half == 0:
                            wait_slot(pe, n)
                        for t in range(TT):
                            mm = product(bank[:, 2 * (c % 2) + t, 0:w],
                                         both(src, every, first_block + k, slice(t * P, (t + 1) * P)),
                                         both(w_parts, every, n % NS, slice(half * 512, half * 512 + w)),
                                         start=(k == 0), stop=(k == depth - 1))
                        if half == 1 or p == panels - 1:
                            mm.then_inc(s["spent"], 1)

            def by_channels(name, src, blocks, free):
                for j in range(blocks):
                    n = SLOT[name] + j
                    if j >= 4:
                        free(j)
                    wait_slot(pe, n)
                    for k in range(KD):
                        mm = product(bank[:, j % 4, 0:T], both(w_parts, every, n % NS, slice(k * P, (k + 1) * P)),
                                     both(src, every, k, slice(0, T)), start=(k == 0), stop=(k == KD - 1))
                    mm.then_inc(s["spent"], 1)

            def free_by(name):
                act0, dve0 = COPY[name]

                def free(j):
                    if j % 2 == 0:
                        pe.wait_ge(s["copied_act"], act0 + (j - 4) // 2 + 1)
                    else:
                        pe.wait_ge(s["copied_dve"], dve0 + (j - 4) // 2 + 1)
                return free

            def into_residual(name, src, depth):
                for k in range(depth):
                    n = SLOT[name] + k
                    wait_slot(pe, n)
                    for t in range(TT):
                        for h in range(2):
                            mm = product(bank[:, 2 * t + h, :],
                                         both(src[k // KD], every, k % KD, slice(t * P, (t + 1) * P)),
                                         both(w_parts, every, n % NS, slice(h * 512, (h + 1) * 512)),
                                         start=(k == 0), stop=(k == depth - 1))
                    mm.then_inc(s["spent"], 1)

            pe.wait_ge(s["params_loaded"], 80)
            norm_turn("attn_norm", NORMS["attn"])
            end(pe)
            begin(pe, 1)
            by_tokens("w_in", h_t, KD, [512] * 6)
            end(pe)
            begin(pe, 2)
            end(pe)
            begin(pe, 3)
            turn("qk", lambda b, t: proj[:, t, b * P:(b + 1) * P] if b < 8 else
                 proj[:, t, 1536 + (b - 8) * P:1536 + (b - 7) * P], 12)
            end(pe)
            begin(pe, 4)
            units = [(h, t) for h in range(HD) for t in range(TT)]

            def diff_scores(u):
                h, t = units[u]
                if u >= 2:
                    pe.wait_ge(s["diff_exp"], u - 1)
                for m in range(2):
                    r = slice(m * 64, m * 64 + 64)
                    mm = pe.matmul(bank[:, 2 * (u % 2) + m, 0:T], qk_t[r, h, t * P:(t + 1) * P],
                                   qk_t[r, 4 + h, :], start=True, stop=True)
                mm.then_inc(s["diff_scores"], 1)

            diff_scores(0)
            for u, (h, t) in enumerate(units):
                if u + 1 < len(units):
                    diff_scores(u + 1)
                pe.wait_ge(s["diff_mixed"], u + 1)
                if u >= 2:
                    pe.wait_ge(s["diff_t_copied"], u - 1)
                for k in range(2):
                    mm = pe.transpose(bank[:, 4 + u % 2, k * P:(k + 1) * P], a_diff[:, u % 2, k * P:(k + 1) * P], ident)
                mm.then_inc(s["diff_turned"], 1)
                pe.wait_ge(s["diff_t_copied"], u + 1)
                if u >= 2:
                    pe.wait_ge(s["diff_out_copied"], u - 1)
                for k in range(2):
                    mm = pe.matmul(bank[:, 6 + u % 2, 0:P], at_diff[:, u % 2, k, :],
                                   proj[:, k, 1024 + h * P:1024 + (h + 1) * P], start=(k == 0), stop=(k == 1))
                mm.then_inc(s["diff_out"], 1)
            end(pe)
            begin(pe, 5)

            def ret_scores(h):
                r = slice((h % 2) * 64, (h % 2) * 64 + 64)
                if h >= 2:
                    pe.wait_ge(s["ret_decayed"], h - 1)
                for j in range(TT):
                    mm = pe.matmul(bank[:, h % 2, j * T:(j + 1) * T], qk_t[r, 10 + h // 2, j * P:(j + 1) * P],
                                   qk_t[r, 8 + h // 2, :], start=True, stop=True)
                mm.then_inc(s["ret_scores"], 1)

            ret_scores(0)
            for h in range(HD):
                if h + 1 < HD:
                    ret_scores(h + 1)
                pe.wait_ge(s["ret_decayed"], h + 1)
                for t in range(TT):
                    for j in range(TT):
                        mm = pe.matmul(bank[:, 2 + t, h * P:(h + 1) * P], p_ret[:, h, j, t * P:(t + 1) * P],
                                       proj[:, j, 2048 + h * P:2048 + (h + 1) * P], start=(j == 0), stop=(j == 1))
                mm.then_inc(s["ret_out"], 1)
            end(pe)
            begin(pe, 6)
            end(pe)
            begin(pe, 7)
            turn("mix", lambda b, t: mix[:, t, b * P:(b + 1) * P], KD)
            end(pe)
            begin(pe, 8)
            into_residual("w_out", [h_t], KD)
            end(pe)
            begin(pe, 9)
            norm_turn("ffn_norm", NORMS["ffn"])
            end(pe)
            begin(pe, 10)
            by_channels("w_query", h_t, 16, lambda j: pe.wait_ge(s["split_dve"], j - 3))
            end(pe)
            begin(pe, 11)
            for b in range(4):
                n = SLOT["sub_keys"] + b // 2
                if b % 2 == 0:
                    wait_slot(pe, n)
                for t in range(TT):
                    for i in range(4):
                        c = (4 * b + i) % 8 * P
                        mm = product(bank[:, 2 * b + t, i * P:(i + 1) * P],
                                     both(pq_t, every, 4 * b + i, slice(t * P, (t + 1) * P)),
                                     both(w_parts, every, n % NS, slice(c, c + P)), start=True, stop=True)
                    if b % 2 == 1 and t == 1:
                        mm.then_inc(s["spent"], 1)
            end(pe)
            begin(pe, 12)
            turn_after_choice = area("chosen", "p (f c) -> p f c", f=6)
            pe.wait_ge(s["choice_made"], 1)
            turn("chosen", lambda b, t: turn_after_choice[:, b * 2 + t, :], 3)
            end(pe)
            begin(pe, 13)
            end(pe)
            begin(pe, 14)
            one_hots = lambda b: work[:, b * 512:(b + 1) * 512].rearrange("p (t k) -> p t k", t=4)

            def spread(g, u):
                pe.wait_ge(s["one_hot_gated"], g + 1)
                pe.wait_ge(s["one_hot_2"], g + 1)
                for i in range(4):
                    mm = pe.matmul(bank[:, u, i * P:(i + 1) * P], one_hots(2 + u)[:, i, :], one_hots(u)[:, i, :],
                                   start=True, stop=True)
                mm.then_inc(s["spread"], 1)

            spread(0, 0)
            spread(1, 1)
            with pe.Fori(1, T // 8) as r:
                for u in range(2):
                    pe.wait_ge(s["spread_copied"], r * 2 + (u - 1))
                    spread(r * 2 + u, u)
            end(pe)
            begin(pe, 15)
            X = SLOT["experts"]
            U3 = 3

            def down(n, k, u):
                pe.wait_ge(s["split"], n + 1)
                for c in range(KD):
                    mm = product(bank[:, 4 + u, 0:T], both(w_parts, every, k, slice(c * P, (c + 1) * P)),
                                 both(h_t, every, c, slice(0, T)), start=(c == 0), stop=(c == KD - 1))
                mm.then_inc(s["spent"], 1)

            def up(n, k, u, done, start=False, stop=False):
                pe.wait_ge(s["split"], n + 1)
                pe.wait_ge(s["weighed"], done)
                for t in range(TT):
                    for h in range(2):
                        mm = product(bank[:, 2 * t + h, :], both(act_t, every, u, slice(t * P, (t + 1) * P)),
                                     both(w_parts, every, k, slice(h * 512, (h + 1) * 512)), start=start, stop=stop,
                                     skip_group_check=True)
                mm.then_inc(s["spent"], 1)

            down(X, X % NS, 0)
            down(X + 1, (X + 1) % NS, 1)
            up(X + 2, (X + 2) % NS, 0, 1, start=True)
            with pe.Fori(0, (NK - 2) // U3) as r:
                for u in range(U3):
                    pe.wait_ge(s["gelu_done"], r * U3 + (u + 1))
                    n = X + 3 + 2 * u
                    down(r * (2 * U3) + n, n % NS, (2 + u) % U3)
                    up(r * (2 * U3) + (n + 1), (n + 1) % NS, (1 + u) % U3, r * U3 + (2 + u))
            n = X + 2 * NK - 1
            up(n, n % NS, (NK - 1) % U3, NK, stop=True)
            end(pe)
            begin(pe, 16)
            end(pe)
            begin(pe, 17)
            norm_turn("norm_mix", NORMS["mix"])
            end(pe)
            begin(pe, 18)
            by_tokens("z", h_t, KD, [512, 512])
            pe.wait_ge(s["copied_act"], COPY["z"][0] + 1)
            pe.wait_ge(s["copied_dve"], COPY["z"][1] + 1)
            by_tokens("dt_q", h_t, KD, [DTQ])
            end(pe)
            begin(pe, 19)
            by_tokens("kv_rope", h_t, KD, [KVR])
            end(pe)
            begin(pe, 20)
            by_channels("xbc", h_t, 16, lambda j: pe.wait_ge(s["conv_done"], 4 * (j - 3)))
            end(pe)
            begin(pe, 21)
            for t in range(TT):
                for b in range(2):
                    for i in range(4):
                        mm = pe.transpose(bank[:, 2 * t + b, i * P:(i + 1) * P], xc[:, 4 * b + i, t * P:(t + 1) * P], ident)
                    mm.then_inc(s["turned"], 1)
            for g in range(SG):
                for j in range(TT):
                    mm = pe.matmul(bank[:, 4 + g % 2, j * T:(j + 1) * T],
                                   xc[:, 8 + g, j * P:(j + 1) * P], xc[:, 12 + g, :], start=True, stop=True)
                mm.then_inc(s["cb_done"], 1)
                if g >= 1 and g + 1 < SG:
                    pe.wait_ge(s["cb_masked"], g)
            pe.wait_ge(s["dt_scaled"], 1)
            pe.wait_ge(s["tri_loaded"], 16)
            adt = area("dts")[:, 0:32].rearrange("p (t h) -> p t h", t=TT)
            tri = const("tri").rearrange("p (j l) -> p j l", j=TT)
            for t in range(TT):
                for j in range(t + 1):
                    mm = pe.matmul(bank[:, 6, t * 16:(t + 1) * 16], tri[:, j, t * P:(t + 1) * P], adt[:, j, :],
                                   start=(j == 0), stop=(j == t))
            mm.then_inc(s["cum_done"], 1)
            end(pe)
            begin(pe, 22)

            def seg_sum(h):
                if h >= 2:
                    pe.wait_ge(s["seg_clipped"], 2 * (h - 1))
                for j in range(TT):
                    mm = pe.matmul(bank[:, h % 2, 0:T], adt[:, j, h:h + 1].to_broadcast([P, P]), tri[:, j, :],
                                   start=(j == 0), stop=(j == 1))
                mm.then_inc(s["seg_sum"], 1)

            seg_sum(0)
            for h in range(SH):
                if h + 1 < SH:
                    seg_sum(h + 1)
                pe.wait_ge(s["seg_weighed"], 2 * (h + 1))
                lo = (h % 8) * 64
                pe.matmul(bank[:, 4 + h // 8, lo:lo + 64], seg[:, h % 2, 0:P], xdt[:, 0, h * 64:(h + 1) * 64],
                          start=True, stop=True)
                pe.matmul(bank[:, 6 + h // 8, lo:lo + 64], seg[:, h % 2, P:2 * P], xdt[:, 0, h * 64:(h + 1) * 64],
                          start=True, stop=False)
                pe.matmul(bank[:, 6 + h // 8, lo:lo + 64], seg[:, h % 2, 2 * P:3 * P], xdt[:, 1, h * 64:(h + 1) * 64],
                          start=False, stop=True).then_inc(s["ssd_out"], 1)
            end(pe)
            begin(pe, 23)
            end(pe)
            begin(pe, 24)
            turn("ssd", lambda b, t: y[:, t, b * P:(b + 1) * P], KD)
            end(pe)
            begin(pe, 25)
            pe.wait_ge(s["latents_scaled"], 1)
            turn("latents", lambda b, t: lat[:, t, 16 + b * P:16 + (b + 1) * P] if b < 3 else
                 lat[:, t, 512 + (b - 3) * P:512 + (b - 2) * P], 5)
            end(pe)
            begin(pe, 26)
            by_tokens("q_up", lat_t, 3, [512] * 3)
            pe.wait_ge(s["copied_act"], COPY["q_up"][0] + 3)
            pe.wait_ge(s["copied_dve"], COPY["q_up"][1] + 3)
            by_tokens("kv_up", lat_t, 2, [512] * 4, first_block=3)
            end(pe)
            begin(pe, 27)
            end(pe)
            begin(pe, 28)
            turn("mla_q", lambda b, t: q[:, t, b * MQ:(b + 1) * MQ], MH, MQ)
            end(pe)
            begin(pe, 29)
            turn("mla_k", lambda b, t: kcat[:, t, b * MQ:(b + 1) * MQ], MH, MQ)
            end(pe)
            begin(pe, 30)
            munits = [(h, t) for h in range(MH) for t in range(TT)]

            def mla_scores(u):
                h, t = munits[u]
                if u >= 2:
                    pe.wait_ge(s["mla_shift"], u - 1)
                pe.matmul(bank[:, u % 2, 0:(t + 1) * P], q_t[0:MQ, h, t * P:(t + 1) * P], k_t[0:MQ, h, 0:(t + 1) * P],
                          start=True, stop=True).then_inc(s["mla_scores"], 1)

            mla_scores(0)
            for u, (h, t) in enumerate(munits):
                if u + 1 < len(munits):
                    mla_scores(u + 1)
                pe.wait_ge(s["mla_exp"], u + 1)
                if u >= 2:
                    pe.wait_ge(s["mla_t_copied"], u - 1)
                for k in range(t + 1):
                    mm = pe.transpose(bank[:, 2 + u % 2, k * P:(k + 1) * P], e_m[:, u % 2, k * P:(k + 1) * P], ident)
                mm.then_inc(s["mla_turned"], 1)
                pe.wait_ge(s["mla_t_copied"], u + 1)
                if u >= 2:
                    pe.wait_ge(s["mla_out_copied"], u - 1)
                for k in range(t + 1):
                    mm = pe.matmul(bank[:, 4 + u % 2, 0:MV], et_m[:, u % 2, k, :],
                                   kv[:, k, h * 128 + MNOPE:(h + 1) * 128], start=(k == 0), stop=(k == t))
                mm.then_inc(s["mla_out"], 1)
            end(pe)
            begin(pe, 31)
            turn("mla_out", lambda b, t: o_m[:, t, b * P:(b + 1) * P], KD)
            end(pe)
            begin(pe, 32)
            into_residual("w_out_2", [h_t, m_t], 16)
            end(pe)
            begin(pe, 33)
            norm_turn("norm_mem", NORMS["mem"])
            end(pe)
            begin(pe, 34)
            norm_turn("norm_memx", NORMS["memx"])
            end(pe)
            begin(pe, 35)
            by_channels("mem_k", mem_t, 8, free_by("mem_k"))
            end(pe)
            begin(pe, 36)
            by_tokens("mem_v", mem_t, KD, [512, 512])
            end(pe)
            begin(pe, 37)
            by_channels("mem_q", h_t, 8, free_by("mem_q"))
            end(pe)
            begin(pe, 38)
            xunits = [(h, t) for h in range(4) for t in range(TT)]

            def mem_scores(u):
                h, t = xunits[u]
                if u >= 2:
                    pe.wait_ge(s["mem_exp"], u - 1)
                for k in range(2):
                    mm = pe.matmul(bank[:, u % 2, 0:T], mq_t[:, 2 * h + k, t * P:(t + 1) * P], mk_t[:, 2 * h + k, :],
                                   start=(k == 0), stop=(k == 1))
                mm.then_inc(s["mem_scores"], 1)

            mem_scores(0)
            for u, (h, t) in enumerate(xunits):
                if u + 1 < len(xunits):
                    mem_scores(u + 1)
                pe.wait_ge(s["mem_scaled"], u + 1)
                if u >= 2:
                    pe.wait_ge(s["mem_t_copied"], u - 1)
                for k in range(2):
                    mm = pe.transpose(bank[:, 2 + u % 2, k * P:(k + 1) * P], e_x[:, u % 2, k * P:(k + 1) * P], ident)
                mm.then_inc(s["mem_turned"], 1)
                if t == 1:
                    pe.wait_ge(s["mem_t_copied"], u + 1)
                    if h >= 2:
                        pe.wait_ge(s["mem_out_copied"], h - 1)
                    for e in range(2):
                        for k in range(2):
                            mm = pe.matmul(bank[:, 4 + h % 2, e * T:(e + 1) * T],
                                           mv[:, k, h * T + e * P:h * T + (e + 1) * P], et_x[:, h % 2, k, :],
                                           start=(k == 0), stop=(k == 1))
                    mm.then_inc(s["mem_out"], 1)
            end(pe)
            begin(pe, 39)
            into_residual("mem_o", [h_t], KD)
            end(pe)
            begin(pe, 40)
            norm_turn("norm_ffn", NORMS["ffn2"])
            end(pe)
            begin(pe, 41)
            F = SLOT["ffn"]
            U2 = 2

            def ffn_up(n, k, u):
                for half in range(2):
                    pe.wait_ge(s["split"], n + (half + 1))
                    for c in range(KD):
                        mm = product(bank[:, 4 + 2 * u + half, 0:T],
                                     both(w_parts, every, (k + half) % NS, slice(c * P, (c + 1) * P)),
                                     both(h_t, every, c, slice(0, T)), start=(c == 0), stop=(c == KD - 1))
                    mm.then_inc(s["spent"], 1)

            def ffn_down(n, k, u, done, start=False, stop=False):
                pe.wait_ge(s["split"], n + 1)
                pe.wait_ge(s["ffn_act"], done)
                for t in range(TT):
                    for h in range(2):
                        mm = product(bank[:, 2 * t + h, :], both(act_t, every, u, slice(t * P, (t + 1) * P)),
                                     both(w_parts, every, k % NS, slice(h * 512, (h + 1) * 512)), start=start, stop=stop,
                                     skip_group_check=True)
                mm.then_inc(s["spent"], 1)

            ffn_up(F, F, 0)
            ffn_up(F + 2, F + 2, 1)
            ffn_down(F + 4, F + 4, 0, 1, start=True)
            with pe.Fori(0, (FF - 2) // U2) as r:
                for u in range(U2):
                    pe.wait_ge(s["ffn_conv_v"], r * U2 + (1 + u))
                    n = F + 5 + 3 * u
                    ffn_up(r * (3 * U2) + n, n, u % 2)
                    ffn_down(r * (3 * U2) + (n + 2), n + 2, (1 + u) % 2, r * U2 + (2 + u))
            n = F + 3 * FF - 1
            ffn_down(n, n, (FF - 1) % 2, FF, stop=True)
            end(pe)

        @block.scalar
        def _(act):
            done = [0]

            def link(ins):
                done[0] += 1
                ins.then_inc(s["act_done"], 1)
                act.wait_ge(s["act_done"], done[0])

            made = [0]

            def hi_part(n, k, load):
                act.wait_ge(loaded[k], load)
                act.wait_ge(s["spent"], n - (NS - 1))
                nc.scalar.copy(w_hi[:, k, :], ring[:, k, :]).then_inc(s["hi_made"], 1)

            def hi_parts(upto):
                for n in range(made[0], upto):
                    if n < NS:
                        act.wait_ge(loaded[n], 16)
                        nc.scalar.copy(w_hi[:, n, :], ring[:, n, :]).then_inc(s["hi_made"], 1)
                    else:
                        hi_part(n, n % NS, 16 * (n // NR + 1))
                made[0] = max(made[0], upto)

            def turned_hi(name, dst, blocks, gain=None):
                for b in range(blocks):
                    if b % 2 == 0:
                        act.wait_ge(s["turned"], TURN[name][0] + b // 2 + 1)
                    at = bank[:, b // 2, (b % 2) * T:(b % 2 + 1) * T]
                    ins = nc.scalar.mul(dst[0][:, b, :], at, gain(b)) if gain else nc.scalar.copy(dst[0][:, b, :], at)
                    ins.then_inc(s["split_act"], 1)

            def turned_out(name, dst, blocks, gain=None, rows_=P):
                first, act0, dve0, n = TURN[name]
                for k in range(0, n, 2):
                    act.wait_ge(s["turned"], first + k + 1)
                    width = min(2, blocks - 2 * k)
                    if gain is None:
                        ins = nc.scalar.copy(dst[0:rows_, 2 * k:2 * k + width, :],
                                             bank[0:rows_, k % 8, 0:width * T].rearrange("p (b t) -> p b t", t=T))
                    else:
                        for i in range(width):
                            ins = nc.scalar.mul(dst[:, 2 * k + i, :], bank[:, k % 8, i * T:(i + 1) * T], gain(2 * k + i))
                    ins.then_inc(s["turned_out_act"], 1)

            def norm(which, src):
                for t in range(TT):
                    nc.scalar.activation(squares, src[:, t, :], ACT.Square, accum_out=ssq[:, t:t + 1]).then_inc(s["norm_summed"], 1)
                    act.wait_ge(s["norm_summed"], 2 * which + t + 1)
                act.wait_ge(s["norm_mean"], which + 1)
                nc.scalar.activation(rstd[:, 0:2], ssq[:, 2:4], ACT.Sqrt).then_inc(s["norm_rooted"], 1)
                act.wait_ge(s["norm_factor"], which + 1)
                nc.scalar.mul(x_scaled[:, 0, :], src[:, 0, :], rstd[:, 2:3]).then_inc(s["norm_scaled"], 1)

            def by_tokens(name, depth, widths, dst):
                for c, w in enumerate(widths):
                    n = SLOT[name] + ((c + 1) * depth + 1) // 2
                    hi_parts(n - 1 + NS)
                    act.wait_ge(s["spent"], n)
                    nc.scalar.copy(dst[:, 0, c * 512:c * 512 + w], bank[:, 2 * (c % 2), 0:w]).then_inc(s["copied_act"], 1)

            def by_channels(name, blocks, dst):
                for j in range(0, blocks, 2):
                    hi_parts(SLOT[name] + j + NS)
                    act.wait_ge(s["spent"], SLOT[name] + j + 1)
                    nc.scalar.copy(dst[:, j, :], bank[:, j % 4, 0:T]).then_inc(s["copied_act"], 1)
                hi_parts(SLOT[name] + blocks)

            act.wait_ge(s["x_loaded"], 16)
            norm(NORMS["attn"], xres)
            hi_parts(NS)
            act.wait_ge(s["params_loaded"], 80)
            turned_hi("attn_norm", h_t, KD, lambda b: col("attn_g", b))
            end(act)
            begin(act, 1)
            by_tokens("w_in", KD, [512] * 6, proj)
            end(act)
            begin(act, 2)
            nc.scalar.activation(gate_r[:, :, :], proj[:, :, 2560:3072], ACT.Silu)
            act.wait_ge(s["lambda_products"], 1)
            nc.scalar.activation(lam[:, 2:4], lam[:, 0:2], ACT.Exp).then_inc(s["lambda_exp"], 1)
            nc.scalar.activation(log_g[:, :], row("decay"), ACT.Exp).then_inc(s["lambda_exp"], 1)
            for h in range(HD):
                act.wait_ge(s["decay_arg"], h + 1)
                nc.scalar.activation(decay[:, h, :, :], decay[:, h, :, :], ACT.Exp)
            end(act)
            begin(act, 3)
            turned_out("qk", qk_t, 12)
            end(act)
            begin(act, 4)
            for u in range(8):
                act.wait_ge(s["diff_shift"], u + 1)
                if u >= 2:
                    act.wait_ge(s["diff_mixed"], u - 1)
                for m in range(2):
                    ins = nc.scalar.activation(e_diff[:, u % 2, m, :], bank[:, 2 * (u % 2) + m, 0:T], ACT.Exp,
                                               bias=sm[:, u % 2, m:m + 1], scale=0.125,
                                               accum_out=sm[:, u % 2, 2 + m:3 + m])
                ins.then_inc(s["diff_exp"], 1)
                act.wait_ge(s["diff_turned"], u + 1)
                if u >= 2:
                    act.wait_ge(s["diff_out"], u - 1)
                nc.scalar.copy(at_diff[:, u % 2, :, :], bank[:, 4 + u % 2, 0:T].rearrange("p (k q) -> p k q", k=2))\
                    .then_inc(s["diff_t_copied"], 1)
            end(act)
            begin(act, 5)
            end(act)
            begin(act, 6)
            for i in range(2):
                act.wait_ge(s["head_mean"], i + 1)
                nc.scalar.activation(area("stat")[:, 32 * i + 16:32 * i + 24], area("stat")[:, 32 * i + 8:32 * i + 16], ACT.Sqrt)\
                    .then_inc(s["head_root"], 1)
            end(act)
            begin(act, 7)
            turned_hi("mix", h_t, KD)
            end(act)
            begin(act, 8)
            hi_parts(SLOT["w_out"] + KD + NS - 1)
            end(act)
            begin(act, 9)
            norm(NORMS["ffn"], xres)
            turned_hi("ffn_norm", h_t, KD, lambda b: col("ffn_g", b))
            end(act)
            begin(act, 10)
            for j in range(16):
                n = SLOT["w_query"] + j
                hi_parts(n + NS)
                act.wait_ge(s["spent"], n + 1)
                nc.scalar.copy(pq_t[0][:, j, :], bank[:, j % 4, 0:T]).then_inc(s["split_act"], 1)
            end(act)
            begin(act, 11)
            for b in range(4):
                hi_parts(SLOT["sub_keys"] + b // 2 + NS)
                act.wait_ge(s["spent"], SLOT["sub_keys"] + b // 2 + 1)
                nc.scalar.copy(keys[:, 0, b, :], bank[:, 2 * b, :])
            hi_parts(SLOT["experts"] + NS)
            end(act)
            begin(act, 12)
            gst = area("gst")
            for t in range(TT):
                best = area("best", "p (t c) -> p t c", t=TT)[:, t, :]
                act.wait_ge(s["gate_shifted"], t + 1)
                nc.scalar.activation(best, best, ACT.Exp).then_inc(s["gate_exp"], 1)
            turned_out("chosen", chosen_t, 3)
            end(act)
            begin(act, 13)
            end(act)
            begin(act, 14)

            def table(g, u):
                act.wait_ge(s["spread"], g + 1)
                nc.scalar.copy(gates[:, :, bass.ds(g * 4, 4)], bank[:, u, :].rearrange("p (t i) -> p i t", t=4))\
                    .then_inc(s["spread_copied"], 1)

            with act.Fori(0, T // 8) as r:
                for u in range(2):
                    table(r * 2 + u, u)
            end(act)
            begin(act, 15)
            X = SLOT["experts"]
            U3 = 3

            def gelu(spent, u):
                act.wait_ge(s["spent"], spent)
                nc.scalar.activation(work[:, u * T:(u + 1) * T], bank[:, 4 + u, 0:T], ACT.Gelu).then_inc(s["gelu_done"], 1)

            hi_parts(X + NS)
            gelu(X + 1, 0)
            hi_parts(X + 4)
            gelu(X + 2, 1)
            hi_parts(X + 6)
            gelu(X + 4, 2)
            with act.Fori(1, NK // U3) as r:
                for u in range(U3):
                    for n in (X + 2 * u, X + 2 * u + 1):
                        hi_part(r * (2 * U3) + n, n % NS, r * (16 * 2 * U3 // NR) + 16 * (n // NR + 1))
                    act.wait_ge(s["weighed"], r * U3 + (u - 2))
                    gelu(r * (2 * U3) + (X + 2 * u), u)
            made[0] = X + 2 * (NK // U3 * U3)
            for k in range(NK // U3 * U3, NK):
                hi_parts(X + 2 * k + 2)
                act.wait_ge(s["weighed"], k - 2)
                gelu(X + 2 * k, k % U3)
            hi_parts(X + 2 * NK - 1 + NS)
            end(act)
            begin(act, 16)
            act.dma_start(area("final_g"), rows_in[:, ROW["final1_g"][0]:ROW["final1_g"][1]]).then_inc(s["gain_loaded"], 16)
            act.dma_start(area("tri"), consts[:, CAT["tri"][0]:CAT["tri"][1]]).then_inc(s["tri_loaded"], 16)
            act.wait_ge(s["residual_ready"], 1)
            norm(NORMS["final1"], xres)
            end(act)
            begin(act, 17)
            norm(NORMS["mix"], xres)
            turned_hi("norm_mix", h_t, KD, lambda b: col("mix_g", b))
            end(act)
            begin(act, 18)
            by_tokens("z", KD, [512, 512], z)
            by_tokens("dt_q", KD, [DTQ], lat)
            end(act)
            begin(act, 19)
            hi_parts(SLOT["kv_rope"] + 3 + NS)
            act.wait_ge(s["spent"], SLOT["kv_rope"] + 4)
            nc.scalar.copy(lat[:, 0, 512:512 + KVR], bank[:, 0, 0:KVR]).then_inc(s["copied_act"], 1)
            nc.scalar.activation(z[:, 0, :], z[:, 0, :], ACT.Silu)
            nc.scalar.activation(z[:, 1, :], z[:, 1, :], ACT.Silu)
            end(act)
            begin(act, 20)
            for j in range(16):
                hi_parts(SLOT["xbc"] + j + NS)
                act.wait_ge(s["conv_done"], 4 * (j + 1))
                nc.scalar.activation(xc[:, j, :], xc[:, j, :], ACT.Silu)
            end(act)
            begin(act, 21)
            dts = area("dts")
            act.wait_ge(s["dt_arg"], 1)
            nc.scalar.activation(dts[:, 96:128], dts[:, 64:96], ACT.Exp, scale=-1.0).then_inc(s["dt_e"], 1)
            act.wait_ge(s["dt_e"], 1)
            nc.scalar.activation(dts[:, 128:160], dts[:, 96:128], ACT.Ln, bias=1.0).then_inc(s["dt_l"], 1)
            nc.scalar.activation(dts[:, 160:176], row("a_log"), ACT.Exp).then_inc(s["dt_l"], 1)
            for k in range(0, 4, 2):
                act.wait_ge(s["turned"], TURN["xs"][0] + k + 1)
                t, b = k // 2, k % 2
                nc.scalar.copy(xs[:, t, b * 512:(b + 1) * 512], bank[:, k, :]).then_inc(s["turned_out_act"], 1)
            end(act)
            begin(act, 22)
            for h in range(SH):
                act.wait_ge(s["seg_clipped"], 2 * (h + 1))
                nc.scalar.activation(seg[:, h % 2, 0:3 * P], seg[:, h % 2, 0:3 * P], ACT.Exp).then_inc(s["seg_exp"], 1)
            end(act)
            begin(act, 23)
            act.wait_ge(s["group_mean"], 1)
            nc.scalar.activation(dts[:, 208:216], dts[:, 200:208], ACT.Sqrt).then_inc(s["group_root"], 1)
            end(act)
            begin(act, 24)
            turned_hi("ssd", h_t, KD, lambda b: col("ssd_g", b))
            end(act)
            begin(act, 25)
            act.wait_ge(s["group_mean"], 2)
            nc.scalar.activation(dts[:, 208:212], dts[:, 200:204], ACT.Sqrt).then_inc(s["group_root"], 1)
            turned_hi("latents", lat_t, 5, lambda b: col("q_g", b) if b < 3 else col("kv_g", b - 3))
            rope = area("rope")
            act.wait_ge(s["trig_arg"], 1)
            nc.scalar.activation(rope[:, 192:256], rope[:, 128:192], ACT.Sin).then_inc(s["trig_done"], 1)
            end(act)
            begin(act, 26)
            act.dma_start(area("mask"), consts[:, CAT["mask"][0]:CAT["mask"][1]]).then_inc(s["mask_loaded"], 16)
            by_tokens("q_up", 3, [512] * 3, q)
            by_tokens("kv_up", 2, [512] * 4, kv)
            end(act)
            begin(act, 27)
            end(act)
            begin(act, 28)
            turned_out("mla_q", q_t, MH, rows_=MQ)
            end(act)
            begin(act, 29)
            turned_out("mla_k", k_t, MH, rows_=MQ)
            end(act)
            begin(act, 30)
            for u in range(2 * MH):
                h, t = u // 2, u % 2
                w = (t + 1) * P
                act.wait_ge(s["mla_shift"], u + 1)
                if u >= 2:
                    act.wait_ge(s["mla_turned"], u - 1)
                nc.scalar.activation(e_m[:, u % 2, 0:w], s_m[:, u % 2, 0:w], ACT.Exp, bias=sm[:, u % 2, 0:1],
                                     accum_out=sm[:, u % 2, 1:2]).then_inc(s["mla_exp"], 1)
                act.wait_ge(s["mla_turned"], u + 1)
                if u >= 2:
                    act.wait_ge(s["mla_out"], u - 1)
                nc.scalar.copy(et_m[:, u % 2, 0:t + 1, :], bank[:, 2 + u % 2, 0:w].rearrange("p (k q) -> p k q", q=P))\
                    .then_inc(s["mla_t_copied"], 1)
            end(act)
            begin(act, 31)
            act.dma_start(mem[:, :, :], mem_in).then_inc(s["mem_loaded"], 16)
            act.dma_start(area("final_g"), rows_in[:, ROW["final2_g"][0]:ROW["final2_g"][1]]).then_inc(s["gain_loaded"], 16)
            turned_hi("mla_out", m_t, KD)
            end(act)
            begin(act, 32)
            hi_parts(SLOT["w_out_2"] + 16 + NS - 1)
            end(act)
            begin(act, 33)
            act.wait_ge(s["mem_loaded"], 16)
            norm(NORMS["mem"], mem)
            turned_hi("norm_mem", mem_t, KD, lambda b: col("mem_g", b))
            end(act)
            begin(act, 34)
            norm(NORMS["memx"], xres)
            turned_hi("norm_memx", h_t, KD, lambda b: col("memx_g", b))
            end(act)
            begin(act, 35)
            by_channels("mem_k", 8, mk_t)
            end(act)
            begin(act, 36)
            by_tokens("mem_v", KD, [512, 512], mv)
            end(act)
            begin(act, 37)
            by_channels("mem_q", 8, mq_t)
            end(act)
            begin(act, 38)
            for u in range(8):
                h, t = u // 2, u % 2
                act.wait_ge(s["mem_shift"], u + 1)
                if u >= 2:
                    act.wait_ge(s["mem_turned"], u - 1)
                nc.scalar.activation(e_x[:, u % 2, :], bank[:, u % 2, 0:T], ACT.Exp, bias=sm[:, u % 2, 0:1],
                                     scale=0.0625, accum_out=sm[:, u % 2, 1:2]).then_inc(s["mem_exp"], 1)
                act.wait_ge(s["mem_turned"], u + 1)
                if h >= 2:
                    act.wait_ge(s["mem_out"], h - 1)
                nc.scalar.copy(et_x[:, h % 2, :, t * P:(t + 1) * P],
                               bank[:, 2 + u % 2, 0:T].rearrange("p (k q) -> p k q", q=P)).then_inc(s["mem_t_copied"], 1)
                if t == 1:
                    act.wait_ge(s["mem_out"], h + 1)
                    nc.scalar.copy(h_t[0][:, 2 * h:2 * h + 2, :], bank[:, 4 + h % 2, :].rearrange("p (e t) -> p e t", e=2))\
                        .then_inc(s["mem_hi_made"], 1)
            end(act)
            begin(act, 39)
            hi_parts(SLOT["mem_o"] + KD + NS - 1)
            end(act)
            begin(act, 40)
            norm(NORMS["ffn2"], xres)
            turned_hi("norm_ffn", h_t, KD, lambda b: col("ffn2_g", b))
            end(act)
            begin(act, 41)
            F = SLOT["ffn"]
            gate_f = area("gate_f", "p (b t) -> p b t", t=T)

            def ffn_silu(done, u):
                act.wait_ge(s["ffn_conv_g"], done)
                nc.scalar.activation(gate_f[:, u, :], gate_f[:, u, :], ACT.Silu).then_inc(s["ffn_silu"], 1)

            hi_parts(F + 3)
            ffn_silu(1, 0)
            hi_parts(F + 5)
            ffn_silu(2, 1)
            with act.Fori(1, FF // 2) as r:
                for u in range(2):
                    for i in range(3):
                        n = F + 3 * u - 1 + i
                        hi_part(r * 6 + n, n % NS, r * (16 * 6 // NR) + 16 * (n // NR + 1))
                    ffn_silu(r * 2 + (u + 1), u)
            made[0] = F + 3 * FF - 1
            hi_parts(F + 3 * FF)
            end(act)
            begin(act, 42)
            act.wait_ge(s["residual_ready"], 2)
            norm(NORMS["final2"], xres)
            act.wait_ge(s["norm_scaled"], 2 * NORMS["final2"] + 2 + 2)
            act.dma_start(out, out_sb[:, :, :]).then_inc(s["out_stored"], 16)
            act.wait_ge(s["out_stored"], 16)

        @block.vector
        def _(dve):
            v = nc.vector
            done = [0]

            def link(ins):
                done[0] += 1
                ins.then_inc(s["dve_done"], 1)
                dve.wait_ge(s["dve_done"], done[0])

            def signal(name):
                dve.drain().then_inc(s[name], 1)

            def turned_out(name, dst, blocks, gain=None, rows_=P):
                first, act0, dve0, n = TURN[name]
                for k in range(1, n, 2):
                    dve.wait_ge(s["turned"], first + k + 1)
                    width = min(2, blocks - 2 * k)
                    if gain is None:
                        ins = v.tensor_copy(dst[0:rows_, 2 * k:2 * k + width, :],
                                            bank[0:rows_, k % 8, 0:width * T].rearrange("p (b t) -> p b t", t=T))
                    else:
                        for i in range(width):
                            ins = v.tensor_scalar(dst[:, 2 * k + i, :], bank[:, k % 8, i * T:(i + 1) * T],
                                                  gain(2 * k + i), None, ALU.mult)
                    ins.then_inc(s["turned_out_dve"], 1)

            def turned_lo(name, dst, blocks, gain=None):
                for b in range(blocks):
                    at = bank[:, b // 2, (b % 2) * T:(b % 2 + 1) * T]
                    hi = dst[0][:, b, :].bitcast(F32)
                    dve.wait_ge(s["split_act"], SPLIT[name] + min(b - b % 2 + 2, blocks))
                    if gain is None:
                        v.tensor_tensor(dst[1][:, b, :], at, hi, ALU.subtract)
                    else:
                        v.scalar_tensor_tensor(out=dst[1][:, b, :], in0=at, scalar=gain(b), in1=hi,
                                               op0=ALU.mult, op1=ALU.subtract)

            def norm(which, src):
                dve.wait_ge(s["norm_summed"], 2 * which + 2)
                v.tensor_scalar(ssq[:, 2:4], ssq[:, 0:2], 1.0 / D, EPS, ALU.mult, ALU.add).then_inc(s["norm_mean"], 1)
                dve.wait_ge(s["norm_rooted"], which + 1)
                v.reciprocal(rstd[:, 2:4], rstd[:, 0:2]).then_inc(s["norm_factor"], 1)
                dve.wait_ge(s["norm_factor"], which + 1)
                v.tensor_scalar(x_scaled[:, 1, :], src[:, 1, :], rstd[:, 3:4], None, ALU.mult).then_inc(s["norm_scaled"], 1)

            def by_tokens(name, depth, widths, dst):
                for c, w in enumerate(widths):
                    p = (c + 1) * depth
                    dve.wait_ge(s["spent"], SLOT[name] + (p + 1) // 2)
                    v.tensor_copy(dst[:, 1, c * 512:c * 512 + w], bank[:, 2 * (c % 2) + 1, 0:w]).then_inc(s["copied_dve"], 1)

            def by_channels(name, blocks, dst):
                for j in range(1, blocks, 2):
                    dve.wait_ge(s["spent"], SLOT[name] + j + 1)
                    v.tensor_copy(dst[:, j, :], bank[:, j % 4, 0:T]).then_inc(s["copied_dve"], 1)

            def into_residual(spent):
                dve.wait_ge(s["spent"], spent)
                for t in range(TT):
                    for h in range(2):
                        link(v.tensor_tensor(xres[:, t, h * 512:(h + 1) * 512], xres[:, t, h * 512:(h + 1) * 512],
                                             bank[:, 2 * t + h, :], ALU.add))

            def rotate(x1, x2, cos, sin, tmp):
                v.tensor_tensor(tmp(0), x1, cos, ALU.mult)
                v.tensor_tensor(tmp(1), x2, sin, ALU.mult)
                v.tensor_tensor(tmp(2), x2, cos, ALU.mult)
                link(v.tensor_tensor(tmp(3), x1, sin, ALU.mult))
                v.tensor_tensor(x1, tmp(0), tmp(1), ALU.subtract)
                link(v.tensor_tensor(x2, tmp(2), tmp(3), ALU.add))

            dve.wait_ge(s["x_loaded"], 16)
            norm(NORMS["attn"], xres)
            dve.wait_ge(s["params_loaded"], 80)
            turned_lo("attn_norm", h_t, KD, lambda b: col("attn_g", b))
            end(dve)
            begin(dve, 1)
            by_tokens("w_in", KD, [512] * 6, proj)
            end(dve)
            begin(dve, 2)
            lp = row("lam").rearrange("p (a b d) -> p a b d", a=2, b=2)
            lt = area("rot")[:, 0:128].rearrange("p (a d) -> p a d", a=2)
            link(v.tensor_tensor(lt, lp[:, :, 0, :], lp[:, :, 1, :], ALU.mult))
            v.tensor_reduce(lam[:, 0:2], lt, AX, ALU.add).then_inc(s["lambda_products"], 1)
            dve.wait_ge(s["lambda_exp"], 2)
            link(v.tensor_tensor(lam[:, 4:5], lam[:, 3:4], lam[:, 2:3], ALU.subtract))
            link(v.tensor_scalar(lam[:, 5:6], lam[:, 4:5], -LAMBDA_INIT, None, ALU.add))
            later, earlier = const("later"), const("earlier")
            for h in range(HD):
                dh = decay[:, h, :, :].rearrange("p j i -> p (j i)")
                link(v.tensor_scalar(dh, earlier, log_g[:, 4 + h:5 + h], -1.0, ALU.mult, ALU.mult))
                link(v.tensor_scalar(area("p_ret")[:, 0:512], later, log_g[:, h:h + 1], -1.0, ALU.mult, ALU.mult))
                v.tensor_tensor(dh, dh, area("p_ret")[:, 0:512], ALU.add).then_inc(s["decay_arg"], 1)
                dve.wait_ge(s["decay_arg"], h + 1)
            rot = area("rot")
            for t in range(TT):
                dqk = proj[:, t, 0:1024].rearrange("p (g d) -> p g d", d=64)
                cd = const("cos_d")[:, t * 8:(t + 1) * 8].unsqueeze(1).broadcast_to([P, 16, 8])
                sd = const("sin_d")[:, t * 8:(t + 1) * 8].unsqueeze(1).broadcast_to([P, 16, 8])
                rotate(dqk[:, :, 0:8], dqk[:, :, 8:16], cd, sd,
                       lambda i: rot[:, i * 128:(i + 1) * 128].rearrange("p (g d) -> p g d", d=8))
                rqk = proj[:, t, 1536:2048].rearrange("p (g d) -> p g d", d=64)
                cr = const("cos_r")[:, t * 32:(t + 1) * 32].unsqueeze(1).broadcast_to([P, 8, 32])
                sr = const("sin_r")[:, t * 32:(t + 1) * 32].unsqueeze(1).broadcast_to([P, 8, 32])
                rotate(rqk[:, :, 0:32], rqk[:, :, 32:64], cr, sr,
                       lambda i: rot[:, 1024 + i * 256:1024 + (i + 1) * 256].rearrange("p (g d) -> p g d", d=32))
            end(dve)
            begin(dve, 3)
            turned_out("qk", qk_t, 12)
            end(dve)
            begin(dve, 4)

            def diff_shift(u):
                dve.wait_ge(s["diff_scores"], u + 1)
                if u >= 2:
                    dve.wait_ge(s["diff_exp"], u - 1)
                link(v.tensor_reduce(sm[:, u % 2, 4:6], bank[:, 2 * (u % 2):2 * (u % 2) + 2, 0:T], AX, ALU.max))
                v.tensor_scalar(sm[:, u % 2, 0:2], sm[:, u % 2, 4:6], -0.125, None, ALU.mult).then_inc(s["diff_shift"], 1)

            diff_shift(0)
            for u in range(8):
                h, t = u // 2, u % 2
                if u + 1 < 8:
                    diff_shift(u + 1)
                dve.wait_ge(s["diff_exp"], u + 1)
                if u >= 2:
                    dve.wait_ge(s["diff_turned"], u - 1)
                link(v.reciprocal(sm[:, u % 2, 6:8], sm[:, u % 2, 2:4]))
                link(v.tensor_scalar(sm[:, u % 2, 8:9], sm[:, u % 2, 7:8], lam[:, 5:6], None, ALU.mult))
                link(v.tensor_scalar(e_diff[:, u % 2, 1, :], e_diff[:, u % 2, 1, :], sm[:, u % 2, 8:9], None, ALU.mult))
                v.scalar_tensor_tensor(out=a_diff[:, u % 2, :], in0=e_diff[:, u % 2, 0, :], scalar=sm[:, u % 2, 6:7],
                                       in1=e_diff[:, u % 2, 1, :], op0=ALU.mult, op1=ALU.add).then_inc(s["diff_mixed"], 1)
                dve.wait_ge(s["diff_out"], u + 1)
                v.tensor_copy(o_diff[:, t, h * P:(h + 1) * P], bank[:, 6 + u % 2, 0:P]).then_inc(s["diff_out_copied"], 1)
            end(dve)
            begin(dve, 5)
            for h in range(HD):
                dve.wait_ge(s["ret_scores"], h + 1)
                v.scalar_tensor_tensor(out=p_ret[:, h, :, :].rearrange("p j i -> p (j i)"), in0=bank[:, h % 2, :],
                                       scalar=0.125, in1=decay[:, h, :, :].rearrange("p j i -> p (j i)"),
                                       op0=ALU.mult, op1=ALU.mult).then_inc(s["ret_decayed"], 1)
            dve.wait_ge(s["ret_out"], HD)
            for t in range(TT):
                v.tensor_copy(o_ret[:, t, :], bank[:, 2 + t, :])
            end(dve)
            begin(dve, 6)
            stat = area("stat")
            by_head = lambda a: a.rearrange("p t (h c) -> p (t h) c", c=P)
            sq = area("rot", "p (g c) -> p g c", c=P)[:, 0:8, :]
            od, orr = by_head(o_diff), by_head(o_ret)
            link(v.tensor_tensor(sq, od, od, ALU.mult))
            link(v.tensor_reduce(stat[:, 0:8], sq, AX, ALU.add))
            v.tensor_scalar(stat[:, 8:16], stat[:, 0:8], 1.0 / P, EPS, ALU.mult, ALU.add).then_inc(s["head_mean"], 1)
            link(v.tensor_reduce(stat[:, 64:72], orr, AX, ALU.add))
            link(v.tensor_scalar(stat[:, 72:80], stat[:, 64:72], 1.0 / P, None, ALU.mult))
            link(v.tensor_tensor(orr, orr, stat[:, 72:80].unsqueeze(2).broadcast_to([P, 8, P]), ALU.subtract))
            link(v.tensor_tensor(sq, orr, orr, ALU.mult))
            link(v.tensor_reduce(stat[:, 32:40], sq, AX, ALU.add))
            v.tensor_scalar(stat[:, 40:48], stat[:, 32:40], 1.0 / P, EPS, ALU.mult, ALU.add).then_inc(s["head_mean"], 1)
            dve.wait_ge(s["head_root"], 1)
            link(v.reciprocal(stat[:, 24:32], stat[:, 16:24]))
            link(v.tensor_scalar(stat[:, 24:32], stat[:, 24:32], 1.0 - LAMBDA_INIT, None, ALU.mult))
            link(v.tensor_tensor(od, od, stat[:, 24:32].unsqueeze(2).broadcast_to([P, 8, P]), ALU.mult))
            for t in range(TT):
                v.tensor_tensor(mix[:, t, 0:512].rearrange("p (h c) -> p h c", c=P), od[:, 4 * t:4 * t + 4, :],
                                row("diff_g").unsqueeze(1).broadcast_to([P, HD, P]), ALU.mult)
            dve.wait_ge(s["head_root"], 2)
            link(v.reciprocal(stat[:, 56:64], stat[:, 48:56]))
            link(v.tensor_tensor(orr, orr, stat[:, 56:64].unsqueeze(2).broadcast_to([P, 8, P]), ALU.mult))
            for t in range(TT):
                link(v.tensor_tensor(o_ret[:, t, :], o_ret[:, t, :], row("ret_g"), ALU.mult))
                v.tensor_tensor(mix[:, t, 512:1024], o_ret[:, t, :], gate_r[:, t, :], ALU.mult)
            end(dve)
            begin(dve, 7)
            turned_lo("mix", h_t, KD)
            end(dve)
            begin(dve, 8)
            into_residual(SLOT["w_out"] + 8)
            end(dve)
            begin(dve, 9)
            norm(NORMS["ffn"], xres)
            turned_lo("ffn_norm", h_t, KD, lambda b: col("ffn_g", b))
            end(dve)
            begin(dve, 10)
            for j in range(16):
                dve.wait_ge(s["split_act"], SPLIT["w_query"] + j + 1)
                v.tensor_tensor(pq_t[1][:, j, :], bank[:, j % 4, 0:T], pq_t[0][:, j, :].bitcast(F32), ALU.subtract)\
                    .then_inc(s["split_dve"], 1)
            end(dve)
            begin(dve, 11)
            for b in range(4):
                dve.wait_ge(s["spent"], SLOT["sub_keys"] + b // 2 + 1)
                v.tensor_copy(keys[:, 1, b, :], bank[:, 2 * b + 1, :])
            end(dve)
            begin(dve, 12)
            vals = area("vals", "p (g c) -> p g c", c=TOPK)
            idx = area("idx", "p (g c) -> p g c", c=TOPK).bitcast(U32)
            spare = area("spare")
            sets = keys.rearrange("p t b (i c) -> p (t b i) c", c=NK)

            def top16(values, top, index, rest):
                link(v.max(top[:, 0:8], values))
                v.max_index(index[:, 0:8], top[:, 0:8], values)
                link(v.match_replace(rest, top[:, 0:8], values, -3.0e38))
                link(v.max(top[:, 8:16], rest))
                v.max_index(index[:, 8:16], top[:, 8:16], rest)

            for g in range(2 * 2 * PH):
                top16(sets[:, g, :], vals[:, g, :], idx[:, g, :], spare[:, (g % 2) * NK:(g % 2 + 1) * NK])
            cand = area("cand", "p (g i j) -> p g i j", i=TOPK, j=TOPK)
            pairs = vals.rearrange("p (g s) c -> p g s c", s=2)
            best = area("best", "p (g c) -> p g c", c=TOPK)
            pos = area("pos", "p (g c) -> p g c", c=TOPK).bitcast(U32)
            dve.wait_ge(s["dve_done"], done[0])
            for g in range(2 * PH):
                link(v.tensor_tensor(cand[:, g, :, :], pairs[:, g, 0, :].unsqueeze(2).broadcast_to([P, TOPK, TOPK]),
                                     pairs[:, g, 1, :].unsqueeze(1).broadcast_to([P, TOPK, TOPK]), ALU.add))
                top16(cand[:, g, :, :].rearrange("p i j -> p (i j)"), best[:, g, :], pos[:, g, :],
                      spare[:, (g % 2) * 256:(g % 2 + 1) * 256])
            link(v.tensor_copy(area("idxf"), area("idx").bitcast(U32)))
            hi_i, lo_i = area("hi").bitcast(U32), area("lo").bitcast(U32)
            posv = area("pos").bitcast(U32)
            link(v.tensor_scalar(hi_i, posv, 4, None, ALU.logical_shift_right))
            link(v.tensor_scalar(lo_i, posv, 15, None, ALU.bitwise_and))
            link(v.tensor_copy(area("hi"), hi_i))
            link(v.tensor_copy(area("lo"), lo_i))
            chosen = area("chosen", "p (f c) -> p f c", f=6)
            eq = area("eq", "p (k a) -> p k a", a=TOPK)
            idxf = area("idxf", "p (t h s a) -> p t h s a", t=TT, s=2, a=TOPK)
            iota16 = const("iota")[:, 0:TOPK].unsqueeze(1).broadcast_to([P, P, TOPK])
            for t in range(TT):
                for f, ch in enumerate(("hi", "lo")):
                    pick = area(ch)[:, t * P:(t + 1) * P].unsqueeze(2).broadcast_to([P, P, TOPK])
                    link(v.tensor_tensor(eq, pick, iota16, ALU.is_equal))
                    e4 = eq.rearrange("p (h k) a -> p h k a", h=PH)
                    link(v.tensor_tensor(e4, e4, idxf[:, t, :, f, :].unsqueeze(2).broadcast_to([P, PH, TOPK, TOPK]), ALU.mult))
                    link(v.tensor_reduce(chosen[:, 2 * f + t, :], eq, AX, ALU.add))
            gst = area("gst")
            for t in range(TT):
                bt = best[:, 8 * t:8 * t + 8, :]
                link(v.tensor_copy(gst[:, t * 8:t * 8 + 8], bt[:, :, 0:1].rearrange("p h o -> p (h o)")))
                v.tensor_tensor(bt, bt, gst[:, t * 8:t * 8 + 8].unsqueeze(2).broadcast_to([P, PH, TOPK]), ALU.subtract)\
                    .then_inc(s["gate_shifted"], 1)
            for t in range(TT):
                bt = best[:, 8 * t:8 * t + 8, :]
                dve.wait_ge(s["gate_exp"], t + 1)
                link(v.tensor_reduce(gst[:, 16 + t * 8:24 + t * 8], bt, AX, ALU.add))
                link(v.reciprocal(gst[:, 32 + t * 8:40 + t * 8], gst[:, 16 + t * 8:24 + t * 8]))
                link(v.tensor_tensor(chosen[:, 4 + t, :].rearrange("p (h k) -> p h k", h=PH), bt,
                                     gst[:, 32 + t * 8:40 + t * 8].unsqueeze(2).broadcast_to([P, PH, TOPK]), ALU.mult))
            signal("choice_made")
            turned_out("chosen", chosen_t, 3)
            end(dve)
            begin(dve, 13)
            end(dve)
            begin(dve, 14)
            iota4 = const("iota").unsqueeze(1).broadcast_to([P, 4, NK])
            one_hots = lambda b: work[:, b * 512:(b + 1) * 512].rearrange("p (t k) -> p t k", t=4)

            def compared(g, u):
                keys4 = lambda f: chosen_t[:, f, bass.ds(g * 4, 4)].unsqueeze(2).broadcast_to([P, 4, NK])
                v.tensor_tensor(one_hots(u), iota4, keys4(0), ALU.is_equal).then_inc(s["one_hot_1"], 1)
                v.tensor_tensor(one_hots(2 + u), iota4, keys4(1), ALU.is_equal).then_inc(s["one_hot_2"], 1)

            compared(0, 0)
            compared(1, 1)
            with dve.Fori(1, T // 8) as r:
                for u in range(2):
                    dve.wait_ge(s["spread"], r * 2 + (u - 1))
                    compared(r * 2 + u, u)
            end(dve)
            begin(dve, 15)
            X = SLOT["experts"]
            U3 = 3

            def weigh(k, u, before, spent=None):
                dve.wait_ge(s["gelu_done"], k + 1)
                g = gates[:, bass.ds(k, 1), :].rearrange("p a t -> p (a t)")
                a = work[:, u * T:(u + 1) * T]
                v.tensor_tensor(a, a, g, ALU.mult).then_inc(s["act_product"], 1)
                dve.wait_ge(s["act_product"], before + 1)
                if spent is not None:
                    dve.wait_ge(s["spent"], spent)
                v.tensor_copy(act_t[0][:, u, :], a).then_inc(s["act_hi_made"], 1)
                dve.wait_ge(s["act_hi_made"], before + 1)
                v.tensor_tensor(act_t[1][:, u, :], a, act_t[0][:, u, :].bitcast(F32), ALU.subtract).then_inc(s["weighed"], 1)

            for k in range(3):
                weigh(k, k, k)
            with dve.Fori(1, NK // U3) as r:
                for u in range(U3):
                    weigh(r * U3 + u, u, r * U3 + u, r * (2 * U3) + (X + 2 * u - 3))
            for k in range(NK // U3 * U3, NK):
                weigh(k, k % U3, k, X + 2 * k - 3)
            end(dve)
            begin(dve, 16)
            into_residual(X + 2 * NK)
            signal("residual_ready")
            norm(NORMS["final1"], xres)
            dve.wait_ge(s["norm_scaled"], 2 * NORMS["final1"] + 2)
            dve.wait_ge(s["gain_loaded"], 16)
            for t in range(TT):
                v.tensor_tensor(xres[:, t, :], x_scaled[:, t, :], area("final_g"), ALU.mult)
            end(dve)
            begin(dve, 17)
            norm(NORMS["mix"], xres)
            turned_lo("norm_mix", h_t, KD, lambda b: col("mix_g", b))
            end(dve)
            begin(dve, 18)
            by_tokens("z", KD, [512, 512], z)
            by_tokens("dt_q", KD, [DTQ], lat)
            end(dve)
            begin(dve, 19)
            dve.wait_ge(s["spent"], SLOT["kv_rope"] + 4)
            v.tensor_copy(lat[:, 1, 512:512 + KVR], bank[:, 1, 0:KVR]).then_inc(s["copied_dve"], 1)
            end(dve)
            begin(dve, 20)
            for j in range(16):
                dve.wait_ge(s["spent"], SLOT["xbc"] + j + 1)
                b = bank[:, j % 4, :]
                v.tensor_scalar(xc[:, j, :], b[:, 0:T], col("xw", 4 * j + 3), col("xb", j), ALU.mult, ALU.add)\
                    .then_inc(s["conv_done"], 1)
                for d in range(1, 4):
                    dve.wait_ge(s["conv_done"], 4 * j + d)
                    v.scalar_tensor_tensor(out=xc[:, j, d:T], in0=b[:, 0:T - d], scalar=col("xw", 4 * j + 3 - d),
                                           in1=xc[:, j, d:T], op0=ALU.mult, op1=ALU.add).then_inc(s["conv_done"], 1)
            end(dve)
            begin(dve, 21)
            dts = area("dts")
            t2 = lambda a: dts[:, a:a + 32].rearrange("p (t h) -> p t h", t=TT)
            wide = lambda r_: row(r_).unsqueeze(1).broadcast_to([P, TT, 16])
            link(v.tensor_tensor(t2(32), lat[:, :, 0:16], wide("dt_bias"), ALU.add))
            link(v.scalar_tensor_tensor(out=dts[:, 64:96], in0=dts[:, 32:64], scalar=-1.0, in1=dts[:, 32:64],
                                        op0=ALU.mult, op1=ALU.max))
            signal("dt_arg")
            dve.wait_ge(s["dt_l"], 2)
            link(v.scalar_tensor_tensor(out=dts[:, 32:64], in0=dts[:, 32:64], scalar=0.0, in1=dts[:, 128:160],
                                        op0=ALU.max, op1=ALU.add))
            link(v.tensor_scalar(dts[:, 160:176], dts[:, 160:176], -1.0, None, ALU.mult))
            v.tensor_tensor(t2(0), t2(32), dts[:, 160:176].unsqueeze(1).broadcast_to([P, TT, 16]), ALU.mult)\
                .then_inc(s["dt_scaled"], 1)
            for k in range(1, 4, 2):
                dve.wait_ge(s["turned"], TURN["xs"][0] + k + 1)
                t, b = k // 2, k % 2
                v.tensor_copy(xs[:, t, b * 512:(b + 1) * 512], bank[:, k, :]).then_inc(s["turned_out_dve"], 1)
            dve.wait_ge(s["turned_out_act"], TURN["xs"][1] + 2)
            dve.wait_ge(s["turned_out_dve"], TURN["xs"][2] + 2)
            for t in range(TT):
                v.tensor_tensor(xdt[:, t, :].rearrange("p (h c) -> p h c", c=64),
                                xs[:, t, :].rearrange("p (h c) -> p h c", c=64),
                                t2(32)[:, t, :].unsqueeze(2).broadcast_to([P, SH, 64]), ALU.mult)
            dve.wait_ge(s["tri_loaded"], 16)
            for g in range(SG):
                dve.wait_ge(s["cb_done"], g + 1)
                v.tensor_tensor(cb[:, g, :, :].rearrange("p j l -> p (j l)"), bank[:, 4 + g % 2, :], const("tri"), ALU.mult)\
                    .then_inc(s["cb_masked"], 1)
            dve.wait_ge(s["cum_done"], 1)
            v.tensor_copy(dts[:, 64:96], bank[:, 6, 0:32])
            end(dve)
            begin(dve, 22)

            def clip(h):
                dve.wait_ge(s["seg_sum"], h + 1)
                if h >= 2:
                    dve.wait_ge(s["ssd_out"], h - 1)
                for st in range(TT):
                    v.tensor_scalar(seg[:, h % 2, 2 * P * st:2 * P * st + (2 - st) * P], bank[:, h % 2, st * P:T],
                                    dts[:, 64 + st * 16 + h:65 + st * 16 + h], 0.0, ALU.subtract, ALU.min)\
                        .then_inc(s["seg_clipped"], 1)

            clip(0)
            for h in range(SH):
                if h + 1 < SH:
                    clip(h + 1)
                dve.wait_ge(s["seg_exp"], h + 1)
                g = h // 4
                for st in range(TT):
                    sl = seg[:, h % 2, 2 * P * st:2 * P * st + (2 - st) * P]
                    v.tensor_tensor(sl, sl, cb[:, g, st, st * P:T], ALU.mult).then_inc(s["seg_weighed"], 1)
            end(dve)
            begin(dve, 23)
            for t in range(TT):
                link(v.tensor_tensor(xs[:, t, :].rearrange("p (h c) -> p h c", c=64),
                                     xs[:, t, :].rearrange("p (h c) -> p h c", c=64),
                                     row("d_skip").unsqueeze(2).broadcast_to([P, SH, 64]), ALU.mult))
                link(v.tensor_tensor(y[:, t, 0:512], xs[:, t, 0:512], bank[:, 4 + 2 * t, :], ALU.add))
                link(v.tensor_tensor(y[:, t, 512:1024], xs[:, t, 512:1024], bank[:, 5 + 2 * t, :], ALU.add))
                link(v.tensor_tensor(y[:, t, :], y[:, t, :], z[:, t, :], ALU.mult))
                link(v.tensor_tensor(xs[:, t, :], y[:, t, :], y[:, t, :], ALU.mult))
                link(v.tensor_reduce(dts[:, 192 + 4 * t:196 + 4 * t], xs[:, t, :].rearrange("p (g c) -> p g c", c=256), AX, ALU.add))
            v.tensor_scalar(dts[:, 200:208], dts[:, 192:200], 1.0 / 256, EPS, ALU.mult, ALU.add).then_inc(s["group_mean"], 1)
            dve.wait_ge(s["group_root"], 1)
            link(v.reciprocal(dts[:, 192:200], dts[:, 208:216]))
            for t in range(TT):
                yg = y[:, t, :].rearrange("p (g c) -> p g c", c=256)
                v.tensor_tensor(yg, yg, dts[:, 192 + 4 * t:196 + 4 * t].unsqueeze(2).broadcast_to([P, SG, 256]), ALU.mult)
            end(dve)
            begin(dve, 24)
            turned_lo("ssd", h_t, KD, lambda b: col("ssd_g", b))
            end(dve)
            begin(dve, 25)
            ql, kl = lat[:, :, 16:400], lat[:, :, 512:768]
            sq1 = area("squares")[:, 0:768].rearrange("p (t c) -> p t c", t=TT)
            sq2 = area("x_scaled")[:, 0:512].rearrange("p (t c) -> p t c", t=TT)
            v.tensor_tensor(sq1, ql, ql, ALU.mult)
            link(v.tensor_tensor(sq2, kl, kl, ALU.mult))
            v.tensor_reduce(dts[:, 192:194], sq1, AX, ALU.add)
            link(v.tensor_reduce(dts[:, 194:196], sq2, AX, ALU.add))
            link(v.tensor_scalar(dts[:, 200:202], dts[:, 192:194], 1.0 / 384, EPS, ALU.mult, ALU.add))
            v.tensor_scalar(dts[:, 202:204], dts[:, 194:196], 1.0 / 256, EPS, ALU.mult, ALU.add).then_inc(s["group_mean"], 1)
            dve.wait_ge(s["group_root"], 2)
            link(v.reciprocal(dts[:, 192:196], dts[:, 208:212]))
            for t in range(TT):
                link(v.tensor_scalar(ql[:, t, :], ql[:, t, :], dts[:, 192 + t:193 + t], None, ALU.mult))
                link(v.tensor_scalar(kl[:, t, :], kl[:, t, :], dts[:, 194 + t:195 + t], None, ALU.mult))
            signal("latents_scaled")
            rope = area("rope")
            link(v.tensor_copy(rope[:, 0:2], pos_i[:, :]))
            for t in range(TT):
                link(v.tensor_scalar(rope[:, 32 + t * 16:48 + t * 16], const("inv_m"), rope[:, t:t + 1], None, ALU.mult))
            ang = rope[:, 32:64]
            BIG = 12582912.0
            for i, shift in enumerate((0.0, 0.25)):
                turns = rope[:, 64 + 32 * i:96 + 32 * i]
                r_ = rope[:, 128 + 32 * i:160 + 32 * i]
                link(v.tensor_scalar(turns, ang, 0.15915494309189535, shift, ALU.mult, ALU.add))
                link(v.tensor_scalar(turns, turns, BIG, None, ALU.add))
                link(v.tensor_scalar(turns, turns, BIG, None, ALU.subtract))
                link(v.scalar_tensor_tensor(out=r_, in0=turns, scalar=-6.28125, in1=ang, op0=ALU.mult, op1=ALU.add))
                link(v.scalar_tensor_tensor(out=r_, in0=turns, scalar=-0.0019340515136718750, in1=r_, op0=ALU.mult, op1=ALU.add))
                link(v.scalar_tensor_tensor(out=r_, in0=turns, scalar=-1.2556659146e-06, in1=r_, op0=ALU.mult, op1=ALU.add))
                if i:
                    link(v.tensor_scalar(r_, r_, 1.5707963267948966, None, ALU.add))
                link(v.tensor_scalar(r_, r_, 3.1415925, -3.1415925, ALU.min, ALU.max))
            signal("trig_arg")
            turned_lo("latents", lat_t, 5, lambda b: col("q_g", b) if b < 3 else col("kv_g", b - 3))
            end(dve)
            begin(dve, 26)
            by_tokens("q_up", 3, [512] * 3, q)
            by_tokens("kv_up", 2, [512] * 4, kv)
            end(dve)
            begin(dve, 27)
            xsc = area("x_scaled")
            for t in range(TT):
                sin = rope[:, 192 + t * 16:208 + t * 16]
                cos = rope[:, 224 + t * 16:240 + t * 16]
                qh = q[:, t, :].rearrange("p (h c) -> p h c", c=MQ)
                w16 = lambda a: a.unsqueeze(1).broadcast_to([P, MH, 16])
                rotate(qh[:, :, 64:80], qh[:, :, 80:96], w16(cos), w16(sin),
                       lambda i: xsc[:, i * 256:(i + 1) * 256].rearrange("p (h c) -> p h c", c=16))
                rotate(lat[:, t, 768:784], lat[:, t, 784:800], cos, sin, lambda i: xsc[:, 1024 + i * 16:1040 + i * 16])
                kc = kcat[:, t, :].rearrange("p (h c) -> p h c", c=MQ)
                v.tensor_copy(kc[:, :, 0:64], kv[:, t, :].rearrange("p (h c) -> p h c", c=128)[:, :, 0:64])
                v.tensor_copy(kc[:, :, 64:96], lat[:, t, 768:800].unsqueeze(1).broadcast_to([P, MH, 32]))
            end(dve)
            begin(dve, 28)
            turned_out("mla_q", q_t, MH, rows_=MQ)
            end(dve)
            begin(dve, 29)
            turned_out("mla_k", k_t, MH, rows_=MQ)
            end(dve)
            begin(dve, 30)
            dve.wait_ge(s["mask_loaded"], 16)
            mask = const("mask").rearrange("p (t k) -> p t k", t=TT)

            def mla_shift(u):
                t = u % 2
                w = (t + 1) * P
                dve.wait_ge(s["mla_scores"], u + 1)
                if u >= 2:
                    dve.wait_ge(s["mla_exp"], u - 1)
                link(v.scalar_tensor_tensor(out=s_m[:, u % 2, 0:w], in0=bank[:, u % 2, 0:w], scalar=float(MQ) ** -0.5,
                                            in1=mask[:, t, 0:w], op0=ALU.mult, op1=ALU.add))
                v.tensor_reduce(sm[:, u % 2, 0:1], s_m[:, u % 2, 0:w], AX, ALU.max, negate=True).then_inc(s["mla_shift"], 1)

            mla_shift(0)
            for u in range(2 * MH):
                h, t = u // 2, u % 2
                dve.wait_ge(s["mla_exp"], u + 1)
                link(v.reciprocal(sm[:, u % 2, 2:3], sm[:, u % 2, 1:2]))
                if u + 1 < 2 * MH:
                    mla_shift(u + 1)
                dve.wait_ge(s["mla_out"], u + 1)
                v.tensor_scalar(o_m[:, t, h * 64:(h + 1) * 64], bank[:, 4 + u % 2, 0:MV], sm[:, u % 2, 2:3], None, ALU.mult)\
                    .then_inc(s["mla_out_copied"], 1)
            end(dve)
            begin(dve, 31)
            turned_lo("mla_out", m_t, KD)
            end(dve)
            begin(dve, 32)
            into_residual(SLOT["w_out_2"] + 16)
            end(dve)
            begin(dve, 33)
            norm(NORMS["mem"], mem)
            turned_lo("norm_mem", mem_t, KD, lambda b: col("mem_g", b))
            end(dve)
            begin(dve, 34)
            norm(NORMS["memx"], xres)
            turned_lo("norm_memx", h_t, KD, lambda b: col("memx_g", b))
            end(dve)
            begin(dve, 35)
            by_channels("mem_k", 8, mk_t)
            end(dve)
            begin(dve, 36)
            by_tokens("mem_v", KD, [512, 512], mv)
            end(dve)
            begin(dve, 37)
            by_channels("mem_q", 8, mq_t)
            end(dve)
            begin(dve, 38)

            def mem_shift(u):
                dve.wait_ge(s["mem_scores"], u + 1)
                if u >= 2:
                    dve.wait_ge(s["mem_exp"], u - 1)
                link(v.tensor_reduce(sm[:, u % 2, 3:4], bank[:, u % 2, 0:T], AX, ALU.max))
                v.tensor_scalar(sm[:, u % 2, 0:1], sm[:, u % 2, 3:4], -0.0625, None, ALU.mult).then_inc(s["mem_shift"], 1)

            mem_shift(0)
            for u in range(8):
                h, t = u // 2, u % 2
                if u + 1 < 8:
                    mem_shift(u + 1)
                dve.wait_ge(s["mem_exp"], u + 1)
                link(v.reciprocal(sm[:, u % 2, 2:3], sm[:, u % 2, 1:2]))
                v.tensor_scalar(e_x[:, u % 2, :], e_x[:, u % 2, :], sm[:, u % 2, 2:3], None, ALU.mult).then_inc(s["mem_scaled"], 1)
                if t == 1:
                    dve.wait_ge(s["mem_hi_made"], h + 1)
                    v.tensor_tensor(h_t[1][:, 2 * h:2 * h + 2, :], bank[:, 4 + h % 2, :].rearrange("p (e t) -> p e t", e=2),
                                    h_t[0][:, 2 * h:2 * h + 2, :].bitcast(F32), ALU.subtract)\
                        .then_inc(s["mem_out_copied"], 1)
            end(dve)
            begin(dve, 39)
            into_residual(SLOT["mem_o"] + 8)
            end(dve)
            begin(dve, 40)
            norm(NORMS["ffn2"], xres)
            turned_lo("norm_ffn", h_t, KD, lambda b: col("ffn2_g", b))
            end(dve)
            begin(dve, 41)
            F = SLOT["ffn"]

            def ffn_filter(k, u, half, dst, name, count):
                b = bank[:, 4 + 2 * u + half, :]
                c0 = COL["fw"][0] + half * 66
                w = lambda d: cols[:, bass.ds(k * 3 + (c0 + 2 - d), 1)]
                v.tensor_scalar(dst, b[:, 0:T], w(0), cols[:, bass.ds(k + (COL["fb"][0] + half * 22), 1)], ALU.mult, ALU.add)\
                    .then_inc(s["filter_step"], 1)
                dve.wait_ge(s["filter_step"], count)
                v.scalar_tensor_tensor(out=dst[:, 1:T], in0=b[:, 0:T - 1], scalar=w(1), in1=dst[:, 1:T],
                                       op0=ALU.mult, op1=ALU.add).then_inc(s["filter_step"], 1)
                dve.wait_ge(s["filter_step"], count + 1)
                v.scalar_tensor_tensor(out=dst[:, 2:T], in0=b[:, 0:T - 2], scalar=w(2), in1=dst[:, 2:T],
                                       op0=ALU.mult, op1=ALU.add).then_inc(s[name], 1)

            def ffn_block(k, u, spent, r4, down_spent):
                dve.wait_ge(s["spent"], spent)
                ffn_filter(k, u, 0, gate_f[:, u, :], "ffn_conv_g", r4 + 1)
                dve.wait_ge(s["spent"], spent + 1)
                ffn_filter(k, u, 1, value_f[:, u, :], "ffn_conv_v", r4 + 3)
                dve.wait_ge(s["ffn_silu"], k + 1)
                dve.wait_ge(s["ffn_conv_v"], k + 1)
                v.tensor_tensor(gate_f[:, u, :], gate_f[:, u, :], value_f[:, u, :], ALU.mult).then_inc(s["act_product"], 1)
                dve.wait_ge(s["act_product"], k + (NK + 1))
                if down_spent is not None:
                    dve.wait_ge(s["spent"], down_spent)
                v.tensor_copy(act_t[0][:, u, :], gate_f[:, u, :]).then_inc(s["act_hi_made"], 1)
                dve.wait_ge(s["act_hi_made"], k + (NK + 1))
                v.tensor_tensor(act_t[1][:, u, :], gate_f[:, u, :], act_t[0][:, u, :].bitcast(F32), ALU.subtract)\
                    .then_inc(s["ffn_act"], 1)

            gate_f = area("gate_f", "p (b t) -> p b t", t=T)
            value_f = area("value_f", "p (b t) -> p b t", t=T)
            ffn_block(0, 0, F + 1, 0, None)
            ffn_block(1, 1, F + 3, 4, None)
            with dve.Fori(1, FF // 2) as r:
                for u in range(2):
                    k = r * 2 + u
                    ffn_block(k, u, r * 6 + (F + 3 * u), r * 8 + 4 * u, r * 6 + (F + 3 * u - 1))
            end(dve)
            begin(dve, 42)
            into_residual(F + 3 * FF)
            signal("residual_ready")
            norm(NORMS["final2"], xres)
            dve.wait_ge(s["norm_scaled"], 2 * NORMS["final2"] + 2)
            dve.wait_ge(s["gain_loaded"], 32)
            for t in range(TT):
                v.tensor_tensor(out_sb[:, t, :], x_scaled[:, t, :], area("final_g"), ALU.mult).then_inc(s["norm_scaled"], 1)


def lay_out(i):
    a = {k: np.asarray(v) for k, v in i.items()}
    z = lambda *shape: np.zeros(shape, np.float32)

    def panels(w):
        K, C = w.shape
        wide = -(-C // 512) * 512
        if wide > C:
            w = np.concatenate([w, z(K, wide - C)], axis=1)
        p = w.reshape(K // P, P, wide // 512, 512).transpose(2, 0, 1, 3).reshape(-1, P, 512)
        if len(p) % 2:
            p = np.concatenate([p, z(1, P, 512)])
        return p.reshape(-1, 2, P, 512).transpose(0, 2, 1, 3).reshape(-1, P, 1024)

    def channels(w):
        return w.reshape(KD, P, -1, P).transpose(2, 1, 0, 3).reshape(-1, P, 1024)

    def deep(w):
        return w.reshape(-1, P, D)

    def interleave(ahead, *parts):
        n = len(parts[-1])
        out = [p[0:1] for p in parts[:-1]]
        for k in range(n):
            if k + 1 < n:
                out += [p[k + 1:k + 2] for p in parts[:-1]]
            out.append(parts[-1][k:k + 1])
        return np.concatenate(out)

    w2 = a["w_in_2"][0]
    sub = a["peer_sub_keys"][0].transpose(3, 0, 1, 2).reshape(P, 2, 1024).transpose(1, 0, 2)
    ffn = channels(a["w_ffn_up_2"][0])
    order = [panels(a["w_in"][0]), deep(a["w_out"][0]), channels(a["peer_w_query"][0]), sub,
             interleave(1, a["peer_u"][0].reshape(NK, NK, KD, P).transpose(0, 3, 2, 1).reshape(NK, P, 1024),
                        a["peer_v"][0].reshape(NK, P, D)),
             panels(w2[:, 0:1024]), panels(w2[:, 3072:3072 + DTQ]), panels(w2[:, 3072 + DTQ:]),
             channels(w2[:, 1024:3072]), panels(a["mla_w_q_up_2"][0]), panels(a["mla_w_kv_up_2"][0]),
             deep(a["w_out_2"][0]), channels(a["w_mem_k_2"][0]), panels(a["w_mem_v_2"][0]),
             channels(a["w_mem_q_2"][0]), deep(a["w_mem_o_2"][0]),
             interleave(1, ffn[:FF], ffn[FF:], deep(a["w_ffn_down_2"][0]))]
    assert [len(o) for o in order] == [n for _, n in STAGES]
    by_part = lambda v: v.reshape(-1, P).T
    taps = lambda v: v.reshape(v.shape[0], -1, P).transpose(2, 1, 0).reshape(P, -1)
    cols = [by_part(a[n].reshape(-1)) for n in ("attn_norm_g", "ffn_norm_g", "norm_mix_w_2", "norm_mem_w_2", "norm_memx_w_2",
                                                "norm_ffn_w_2", "ssd_norm_w_2", "mla_q_norm_w_2", "mla_kv_norm_w_2")]
    cols += [taps(a["ssd_conv_w_2"][0]), by_part(a["ssd_conv_b_2"].reshape(-1)),
             taps(a["ffn_conv_w_2"][0]), by_part(a["ffn_conv_b_2"].reshape(-1))]
    rows = np.concatenate([a[n].reshape(-1) for n in ("diff_norm_g", "ret_norm_g", "diff_lambda", "ret_log_decay", "ssd_dt_bias_2",
                                                      "ssd_a_log_2", "ssd_d_2", "final_norm_g", "norm_final_w_2")])
    by_token = lambda v: np.ascontiguousarray(v.reshape(TT, P, -1).transpose(1, 0, 2))
    return {
        "weights": np.concatenate(order),
        "consts": CONST,
        "cols": np.ascontiguousarray(np.concatenate(cols, axis=1)),
        "rows": np.ascontiguousarray(np.broadcast_to(rows, (P, len(rows)))),
        "x": by_token(a["x"]),
        "mem": by_token(a["mem_2"]),
        "positions": np.ascontiguousarray(a["positions_2"].reshape(TT, P).T),
    }


def kernel(**inputs):
    import concourse.bacc as bacc
    from concourse.bass_utils import run_bass_kernel_spmd

    arrays = lay_out(inputs)
    nc = bacc.Bacc("TRN2", target_bir_lowering=False, num_devices=1)
    args = [nc.dram_tensor(name + "_in", v.shape, mybir.dt.from_np(v.dtype), kind="ExternalInput").ap()
            for name, v in arrays.items()]
    out = nc.dram_tensor("out", (P, TT, D), F32, kind="ExternalOutput").ap()
    two_blocks(nc, *args, out)
    r = run_bass_kernel_spmd(nc, [{n + "_in": v for n, v in arrays.items()}], core_ids=[0])
    got = r.results[0]["out"]
    return got.transpose(1, 0, 2).reshape(1, T, D)
```

```python
from contextlib import ExitStack

import numpy as np

import concourse.bass as bass
from concourse import mybir

ALU = mybir.AluOpType
ACT = mybir.ActivationFunctionType
F32 = mybir.dt.float32
F32R = mybir.dt.float32r
I32 = mybir.dt.int32
U32 = mybir.dt.uint32
AX = mybir.AxisListType.X

P = 128
T, D = 256, 1024
TT = T // P
KD = D // P
EPS = 1e-6

HD = 4
LAMBDA_INIT = 0.2
PH, TOPK, NK = 8, 16, 128
SH, SP_, SG = 16, 64, 4
MH, MNOPE, MROPE, MV = 16, 64, 32, 64
MQ = MNOPE + MROPE
DTQ, KVR = 16 + 384, 256 + 32
FF = 2816 // P
NEG = -1.0e30

NR = 3
NS = 3

STAGES = [("w_in", 24), ("w_out", 8), ("queries", 20), ("mem_k", 8), ("mem_v", 8), ("experts", 2 * NK),
          ("z", 8), ("dt_q", 4), ("kv_rope", 4), ("xbc", 16), ("q_up", 5), ("kv_up", 4),
          ("w_out_2", 16), ("mem_q", 8), ("mem_o", 8), ("ffn", 3 * FF)]
SLOT, _n = {}, 0
for _name, _k in STAGES:
    SLOT[_name] = _n
    _n += _k
N_SLOTS = _n

TURNS = [("attn_norm", 4), ("qk", 6), ("mix", 4), ("ffn_norm", 4), ("norm_mem", 4), ("chosen", 2), ("norm_mix", 4),
         ("xs", 4), ("ssd", 4), ("latents", 3), ("mla_q", 8), ("mla_k", 8), ("mla_out", 4),
         ("norm_memx", 4), ("norm_ffn", 4)]
COPIES = [("w_in", 6, 6), ("mem_k", 8, 0), ("mem_v", 4, 0), ("z", 2, 2), ("dt_q", 1, 1), ("kv_rope", 1, 1),
          ("q_up", 3, 3), ("kv_up", 4, 4), ("mem_q", 4, 4)]


def _bases():
    turn, at, av = {}, 0, 0
    b = 0
    for name, n in TURNS:
        turn[name] = (b, at, av, n)
        b += n
        if name in ("qk", "chosen", "xs", "mla_q", "mla_k"):
            at, av = at + (n + 1) // 2, av + n // 2
    copy, ca, cv = {}, 0, 0
    for name, a, v in COPIES:
        copy[name] = (ca, cv)
        ca, cv = ca + a, cv + v
    return turn, copy


TURN, COPY = _bases()
SPLIT, _n = {}, 0
for _name, _k in [("attn_norm", 8), ("mix", 8), ("ffn_norm", 8), ("norm_mem", 8), ("w_query", 16), ("norm_mix", 8), ("ssd", 8),
                  ("latents", 5), ("mla_out", 8), ("norm_memx", 8), ("norm_ffn", 8)]:
    SPLIT[_name] = _n
    _n += _k
NORMS = {"attn": 0, "ffn": 1, "mem": 2, "final1": 3, "mix": 4, "memx": 5, "ffn2": 6, "final2": 7}



def shape_constants():
    f = np.float32
    pos = np.arange(T, dtype=f)
    rot = 16
    inv = np.power(f(500000.0), -np.arange(rot // 2, dtype=f) * f(2.0) / f(rot)).astype(f)
    ret = (f(1.0) / np.power(f(10000.0), np.linspace(0.0, 1.0, 32, dtype=f))).astype(f)
    mla = (f(1.0) / np.power(f(10000.0), np.arange(0, 32, 2, dtype=f) / f(32))).astype(f)
    by_token = lambda a: a.reshape(TT, P, -1).transpose(1, 0, 2).reshape(P, -1)
    a1, a2 = pos[:, None] * inv[None], pos[:, None] * ret[None]
    i, j = np.arange(T)[None, :], np.arange(T)[:, None]
    parts = [
        ("ident", np.eye(P)),
        ("iota", np.broadcast_to(np.arange(P), (P, P))),
        ("cos_d", by_token(np.cos(a1))), ("sin_d", by_token(np.sin(a1))),
        ("cos_r", by_token(np.cos(a2))), ("sin_r", by_token(np.sin(a2))),
        ("inv_m", np.broadcast_to(mla, (P, 16))),
        ("later", by_token(np.maximum(i - j, 0))),
        ("earlier", by_token(np.maximum(j - i, 0))),
        ("tri", by_token((j <= i))),
        ("mask", by_token(np.where(i // 64 <= j // 64, 0.0, NEG))),
    ]
    at, n = {}, 0
    for name, a in parts:
        at[name] = (n, n + a.shape[1])
        n += a.shape[1]
    return np.concatenate([np.asarray(a, f) for _, a in parts], axis=1), at


CONST, CAT = shape_constants()
NCONST = CAT["later"][0]

COLS = [("attn_g", 8), ("ffn_g", 8), ("mix_g", 8), ("mem_g", 8), ("memx_g", 8), ("ffn2_g", 8),
        ("ssd_g", 8), ("q_g", 3), ("kv_g", 2), ("xw", 64), ("xb", 16), ("fw", 44 * 3), ("fb", 44)]
ROWS = [("diff_g", 128), ("ret_g", 512), ("lam", 256), ("decay", 8), ("dt_bias", 16), ("a_log", 16), ("d_skip", 16),
        ("final1_g", 1024), ("final2_g", 1024)]


def _places(parts):
    at, n = {}, 0
    for name, k in parts:
        at[name] = (n, n + k)
        n += k
    return at, n


COL, NCOLS = _places(COLS)
ROW, _ = _places(ROWS)
NROWS = ROW["final1_g"][0]

AREA = dict(
    x_scaled=(24576, 26624), squares=(26624, 27648),
    proj=(0, 6144), qk_t=(6144, 9216), decay=(9216, 11264), gate_r=(11264, 12288), e_diff=(12288, 13312),
    a_diff=(13312, 13824), at_diff=(13824, 14336), o_diff=(14336, 15360), p_ret=(15360, 17408),
    later_earlier=(27648, 28672), final_g=(31744, 32768), tri=(22016, 22528), mask=(27136, 27648),
    o_ret=(17408, 18432), mix=(18432, 20480), rot=(20480, 22528), stat=(22528, 22784),
    pq_hi=(18432, 22528), pq_lo=(22528, 26624), keys=(4096, 8192), spare=(8192, 8704), vals=(8704, 9216), idx=(9216, 9728), idxf=(9728, 10240),
    cand=(10240, 14336), best=(14336, 14592), pos=(14592, 14848), hi=(14848, 15104), lo=(15104, 15360),
    eq=(15360, 17408), chosen=(17408, 18176), gst=(18176, 18432),
    z=(0, 2048), lat=(2048, 4096), xc=(4096, 8192), xs=(8192, 10240), xdt=(10240, 12288), cb=(12288, 14336),
    seg=(27648, 29696), y=(15360, 17408), dts=(17408, 17920), m_hi=(17920, 19968), m_lo=(19968, 22016), lat_hi=(22016, 23296), lat_lo=(24576, 25856),
    rope=(23296, 24576),
    q=(4096, 7168), kv=(7168, 11264), kcat=(11264, 14336), q_t=(27648, 31744), k_t=(0, 4096),
    s_m=(14336, 14848), e_m=(14848, 15360), et_m=(15360, 15872), o_m=(15872, 17920),
    mem=(28672, 30720), mem_hi=(0, 2048), mem_lo=(2048, 4096), mk_first=(18432, 20480), mv_first=(20480, 22528), mk_t=(4096, 6144), mv=(6144, 8192), mq_t=(8192, 10240),
    e_x=(10240, 10752), et_x=(10752, 11776),
    gate_f=(0, 512), value_f=(512, 1024), out=(0, 2048),
)


def two_blocks(nc, weights, consts, cols_in, rows_in, x_in, mem_in, pos_in, out):
    with ExitStack() as ctx:
        def sb(name, shape, dt=F32):
            return ctx.enter_context(nc.sbuf_tensor(name, shape, dt))

        base = (nc.sbuf_base + 31) // 32 * 32
        arena = sb("arena", [P, NK * T])
        work = sb("work", [P, 9 * T])
        ring = sb("ring", [P, NR, 1024])
        w_hi, w_lo = sb("w_hi", [P, NS, 1024], F32R), sb("w_lo", [P, NS, 1024], F32R)
        xres = sb("xres", [P, TT, D])
        h_t = sb("h_hi", [P, KD, T], F32R), sb("h_lo", [P, KD, T], F32R)
        cst = sb("cst", [P, NCONST])
        cols = sb("cols", [P, NCOLS])
        rows = sb("rows", [P, NROWS])
        chosen_t = sb("chosen_t", [P, 3, T])
        ssq = sb("ssq", [P, 8])
        rstd = sb("rstd", [P, 8])
        lam = sb("lam", [P, 8])
        log_g = sb("log_g", [P, 8])
        sm = sb("sm", [P, 2, 16])
        pos_i = sb("pos_i", [P, TT], I32)
        bank = ctx.enter_context(nc.psum_tensor("bank", [P, 8, 512], F32))

        def area(name, pattern=None, **kw):
            a, b = AREA[name]
            v = arena[:, a:b]
            return v.rearrange(pattern, **kw) if pattern else v

        def parts(name, column, blocks):
            return nc.alloc_sbuf_tensor_at(name, [P, blocks, T], F32R, offset=base + 4 * column)

        pq_t = parts("pq_hi", AREA["pq_hi"][0], 16), parts("pq_lo", AREA["pq_lo"][0], 16)
        m_t = parts("m_hi", AREA["m_hi"][0], KD), parts("m_lo", AREA["m_lo"][0], KD)
        lat_t = parts("lat_hi", AREA["lat_hi"][0], 5), parts("lat_lo", AREA["lat_lo"][0], 5)
        mem_t = parts("mem_hi", AREA["mem_hi"][0], KD), parts("mem_lo", AREA["mem_lo"][0], KD)
        act_t = parts("act_hi", NK * T + 3 * T, 3), parts("act_lo", NK * T + 6 * T, 3)

        def const(name):
            if name in ("later", "earlier"):
                k = 512 * (name == "earlier")
                return area("later_earlier")[:, k:k + 512]
            if name in ("tri", "mask"):
                return area(name)
            return cst[:, CAT[name][0]:CAT[name][1]]

        def col(name, i, n=1):
            return cols[:, COL[name][0] + i:COL[name][0] + i + n]

        def row(name):
            return rows[:, ROW[name][0]:ROW[name][1]]

        ident = const("ident")
        x_scaled = area("x_scaled", "p (t d) -> p t d", t=TT)
        squares = area("squares")
        proj = area("proj", "p (t c) -> p t c", t=TT)
        qk_t = area("qk_t", "p (b t) -> p b t", t=T)
        decay = area("decay", "p (h j i) -> p h j i", h=HD, j=TT)
        gate_r = area("gate_r", "p (t c) -> p t c", t=TT)
        e_diff = area("e_diff", "p (b m k) -> p b m k", b=2, m=2)
        a_diff = area("a_diff", "p (b k) -> p b k", b=2)
        at_diff = area("at_diff", "p (b k q) -> p b k q", b=2, k=2)
        o_diff = area("o_diff", "p (t c) -> p t c", t=TT)
        p_ret = area("p_ret", "p (h j i) -> p h j i", h=HD, j=TT)
        o_ret = area("o_ret", "p (t c) -> p t c", t=TT)
        mix = area("mix", "p (t c) -> p t c", t=TT)
        keys = area("keys", "p (t b c) -> p t b c", t=TT, c=512)
        gates = arena[:, :].rearrange("p (i t) -> p i t", t=T)
        z = area("z", "p (t c) -> p t c", t=TT)
        lat = area("lat", "p (t c) -> p t c", t=TT)
        xc = area("xc", "p (b t) -> p b t", t=T)
        xs = area("xs", "p (t c) -> p t c", t=TT)
        xdt = area("xdt", "p (t c) -> p t c", t=TT)
        cb = area("cb", "p (g s l) -> p g s l", g=SG, s=TT)
        seg = area("seg", "p (b l) -> p b l", b=4)
        y = area("y", "p (t c) -> p t c", t=TT)
        q = area("q", "p (t c) -> p t c", t=TT)
        kv = area("kv", "p (t c) -> p t c", t=TT)
        kcat = area("kcat", "p (t c) -> p t c", t=TT)
        q_t = area("q_t", "p (h t) -> p h t", t=T)
        k_t = area("k_t", "p (h t) -> p h t", t=T)
        s_m = area("s_m", "p (b k) -> p b k", b=2)
        e_m = area("e_m", "p (b k) -> p b k", b=2)
        et_m = area("et_m", "p (b k q) -> p b k q", b=2, k=2)
        o_m = area("o_m", "p (t c) -> p t c", t=TT)
        mem = area("mem", "p (t c) -> p t c", t=TT)
        mk_first = area("mk_first", "p (b t) -> p b t", t=T)
        mv_first = area("mv_first", "p (t c) -> p t c", t=TT)
        mk_t = area("mk_t", "p (b t) -> p b t", t=T)
        mv = area("mv", "p (t c) -> p t c", t=TT)
        mq_t = area("mq_t", "p (b t) -> p b t", t=T)
        e_x = area("e_x", "p (b k) -> p b k", b=2)
        et_x = area("et_x", "p (b k q) -> p b k q", b=2, k=2)
        out_sb = area("out", "p (t c) -> p t c", t=TT)

        loaded = [ctx.enter_context(nc.semaphore(f"slot_loaded_{i}")) for i in range(NR)]
        s = {name: ctx.enter_context(nc.semaphore(name)) for name in (
            "x_loaded", "params_loaded", "mem_loaded", "out_stored",
            "keys_copied", "mem_kv_stored", "mem_kv_loaded", "chosen_all", "mem_hi_made", "hi_made", "split", "spent", "phase", "split_act", "split_dve", "gain_loaded", "tri_loaded", "mask_loaded", "act_product", "act_hi_made", "dve_done", "act_done",
            "norm_summed", "norm_mean", "norm_rooted", "norm_factor", "norm_scaled",
            "turned", "turned_out_act", "turned_out_dve", "copied_act", "copied_dve",
            "lambda_products", "lambda_exp", "decay_arg", "decay_exp",
            "diff_scores", "diff_shift", "diff_exp", "diff_mixed", "diff_turned", "diff_t_copied", "diff_out", "diff_out_copied",
            "ret_scores", "ret_decayed", "ret_out", "ret_out_copied",
            "head_mean", "head_root", "gate_shifted", "gate_exp",
            "one_hot_1", "one_hot_2", "spread", "spread_copied",
            "gelu_done", "weighed",
            "conv_done", "filter_step", "latents_scaled", "choice_made", "residual_ready",
            "dt_arg", "dt_e", "dt_l", "dt_scaled", "cum_done", "cb_done", "cb_masked",
            "seg_sum", "seg_clipped", "seg_exp", "seg_weighed", "ssd_out",
            "group_mean", "group_root", "trig_arg", "trig_done",
            "mla_scores", "mla_shift", "mla_exp", "mla_turned", "mla_t_copied", "mla_out", "mla_out_copied",
            "mem_scores", "mem_shift", "mem_exp", "mem_scaled", "mem_turned", "mem_t_copied", "mem_out", "mem_out_copied",
            "ffn_conv_g", "ffn_conv_v", "ffn_silu", "ffn_act",
        )}

        def wait_slot(pe, n):
            pe.wait_ge(s["split"], n + 1)

        def begin(eng, n):
            if n:
                eng.wait_ge(s["phase"], 3 * n)

        def end(eng):
            eng.drain().then_inc(s["phase"], 1)

        mem_kv = nc.dram_tensor("mem_kv", (P, 2, 2048), F32).ap()

        block = ctx.enter_context(nc.Block())

        @block.sync
        def _(sp):
            def slot_load(n, k):
                src = weights[bass.ds(n, 1)].rearrange("a p f -> p (a f)")
                sp.dma_start(ring[:, k, :], src).then_inc(loaded[k], 16)

            total = N_SLOTS
            sp.dma_start(xres[:, :, :], x_in).then_inc(s["x_loaded"], 16)
            for n in range(NR):
                slot_load(n, n)
            full = (total - NR) // NR
            with sp.Fori(1, full + 1) as r:
                for k in range(NR):
                    sp.wait_ge(s["split"], r * NR + (k + 1 - NR))
                    slot_load(r * NR + k, k)
            for n in range((full + 1) * NR, total):
                sp.wait_ge(s["split"], n + 1 - NR)
                slot_load(n, n % NR)

        @block.gpsimd
        def _(pool):
            def lo_part(n, k):
                pool.wait_ge(s["hi_made"], n + 1)
                nc.gpsimd.tensor_tensor(w_lo[:, k, :], ring[:, k, :], w_hi[:, k, :].bitcast(F32), ALU.subtract)\
                    .then_inc(s["split"], 1)

            def lo_parts(first, end_):
                n = first
                while n < end_ and n % NS:
                    lo_part(n, n % NS)
                    n += 1
                rounds = (end_ - n) // NS
                with pool.Fori(0, rounds) as r:
                    for k in range(NS):
                        lo_part(r * NS + (n + k), k)
                for m in range(n + rounds * NS, end_):
                    lo_part(m, m % NS)

            pool.dma_start(cols[:, :], cols_in).then_inc(s["params_loaded"], 16)
            pool.dma_start(cst[:, :], consts[:, 0:NCONST]).then_inc(s["params_loaded"], 16)
            pool.dma_start(rows[:, :], rows_in[:, 0:NROWS]).then_inc(s["params_loaded"], 16)
            pool.dma_start(pos_i[:, :], pos_in).then_inc(s["params_loaded"], 16)
            pool.dma_start(mem[:, :, :], mem_in).then_inc(s["mem_loaded"], 16)
            pool.dma_start(area("later_earlier"), consts[:, NCONST:NCONST + 1024]).then_inc(s["params_loaded"], 16)
            lo_parts(0, N_SLOTS)

        @block.tensor
        def _(pe):
            def product(out_, a, b, start, stop, **kw):
                pe.matmul(out_, a[0], b[0], start=start, stop=False, **kw)
                pe.matmul(out_, a[0], b[1], start=False, stop=False, **kw)
                return pe.matmul(out_, a[1], b[0], start=False, stop=stop, **kw)

            def both(pair, *index):
                return [x[index] for x in pair]

            every = slice(0, P)
            w_parts = (w_hi, w_lo)

            def turn(name, source, blocks, width=P, bank0=0):
                first, act0, dve0, n = TURN[name]
                for b in range(blocks):
                    k = b // 2
                    if b % 2 == 0 and k >= 8:
                        if k % 2 == 0:
                            pe.wait_ge(s["turned_out_act"], act0 + (k - 8) // 2 + 1)
                        else:
                            pe.wait_ge(s["turned_out_dve"], dve0 + (k - 8) // 2 + 1)
                    for t in range(TT):
                        at = (b % 2) * T + t * P
                        mm = pe.transpose(bank[0:width, bank0 + k % 8, at:at + P], source(b, t), ident)
                    if b % 2 == 1 or b == blocks - 1:
                        mm.then_inc(s["turned"], 1)

            def norm_turn(name, which, bank0=0):
                pe.wait_ge(s["norm_scaled"], 2 * which + 2)
                turn(name, lambda b, t: x_scaled[:, t, b * P:(b + 1) * P], KD, bank0=bank0)

            def by_tokens(name, src, depth, widths, first_block=0, bank0=0):
                first, (act0, dve0) = SLOT[name], COPY[name]
                panels = len(widths) * depth
                for c, w in enumerate(widths):
                    if c >= 2:
                        pe.wait_ge(s["copied_act"], act0 + c - 1)
                        pe.wait_ge(s["copied_dve"], dve0 + c - 1)
                    for k in range(depth):
                        p = c * depth + k
                        n, half = first + p // 2, p % 2
                        if half == 0:
                            wait_slot(pe, n)
                        for t in range(TT):
                            mm = product(bank[:, bank0 + 2 * (c % 2) + t, 0:w],
                                         both(src, every, first_block + k, slice(t * P, (t + 1) * P)),
                                         both(w_parts, every, n % NS, slice(half * 512, half * 512 + w)),
                                         start=(k == 0), stop=(k == depth - 1))
                        if half == 1 or p == panels - 1:
                            mm.then_inc(s["spent"], 1)

            def by_channels(name, src, blocks, free):
                for j in range(blocks):
                    n = SLOT[name] + j
                    if j >= 4:
                        free(j)
                    wait_slot(pe, n)
                    for k in range(KD):
                        mm = product(bank[:, j % 4, 0:T], both(w_parts, every, n % NS, slice(k * P, (k + 1) * P)),
                                     both(src, every, k, slice(0, T)), start=(k == 0), stop=(k == KD - 1))
                    mm.then_inc(s["spent"], 1)

            def free_by(name):
                act0, dve0 = COPY[name]

                def free(j):
                    if j % 2 == 0:
                        pe.wait_ge(s["copied_act"], act0 + (j - 4) // 2 + 1)
                    else:
                        pe.wait_ge(s["copied_dve"], dve0 + (j - 4) // 2 + 1)
                return free

            def into_residual(name, src, depth):
                for k in range(depth):
                    n = SLOT[name] + k
                    wait_slot(pe, n)
                    for t in range(TT):
                        for h in range(2):
                            mm = product(bank[:, 2 * t + h, :],
                                         both(src[k // KD], every, k % KD, slice(t * P, (t + 1) * P)),
                                         both(w_parts, every, n % NS, slice(h * 512, (h + 1) * 512)),
                                         start=(k == 0), stop=(k == depth - 1))
                    mm.then_inc(s["spent"], 1)

            pe.wait_ge(s["params_loaded"], 80)
            norm_turn("attn_norm", NORMS["attn"])
            end(pe)
            begin(pe, 1)
            by_tokens("w_in", h_t, KD, [512] * 6)
            end(pe)
            begin(pe, 2)
            end(pe)
            begin(pe, 3)
            turn("qk", lambda b, t: proj[:, t, b * P:(b + 1) * P] if b < 8 else
                 proj[:, t, 1536 + (b - 8) * P:1536 + (b - 7) * P], 12)
            end(pe)
            begin(pe, 4)
            units = [(h, t) for h in range(HD) for t in range(TT)]

            def diff_scores(u):
                h, t = units[u]
                if u >= 2:
                    pe.wait_ge(s["diff_exp"], u - 1)
                for m in range(2):
                    r = slice(m * 64, m * 64 + 64)
                    mm = pe.matmul(bank[:, 2 * (u % 2) + m, 0:T], qk_t[r, h, t * P:(t + 1) * P],
                                   qk_t[r, 4 + h, :], start=True, stop=True)
                mm.then_inc(s["diff_scores"], 1)

            def diff_turn(u):
                pe.wait_ge(s["diff_mixed"], u + 1)
                if u >= 2:
                    pe.wait_ge(s["diff_t_copied"], u - 1)
                for k in range(2):
                    mm = pe.transpose(bank[:, 4 + u % 2, k * P:(k + 1) * P], a_diff[:, u % 2, k * P:(k + 1) * P], ident)
                mm.then_inc(s["diff_turned"], 1)

            diff_scores(0)
            diff_scores(1)
            diff_turn(0)
            for u, (h, t) in enumerate(units):
                if u + 2 < len(units):
                    diff_scores(u + 2)
                if u + 1 < len(units):
                    diff_turn(u + 1)
                pe.wait_ge(s["diff_t_copied"], u + 1)
                if u >= 2:
                    pe.wait_ge(s["diff_out_copied"], u - 1)
                for k in range(2):
                    mm = pe.matmul(bank[:, 6 + u % 2, 0:P], at_diff[:, u % 2, k, :],
                                   proj[:, k, 1024 + h * P:1024 + (h + 1) * P], start=(k == 0), stop=(k == 1))
                mm.then_inc(s["diff_out"], 1)
            end(pe)
            begin(pe, 5)

            def ret_scores(h):
                r = slice((h % 2) * 64, (h % 2) * 64 + 64)
                if h >= 2:
                    pe.wait_ge(s["ret_decayed"], h - 1)
                for j in range(TT):
                    mm = pe.matmul(bank[:, h % 2, j * T:(j + 1) * T], qk_t[r, 10 + h // 2, j * P:(j + 1) * P],
                                   qk_t[r, 8 + h // 2, :], start=True, stop=True)
                mm.then_inc(s["ret_scores"], 1)

            ret_scores(0)
            for h in range(HD):
                if h + 1 < HD:
                    ret_scores(h + 1)
                pe.wait_ge(s["ret_decayed"], h + 1)
                for t in range(TT):
                    for j in range(TT):
                        mm = pe.matmul(bank[:, 2 + t, h * P:(h + 1) * P], p_ret[:, h, j, t * P:(t + 1) * P],
                                       proj[:, j, 2048 + h * P:2048 + (h + 1) * P], start=(j == 0), stop=(j == 1))
                mm.then_inc(s["ret_out"], 1)
            end(pe)
            begin(pe, 6)
            end(pe)
            begin(pe, 7)
            turn("mix", lambda b, t: mix[:, t, b * P:(b + 1) * P], KD)
            end(pe)
            begin(pe, 8)
            into_residual("w_out", [h_t], KD)
            end(pe)
            begin(pe, 9)
            norm_turn("ffn_norm", NORMS["ffn"])
            norm_turn("norm_mem", NORMS["mem"], bank0=4)
            end(pe)
            begin(pe, 10)
            for b in range(4):
                for i in range(4):
                    n = SLOT["queries"] + 5 * b + i
                    if b:
                        pe.wait_ge(s["split_dve"], 4 * (b - 1) + i + 1)
                    wait_slot(pe, n)
                    for k in range(KD):
                        mm = product(bank[:, i, 0:T], both(w_parts, every, n % NS, slice(k * P, (k + 1) * P)),
                                     both(h_t, every, k, slice(0, T)), start=(k == 0), stop=(k == KD - 1))
                    mm.then_inc(s["spent"], 1)
                n = SLOT["queries"] + 5 * b + 4
                pe.wait_ge(s["split_dve"], 4 * b + 4)
                if b >= 2:
                    pe.wait_ge(s["keys_copied"], 2 * b - 2)
                wait_slot(pe, n)
                for t in range(TT):
                    for i in range(4):
                        mm = product(bank[:, 4 + 2 * (b % 2) + t, i * P:(i + 1) * P],
                                     both(pq_t, every, 4 * b + i, slice(t * P, (t + 1) * P)),
                                     both(w_parts, every, n % NS, slice(i * P, (i + 1) * P)), start=True, stop=True)
                mm.then_inc(s["spent"], 1)
            end(pe)
            begin(pe, 11)
            turn_after_choice = area("chosen", "p (f c) -> p f c", f=6)
            by_channels("mem_k", mem_t, 8, lambda j: pe.wait_ge(s["copied_act"], COPY["mem_k"][0] + j - 3))
            by_tokens("mem_v", mem_t, KD, [512, 512], bank0=4)
            pe.wait_ge(s["copied_act"], COPY["mem_k"][0] + 8)
            pe.wait_ge(s["choice_made"], 1)
            turn("chosen", lambda b, t: turn_after_choice[:, b * 2 + t, :], 3)
            end(pe)
            begin(pe, 12)
            one_hots = lambda b: work[:, b * 512:(b + 1) * 512].rearrange("p (t k) -> p t k", t=4)

            def spread(g, u):
                pe.wait_ge(s["one_hot_1"], 4 * g + 4)
                pe.wait_ge(s["one_hot_2"], g + 1)
                for i in range(4):
                    mm = pe.matmul(bank[:, u, i * P:(i + 1) * P], one_hots(2 + u)[:, i, :], one_hots(u)[:, i, :],
                                   start=True, stop=True)
                mm.then_inc(s["spread"], 1)

            spread(0, 0)
            spread(1, 1)
            with pe.Fori(1, T // 8) as r:
                for u in range(2):
                    pe.wait_ge(s["spread_copied"], r * 2 + (u - 1))
                    spread(r * 2 + u, u)
            end(pe)
            begin(pe, 13)
            X = SLOT["experts"]
            U3 = 3

            def down(n, k, u):
                pe.wait_ge(s["split"], n + 1)
                for c in range(KD):
                    mm = product(bank[:, 4 + u, 0:T], both(w_parts, every, k, slice(c * P, (c + 1) * P)),
                                 both(h_t, every, c, slice(0, T)), start=(c == 0), stop=(c == KD - 1))
                mm.then_inc(s["spent"], 1)

            def up(n, k, u, done, start=False, stop=False):
                pe.wait_ge(s["split"], n + 1)
                pe.wait_ge(s["weighed"], done)
                for t in range(TT):
                    for h in range(2):
                        mm = product(bank[:, 2 * t + h, :], both(act_t, every, u, slice(t * P, (t + 1) * P)),
                                     both(w_parts, every, k, slice(h * 512, (h + 1) * 512)), start=start, stop=stop,
                                     skip_group_check=True)
                mm.then_inc(s["spent"], 1)

            down(X, X % NS, 0)
            down(X + 1, (X + 1) % NS, 1)
            up(X + 2, (X + 2) % NS, 0, 1, start=True)
            with pe.Fori(0, (NK - 2) // U3) as r:
                for u in range(U3):
                    pe.wait_ge(s["gelu_done"], r * U3 + (u + 1))
                    n = X + 3 + 2 * u
                    down(r * (2 * U3) + n, n % NS, (2 + u) % U3)
                    up(r * (2 * U3) + (n + 1), (n + 1) % NS, (1 + u) % U3, r * U3 + (2 + u))
            n = X + 2 * NK - 1
            up(n, n % NS, (NK - 1) % U3, NK, stop=True)
            end(pe)
            begin(pe, 14)
            end(pe)
            begin(pe, 15)
            norm_turn("norm_mix", NORMS["mix"])
            end(pe)
            begin(pe, 16)
            by_tokens("z", h_t, KD, [512, 512])
            pe.wait_ge(s["copied_act"], COPY["z"][0] + 1)
            pe.wait_ge(s["copied_dve"], COPY["z"][1] + 1)
            by_tokens("dt_q", h_t, KD, [DTQ])
            end(pe)
            begin(pe, 17)
            by_tokens("kv_rope", h_t, KD, [KVR])
            end(pe)
            begin(pe, 18)
            by_channels("xbc", h_t, 16, lambda j: pe.wait_ge(s["conv_done"], 4 * (j - 3)))
            end(pe)
            begin(pe, 19)
            for t in range(TT):
                for b in range(2):
                    for i in range(4):
                        mm = pe.transpose(bank[:, 2 * t + b, i * P:(i + 1) * P], xc[:, 4 * b + i, t * P:(t + 1) * P], ident)
                    mm.then_inc(s["turned"], 1)
            for g in range(SG):
                for j in range(TT):
                    mm = pe.matmul(bank[:, 4 + g % 2, j * T:(j + 1) * T],
                                   xc[:, 8 + g, j * P:(j + 1) * P], xc[:, 12 + g, :], start=True, stop=True)
                mm.then_inc(s["cb_done"], 1)
                if g >= 1 and g + 1 < SG:
                    pe.wait_ge(s["cb_masked"], g)
            pe.wait_ge(s["dt_scaled"], 1)
            pe.wait_ge(s["tri_loaded"], 16)
            adt = area("dts")[:, 0:32].rearrange("p (t h) -> p t h", t=TT)
            tri = const("tri").rearrange("p (j l) -> p j l", j=TT)
            for t in range(TT):
                for j in range(t + 1):
                    mm = pe.matmul(bank[:, 6, t * 16:(t + 1) * 16], tri[:, j, t * P:(t + 1) * P], adt[:, j, :],
                                   start=(j == 0), stop=(j == t))
            mm.then_inc(s["cum_done"], 1)
            end(pe)
            begin(pe, 20)

            def seg_sum(h):
                if h >= 4:
                    pe.wait_ge(s["seg_clipped"], 2 * (h - 3))
                for j in range(TT):
                    mm = pe.matmul(bank[:, h % 4, 0:T], adt[:, j, h:h + 1].to_broadcast([P, P]), tri[:, j, :],
                                   start=(j == 0), stop=(j == 1))
                mm.then_inc(s["seg_sum"], 1)

            for h in range(3):
                seg_sum(h)
            for h in range(SH):
                if h + 3 < SH:
                    seg_sum(h + 3)
                pe.wait_ge(s["seg_weighed"], 2 * (h + 1))
                lo = (h % 8) * 64
                pe.matmul(bank[:, 4 + h // 8, lo:lo + 64], seg[:, h % 4, 0:P], xdt[:, 0, h * 64:(h + 1) * 64],
                          start=True, stop=True)
                pe.matmul(bank[:, 6 + h // 8, lo:lo + 64], seg[:, h % 4, P:2 * P], xdt[:, 0, h * 64:(h + 1) * 64],
                          start=True, stop=False)
                pe.matmul(bank[:, 6 + h // 8, lo:lo + 64], seg[:, h % 4, 2 * P:3 * P], xdt[:, 1, h * 64:(h + 1) * 64],
                          start=False, stop=True).then_inc(s["ssd_out"], 1)
            end(pe)
            begin(pe, 21)
            end(pe)
            begin(pe, 22)
            turn("ssd", lambda b, t: y[:, t, b * P:(b + 1) * P], KD)
            end(pe)
            begin(pe, 23)
            pe.wait_ge(s["latents_scaled"], 1)
            turn("latents", lambda b, t: lat[:, t, 16 + b * P:16 + (b + 1) * P] if b < 3 else
                 lat[:, t, 512 + (b - 3) * P:512 + (b - 2) * P], 5)
            end(pe)
            begin(pe, 24)
            by_tokens("q_up", lat_t, 3, [512] * 3)
            pe.wait_ge(s["copied_act"], COPY["q_up"][0] + 3)
            pe.wait_ge(s["copied_dve"], COPY["q_up"][1] + 3)
            by_tokens("kv_up", lat_t, 2, [512] * 4, first_block=3)
            end(pe)
            begin(pe, 25)
            end(pe)
            begin(pe, 26)
            turn("mla_q", lambda b, t: q[:, t, b * MQ:(b + 1) * MQ], MH, MQ)
            end(pe)
            begin(pe, 27)
            turn("mla_k", lambda b, t: kcat[:, t, b * MQ:(b + 1) * MQ], MH, MQ)
            end(pe)
            begin(pe, 28)
            munits = [(h, t) for h in range(MH) for t in range(TT)]

            def mla_scores(u):
                h, t = munits[u]
                if u >= 2:
                    pe.wait_ge(s["mla_shift"], u - 1)
                pe.matmul(bank[:, u % 2, 0:(t + 1) * P], q_t[0:MQ, h, t * P:(t + 1) * P], k_t[0:MQ, h, 0:(t + 1) * P],
                          start=True, stop=True).then_inc(s["mla_scores"], 1)

            def mla_turn(u):
                t = u % 2
                pe.wait_ge(s["mla_exp"], u + 1)
                if u >= 2:
                    pe.wait_ge(s["mla_t_copied"], u - 1)
                for k in range(t + 1):
                    mm = pe.transpose(bank[:, 2 + u % 2, k * P:(k + 1) * P], e_m[:, u % 2, k * P:(k + 1) * P], ident)
                mm.then_inc(s["mla_turned"], 1)

            mla_scores(0)
            mla_scores(1)
            mla_turn(0)
            for u, (h, t) in enumerate(munits):
                if u + 2 < len(munits):
                    mla_scores(u + 2)
                if u + 1 < len(munits):
                    mla_turn(u + 1)
                pe.wait_ge(s["mla_t_copied"], u + 1)
                if u >= 2:
                    pe.wait_ge(s["mla_out_copied"], u - 1)
                for k in range(t + 1):
                    mm = pe.matmul(bank[:, 4 + u % 2, 0:MV], et_m[:, u % 2, k, :],
                                   kv[:, k, h * 128 + MNOPE:(h + 1) * 128], start=(k == 0), stop=(k == t))
                mm.then_inc(s["mla_out"], 1)
            end(pe)
            begin(pe, 29)
            turn("mla_out", lambda b, t: o_m[:, t, b * P:(b + 1) * P], KD)
            end(pe)
            begin(pe, 30)
            into_residual("w_out_2", [h_t, m_t], 16)
            end(pe)
            begin(pe, 31)
            norm_turn("norm_memx", NORMS["memx"])
            end(pe)
            begin(pe, 32)
            by_channels("mem_q", h_t, 8, free_by("mem_q"))
            end(pe)
            begin(pe, 33)
            xunits = [(h, t) for h in range(4) for t in range(TT)]

            def mem_scores(u):
                h, t = xunits[u]
                if u >= 2:
                    pe.wait_ge(s["mem_exp"], u - 1)
                for k in range(2):
                    mm = pe.matmul(bank[:, u % 2, 0:T], mq_t[:, 2 * h + k, t * P:(t + 1) * P], mk_t[:, 2 * h + k, :],
                                   start=(k == 0), stop=(k == 1))
                mm.then_inc(s["mem_scores"], 1)

            def mem_turn(u):
                pe.wait_ge(s["mem_scaled"], u + 1)
                if u >= 2:
                    pe.wait_ge(s["mem_t_copied"], u - 1)
                for k in range(2):
                    mm = pe.transpose(bank[:, 2 + u % 2, k * P:(k + 1) * P], e_x[:, u % 2, k * P:(k + 1) * P], ident)
                mm.then_inc(s["mem_turned"], 1)

            pe.wait_ge(s["mem_kv_loaded"], 32)
            mem_scores(0)
            mem_scores(1)
            mem_turn(0)
            for u, (h, t) in enumerate(xunits):
                if u + 2 < len(xunits):
                    mem_scores(u + 2)
                if u + 1 < len(xunits):
                    mem_turn(u + 1)
                if t == 1:
                    pe.wait_ge(s["mem_t_copied"], u + 1)
                    if h >= 2:
                        pe.wait_ge(s["mem_out_copied"], h - 1)
                    for e in range(2):
                        for k in range(2):
                            mm = pe.matmul(bank[:, 4 + h % 2, e * T:(e + 1) * T],
                                           mv[:, k, h * T + e * P:h * T + (e + 1) * P], et_x[:, h % 2, k, :],
                                           start=(k == 0), stop=(k == 1))
                    mm.then_inc(s["mem_out"], 1)
            end(pe)
            begin(pe, 34)
            into_residual("mem_o", [h_t], KD)
            end(pe)
            begin(pe, 35)
            norm_turn("norm_ffn", NORMS["ffn2"])
            end(pe)
            begin(pe, 36)
            F = SLOT["ffn"]
            U2 = 2

            def ffn_up(n, k, u):
                for half in range(2):
                    pe.wait_ge(s["split"], n + (half + 1))
                    for c in range(KD):
                        mm = product(bank[:, 4 + 2 * u + half, 0:T],
                                     both(w_parts, every, (k + half) % NS, slice(c * P, (c + 1) * P)),
                                     both(h_t, every, c, slice(0, T)), start=(c == 0), stop=(c == KD - 1))
                    mm.then_inc(s["spent"], 1)

            def ffn_down(n, k, u, done, start=False, stop=False):
                pe.wait_ge(s["split"], n + 1)
                pe.wait_ge(s["ffn_act"], done)
                for t in range(TT):
                    for h in range(2):
                        mm = product(bank[:, 2 * t + h, :], both(act_t, every, u, slice(t * P, (t + 1) * P)),
                                     both(w_parts, every, k % NS, slice(h * 512, (h + 1) * 512)), start=start, stop=stop,
                                     skip_group_check=True)
                mm.then_inc(s["spent"], 1)

            ffn_up(F, F, 0)
            ffn_up(F + 2, F + 2, 1)
            ffn_down(F + 4, F + 4, 0, 1, start=True)
            with pe.Fori(0, (FF - 2) // U2) as r:
                for u in range(U2):
                    pe.wait_ge(s["ffn_conv_v"], r * U2 + (1 + u))
                    n = F + 5 + 3 * u
                    ffn_up(r * (3 * U2) + n, n, u % 2)
                    ffn_down(r * (3 * U2) + (n + 2), n + 2, (1 + u) % 2, r * U2 + (2 + u))
            n = F + 3 * FF - 1
            ffn_down(n, n, (FF - 1) % 2, FF, stop=True)
            end(pe)

        @block.scalar
        def _(act):
            done = [0]

            def link(ins):
                done[0] += 1
                ins.then_inc(s["act_done"], 1)
                act.wait_ge(s["act_done"], done[0])

            made = [0]

            def hi_part(n, k, load):
                act.wait_ge(loaded[k], load)
                act.wait_ge(s["spent"], n - (NS - 1))
                nc.scalar.copy(w_hi[:, k, :], ring[:, k, :]).then_inc(s["hi_made"], 1)

            def hi_parts(upto):
                for n in range(made[0], upto):
                    if n < NS:
                        act.wait_ge(loaded[n], 16)
                        nc.scalar.copy(w_hi[:, n, :], ring[:, n, :]).then_inc(s["hi_made"], 1)
                    else:
                        hi_part(n, n % NS, 16 * (n // NR + 1))
                made[0] = max(made[0], upto)

            def turned_hi(name, dst, blocks, gain=None, bank0=0):
                for b in range(blocks):
                    if b % 2 == 0:
                        act.wait_ge(s["turned"], TURN[name][0] + b // 2 + 1)
                    at = bank[:, bank0 + b // 2, (b % 2) * T:(b % 2 + 1) * T]
                    ins = nc.scalar.mul(dst[0][:, b, :], at, gain(b)) if gain else nc.scalar.copy(dst[0][:, b, :], at)
                    ins.then_inc(s["split_act"], 1)

            def turned_out(name, dst, blocks, gain=None, rows_=P):
                first, act0, dve0, n = TURN[name]
                for k in range(0, n, 2):
                    act.wait_ge(s["turned"], first + k + 1)
                    width = min(2, blocks - 2 * k)
                    if gain is None:
                        ins = nc.scalar.copy(dst[0:rows_, 2 * k:2 * k + width, :],
                                             bank[0:rows_, k % 8, 0:width * T].rearrange("p (b t) -> p b t", t=T))
                    else:
                        for i in range(width):
                            ins = nc.scalar.mul(dst[:, 2 * k + i, :], bank[:, k % 8, i * T:(i + 1) * T], gain(2 * k + i))
                    ins.then_inc(s["turned_out_act"], 1)

            def norm(which, src):
                for t in range(TT):
                    nc.scalar.activation(squares, src[:, t, :], ACT.Square, accum_out=ssq[:, t:t + 1]).then_inc(s["norm_summed"], 1)
                    act.wait_ge(s["norm_summed"], 2 * which + t + 1)
                act.wait_ge(s["norm_mean"], which + 1)
                nc.scalar.activation(rstd[:, 0:2], ssq[:, 2:4], ACT.Sqrt).then_inc(s["norm_rooted"], 1)
                act.wait_ge(s["norm_factor"], which + 1)
                nc.scalar.mul(x_scaled[:, 0, :], src[:, 0, :], rstd[:, 2:3]).then_inc(s["norm_scaled"], 1)

            def by_tokens(name, depth, widths, dst):
                for c, w in enumerate(widths):
                    n = SLOT[name] + ((c + 1) * depth + 1) // 2
                    hi_parts(n + NS)
                    act.wait_ge(s["spent"], n)
                    nc.scalar.copy(dst[:, 0, c * 512:c * 512 + w], bank[:, 2 * (c % 2), 0:w]).then_inc(s["copied_act"], 1)

            def by_channels(name, blocks, dst):
                for j in range(0, blocks, 2):
                    hi_parts(SLOT[name] + j + 1 + NS)
                    act.wait_ge(s["spent"], SLOT[name] + j + 1)
                    nc.scalar.copy(dst[:, j, :], bank[:, j % 4, 0:T]).then_inc(s["copied_act"], 1)
                hi_parts(SLOT[name] + blocks)

            act.wait_ge(s["x_loaded"], 16)
            norm(NORMS["attn"], xres)
            hi_parts(NS)
            act.wait_ge(s["params_loaded"], 80)
            turned_hi("attn_norm", h_t, KD, lambda b: col("attn_g", b))
            end(act)
            begin(act, 1)
            act.wait_ge(s["lambda_products"], 1)
            nc.scalar.activation(lam[:, 2:4], lam[:, 0:2], ACT.Exp).then_inc(s["lambda_exp"], 1)
            nc.scalar.activation(log_g[:, :], row("decay"), ACT.Exp).then_inc(s["lambda_exp"], 1)
            for c in range(6):
                n = SLOT["w_in"] + 4 * (c + 1)
                hi_parts(n + NS)
                if c < HD:
                    act.wait_ge(s["decay_arg"], c + 1)
                    nc.scalar.activation(decay[:, c, :, :], decay[:, c, :, :], ACT.Exp)
                act.wait_ge(s["spent"], n)
                nc.scalar.copy(proj[:, 0, c * 512:(c + 1) * 512], bank[:, 2 * (c % 2), :]).then_inc(s["copied_act"], 1)
            end(act)
            begin(act, 2)
            nc.scalar.activation(gate_r[:, :, :], proj[:, :, 2560:3072], ACT.Silu)
            end(act)
            begin(act, 3)
            turned_out("qk", qk_t, 12)
            end(act)
            begin(act, 4)
            def diff_exp(u):
                act.wait_ge(s["diff_shift"], u + 1)
                if u >= 2:
                    act.wait_ge(s["diff_mixed"], u - 1)
                for m in range(2):
                    ins = nc.scalar.activation(e_diff[:, u % 2, m, :], bank[:, 2 * (u % 2) + m, 0:T], ACT.Exp,
                                               bias=sm[:, u % 2, m:m + 1], scale=0.125,
                                               accum_out=sm[:, u % 2, 2 + m:3 + m])
                ins.then_inc(s["diff_exp"], 1)

            diff_exp(0)
            for u in range(8):
                if u + 1 < 8:
                    diff_exp(u + 1)
                act.wait_ge(s["diff_turned"], u + 1)
                if u >= 2:
                    act.wait_ge(s["diff_out"], u - 1)
                nc.scalar.copy(at_diff[:, u % 2, :, :], bank[:, 4 + u % 2, 0:T].rearrange("p (k q) -> p k q", k=2))\
                    .then_inc(s["diff_t_copied"], 1)
            end(act)
            begin(act, 5)
            end(act)
            begin(act, 6)
            for i in range(2):
                act.wait_ge(s["head_mean"], i + 1)
                nc.scalar.activation(area("stat")[:, 32 * i + 16:32 * i + 24], area("stat")[:, 32 * i + 8:32 * i + 16], ACT.Sqrt)\
                    .then_inc(s["head_root"], 1)
            end(act)
            begin(act, 7)
            turned_hi("mix", h_t, KD)
            end(act)
            begin(act, 8)
            hi_parts(SLOT["w_out"] + KD + NS)
            end(act)
            begin(act, 9)
            norm(NORMS["ffn"], xres)
            turned_hi("ffn_norm", h_t, KD, lambda b: col("ffn_g", b))
            act.wait_ge(s["mem_loaded"], 16)
            norm(NORMS["mem"], mem)
            turned_hi("norm_mem", mem_t, KD, lambda b: col("mem_g", b), bank0=4)
            end(act)
            begin(act, 10)
            for b in range(4):
                for i in range(4):
                    n = SLOT["queries"] + 5 * b + i
                    hi_parts(n + 1 + NS)
                    act.wait_ge(s["spent"], n + 1)
                    nc.scalar.copy(pq_t[0][:, 4 * b + i, :], bank[:, i, 0:T]).then_inc(s["split_act"], 1)
                n = SLOT["queries"] + 5 * b + 4
                hi_parts(n + 1 + NS)
                act.wait_ge(s["spent"], n + 1)
                for t in range(TT):
                    nc.scalar.copy(keys[:, t, b, :], bank[:, 4 + 2 * (b % 2) + t, :]).then_inc(s["keys_copied"], 1)
            end(act)
            begin(act, 11)
            for j in range(8):
                n = SLOT["mem_k"] + j + 1
                hi_parts(n + NS)
                act.wait_ge(s["spent"], n)
                nc.scalar.copy(mk_first[:, j, :], bank[:, j % 4, 0:T]).then_inc(s["copied_act"], 1)
            for c in range(2):
                n = SLOT["mem_v"] + 4 * (c + 1)
                hi_parts(n + NS)
                act.wait_ge(s["spent"], n)
                for t in range(TT):
                    nc.scalar.copy(mv_first[:, t, c * 512:(c + 1) * 512], bank[:, 4 + 2 * c + t, :])\
                        .then_inc(s["copied_act"], 1)
            act.wait_ge(s["copied_act"], COPY["mem_v"][0] + 4)
            act.dma_start(mem_kv[:, 0, :], area("mk_first")).then_inc(s["mem_kv_stored"], 16)
            act.dma_start(mem_kv[:, 1, :], area("mv_first")).then_inc(s["mem_kv_stored"], 16)
            for t in range(TT):
                best = area("best", "p (t c) -> p t c", t=TT)[:, t, :]
                act.wait_ge(s["gate_shifted"], t + 1)
                nc.scalar.activation(best, best, ACT.Exp).then_inc(s["gate_exp"], 1)
            turned_out("chosen", chosen_t, 3)
            end(act)
            begin(act, 12)
            act.wait_ge(s["mem_kv_stored"], 32)

            def table(g, u):
                act.wait_ge(s["spread"], g + 1)
                nc.scalar.copy(gates[:, :, bass.ds(g * 4, 4)], bank[:, u, :].rearrange("p (t i) -> p i t", t=4))\
                    .then_inc(s["spread_copied"], 1)

            with act.Fori(0, T // 8) as r:
                for u in range(2):
                    table(r * 2 + u, u)
            end(act)
            begin(act, 13)
            X = SLOT["experts"]
            U3 = 3

            def gelu(spent, u):
                act.wait_ge(s["spent"], spent)
                nc.scalar.activation(work[:, u * T:(u + 1) * T], bank[:, 4 + u, 0:T], ACT.Gelu).then_inc(s["gelu_done"], 1)

            hi_parts(X + 4)
            gelu(X + 1, 0)
            hi_parts(X + 5)
            gelu(X + 2, 1)
            hi_parts(X + 7)
            gelu(X + 4, 2)
            with act.Fori(1, NK // U3) as r:
                for u in range(U3):
                    for n in (X + 2 * u + 1, X + 2 * u + 2):
                        hi_part(r * (2 * U3) + n, n % NS, r * (16 * 2 * U3 // NR) + 16 * (n // NR + 1))
                    act.wait_ge(s["weighed"], r * U3 + (u - 2))
                    gelu(r * (2 * U3) + (X + 2 * u), u)
            made[0] = X + 2 * (NK // U3 * U3) + 1
            for k in range(NK // U3 * U3, NK):
                hi_parts(X + 2 * k + 3)
                act.wait_ge(s["weighed"], k - 2)
                gelu(X + 2 * k, k % U3)
            hi_parts(X + 2 * NK + NS)
            end(act)
            begin(act, 14)
            act.dma_start(area("final_g"), rows_in[:, ROW["final1_g"][0]:ROW["final1_g"][1]]).then_inc(s["gain_loaded"], 16)
            act.dma_start(area("tri"), consts[:, CAT["tri"][0]:CAT["tri"][1]]).then_inc(s["tri_loaded"], 16)
            act.wait_ge(s["residual_ready"], 1)
            norm(NORMS["final1"], xres)
            end(act)
            begin(act, 15)
            norm(NORMS["mix"], xres)
            turned_hi("norm_mix", h_t, KD, lambda b: col("mix_g", b))
            end(act)
            begin(act, 16)
            by_tokens("z", KD, [512, 512], z)
            by_tokens("dt_q", KD, [DTQ], lat)
            end(act)
            begin(act, 17)
            hi_parts(SLOT["kv_rope"] + 4 + NS)
            act.wait_ge(s["spent"], SLOT["kv_rope"] + 4)
            nc.scalar.copy(lat[:, 0, 512:512 + KVR], bank[:, 0, 0:KVR]).then_inc(s["copied_act"], 1)
            nc.scalar.activation(z[:, 0, :], z[:, 0, :], ACT.Silu)
            nc.scalar.activation(z[:, 1, :], z[:, 1, :], ACT.Silu)
            end(act)
            begin(act, 18)
            for j in range(16):
                hi_parts(SLOT["xbc"] + j + 1 + NS)
                act.wait_ge(s["conv_done"], 4 * (j + 1))
                nc.scalar.activation(xc[:, j, :], xc[:, j, :], ACT.Silu)
            end(act)
            begin(act, 19)
            dts = area("dts")
            act.wait_ge(s["dt_arg"], 1)
            nc.scalar.activation(dts[:, 96:128], dts[:, 64:96], ACT.Exp, scale=-1.0).then_inc(s["dt_e"], 1)
            act.wait_ge(s["dt_e"], 1)
            nc.scalar.activation(dts[:, 128:160], dts[:, 96:128], ACT.Ln, bias=1.0).then_inc(s["dt_l"], 1)
            nc.scalar.activation(dts[:, 160:176], row("a_log"), ACT.Exp).then_inc(s["dt_l"], 1)
            for k in range(0, 4, 2):
                act.wait_ge(s["turned"], TURN["xs"][0] + k + 1)
                t, b = k // 2, k % 2
                nc.scalar.copy(xs[:, t, b * 512:(b + 1) * 512], bank[:, k, :]).then_inc(s["turned_out_act"], 1)
            end(act)
            begin(act, 20)
            for h in range(SH):
                act.wait_ge(s["seg_clipped"], 2 * (h + 1))
                nc.scalar.activation(seg[:, h % 4, 0:3 * P], seg[:, h % 4, 0:3 * P], ACT.Exp).then_inc(s["seg_exp"], 1)
            end(act)
            begin(act, 21)
            act.wait_ge(s["group_mean"], 1)
            nc.scalar.activation(dts[:, 208:216], dts[:, 200:208], ACT.Sqrt).then_inc(s["group_root"], 1)
            end(act)
            begin(act, 22)
            turned_hi("ssd", h_t, KD, lambda b: col("ssd_g", b))
            end(act)
            begin(act, 23)
            act.wait_ge(s["group_mean"], 2)
            nc.scalar.activation(dts[:, 208:212], dts[:, 200:204], ACT.Sqrt).then_inc(s["group_root"], 1)
            turned_hi("latents", lat_t, 5, lambda b: col("q_g", b) if b < 3 else col("kv_g", b - 3))
            rope = area("rope")
            act.wait_ge(s["trig_arg"], 1)
            nc.scalar.activation(rope[:, 192:256], rope[:, 128:192], ACT.Sin).then_inc(s["trig_done"], 1)
            end(act)
            begin(act, 24)
            act.dma_start(area("mask"), consts[:, CAT["mask"][0]:CAT["mask"][1]]).then_inc(s["mask_loaded"], 16)
            by_tokens("q_up", 3, [512] * 3, q)
            by_tokens("kv_up", 2, [512] * 4, kv)
            end(act)
            begin(act, 25)
            end(act)
            begin(act, 26)
            turned_out("mla_q", q_t, MH, rows_=MQ)
            end(act)
            begin(act, 27)
            turned_out("mla_k", k_t, MH, rows_=MQ)
            end(act)
            begin(act, 28)
            def mla_exp(u):
                w = (u % 2 + 1) * P
                act.wait_ge(s["mla_shift"], u + 1)
                if u >= 2:
                    act.wait_ge(s["mla_turned"], u - 1)
                nc.scalar.activation(e_m[:, u % 2, 0:w], s_m[:, u % 2, 0:w], ACT.Exp, bias=sm[:, u % 2, 0:1],
                                     accum_out=sm[:, u % 2, 1:2]).then_inc(s["mla_exp"], 1)

            mla_exp(0)
            for u in range(2 * MH):
                t = u % 2
                if u + 1 < 2 * MH:
                    mla_exp(u + 1)
                act.wait_ge(s["mla_turned"], u + 1)
                if u >= 2:
                    act.wait_ge(s["mla_out"], u - 1)
                nc.scalar.copy(et_m[:, u % 2, 0:t + 1, :], bank[:, 2 + u % 2, 0:(t + 1) * P].rearrange("p (k q) -> p k q", q=P))\
                    .then_inc(s["mla_t_copied"], 1)
            end(act)
            begin(act, 29)
            act.dma_start(area("mk_t"), mem_kv[:, 0, :]).then_inc(s["mem_kv_loaded"], 16)
            act.dma_start(area("mv"), mem_kv[:, 1, :]).then_inc(s["mem_kv_loaded"], 16)
            act.dma_start(area("final_g"), rows_in[:, ROW["final2_g"][0]:ROW["final2_g"][1]]).then_inc(s["gain_loaded"], 16)
            turned_hi("mla_out", m_t, KD)
            end(act)
            begin(act, 30)
            hi_parts(SLOT["w_out_2"] + 16 + NS)
            end(act)
            begin(act, 31)
            norm(NORMS["memx"], xres)
            turned_hi("norm_memx", h_t, KD, lambda b: col("memx_g", b))
            end(act)
            begin(act, 32)
            by_channels("mem_q", 8, mq_t)
            end(act)
            begin(act, 33)
            def mem_exp(u):
                act.wait_ge(s["mem_shift"], u + 1)
                if u >= 2:
                    act.wait_ge(s["mem_turned"], u - 1)
                nc.scalar.activation(e_x[:, u % 2, :], bank[:, u % 2, 0:T], ACT.Exp, bias=sm[:, u % 2, 0:1],
                                     scale=0.0625, accum_out=sm[:, u % 2, 1:2]).then_inc(s["mem_exp"], 1)

            mem_exp(0)
            for u in range(8):
                h, t = u // 2, u % 2
                if u + 1 < 8:
                    mem_exp(u + 1)
                act.wait_ge(s["mem_turned"], u + 1)
                if h >= 2:
                    act.wait_ge(s["mem_out"], h - 1)
                nc.scalar.copy(et_x[:, h % 2, :, t * P:(t + 1) * P],
                               bank[:, 2 + u % 2, 0:T].rearrange("p (k q) -> p k q", q=P)).then_inc(s["mem_t_copied"], 1)
                if t == 1:
                    act.wait_ge(s["mem_out"], h + 1)
                    nc.scalar.copy(h_t[0][:, 2 * h:2 * h + 2, :], bank[:, 4 + h % 2, :].rearrange("p (e t) -> p e t", e=2))\
                        .then_inc(s["mem_hi_made"], 1)
            end(act)
            begin(act, 34)
            hi_parts(SLOT["mem_o"] + KD + NS)
            end(act)
            begin(act, 35)
            norm(NORMS["ffn2"], xres)
            turned_hi("norm_ffn", h_t, KD, lambda b: col("ffn2_g", b))
            end(act)
            begin(act, 36)
            F = SLOT["ffn"]
            gate_f = area("gate_f", "p (b t) -> p b t", t=T)

            def ffn_silu(done, u):
                act.wait_ge(s["ffn_conv_g"], done)
                nc.scalar.activation(gate_f[:, u, :], gate_f[:, u, :], ACT.Silu).then_inc(s["ffn_silu"], 1)

            hi_parts(F + 4)
            ffn_silu(1, 0)
            hi_parts(F + 6)
            ffn_silu(2, 1)
            with act.Fori(1, FF // 2) as r:
                for u in range(2):
                    for i in range(3):
                        n = F + 3 * u + i
                        hi_part(r * 6 + n, n % NS, r * (16 * 6 // NR) + 16 * (n // NR + 1))
                    ffn_silu(r * 2 + (u + 1), u)
            end(act)
            begin(act, 37)
            act.wait_ge(s["residual_ready"], 2)
            norm(NORMS["final2"], xres)
            act.wait_ge(s["norm_scaled"], 2 * NORMS["final2"] + 2 + 2)
            act.dma_start(out, out_sb[:, :, :]).then_inc(s["out_stored"], 16)
            act.wait_ge(s["out_stored"], 16)

        @block.vector
        def _(dve):
            v = nc.vector
            done = [0]

            def link(ins):
                done[0] += 1
                ins.then_inc(s["dve_done"], 1)
                dve.wait_ge(s["dve_done"], done[0])

            def signal(name):
                dve.drain().then_inc(s[name], 1)

            def turned_out(name, dst, blocks, gain=None, rows_=P):
                first, act0, dve0, n = TURN[name]
                for k in range(1, n, 2):
                    dve.wait_ge(s["turned"], first + k + 1)
                    width = min(2, blocks - 2 * k)
                    if gain is None:
                        ins = v.tensor_copy(dst[0:rows_, 2 * k:2 * k + width, :],
                                            bank[0:rows_, k % 8, 0:width * T].rearrange("p (b t) -> p b t", t=T))
                    else:
                        for i in range(width):
                            ins = v.tensor_scalar(dst[:, 2 * k + i, :], bank[:, k % 8, i * T:(i + 1) * T],
                                                  gain(2 * k + i), None, ALU.mult)
                    ins.then_inc(s["turned_out_dve"], 1)

            def turned_lo(name, dst, blocks, gain=None, bank0=0):
                for b in range(blocks):
                    at = bank[:, bank0 + b // 2, (b % 2) * T:(b % 2 + 1) * T]
                    hi = dst[0][:, b, :].bitcast(F32)
                    dve.wait_ge(s["split_act"], SPLIT[name] + min(b - b % 2 + 2, blocks))
                    if gain is None:
                        v.tensor_tensor(dst[1][:, b, :], at, hi, ALU.subtract)
                    else:
                        v.scalar_tensor_tensor(out=dst[1][:, b, :], in0=at, scalar=gain(b), in1=hi,
                                               op0=ALU.mult, op1=ALU.subtract)

            def norm(which, src):
                dve.wait_ge(s["norm_summed"], 2 * which + 2)
                v.tensor_scalar(ssq[:, 2:4], ssq[:, 0:2], 1.0 / D, EPS, ALU.mult, ALU.add).then_inc(s["norm_mean"], 1)
                dve.wait_ge(s["norm_rooted"], which + 1)
                v.reciprocal(rstd[:, 2:4], rstd[:, 0:2]).then_inc(s["norm_factor"], 1)
                dve.wait_ge(s["norm_factor"], which + 1)
                v.tensor_scalar(x_scaled[:, 1, :], src[:, 1, :], rstd[:, 3:4], None, ALU.mult).then_inc(s["norm_scaled"], 1)

            def by_tokens(name, depth, widths, dst):
                for c, w in enumerate(widths):
                    p = (c + 1) * depth
                    dve.wait_ge(s["spent"], SLOT[name] + (p + 1) // 2)
                    v.tensor_copy(dst[:, 1, c * 512:c * 512 + w], bank[:, 2 * (c % 2) + 1, 0:w]).then_inc(s["copied_dve"], 1)

            def by_channels(name, blocks, dst):
                for j in range(1, blocks, 2):
                    dve.wait_ge(s["spent"], SLOT[name] + j + 1)
                    v.tensor_copy(dst[:, j, :], bank[:, j % 4, 0:T]).then_inc(s["copied_dve"], 1)

            def into_residual(spent):
                dve.wait_ge(s["spent"], spent)
                for t in range(TT):
                    for h in range(2):
                        link(v.tensor_tensor(xres[:, t, h * 512:(h + 1) * 512], xres[:, t, h * 512:(h + 1) * 512],
                                             bank[:, 2 * t + h, :], ALU.add))

            def rotate(x1, x2, cos, sin, tmp):
                v.tensor_tensor(tmp(0), x1, cos, ALU.mult)
                v.tensor_tensor(tmp(1), x2, sin, ALU.mult)
                v.tensor_tensor(tmp(2), x2, cos, ALU.mult)
                link(v.tensor_tensor(tmp(3), x1, sin, ALU.mult))
                v.tensor_tensor(x1, tmp(0), tmp(1), ALU.subtract)
                link(v.tensor_tensor(x2, tmp(2), tmp(3), ALU.add))

            dve.wait_ge(s["x_loaded"], 16)
            norm(NORMS["attn"], xres)
            dve.wait_ge(s["params_loaded"], 80)
            turned_lo("attn_norm", h_t, KD, lambda b: col("attn_g", b))
            end(dve)
            begin(dve, 1)
            lp = row("lam").rearrange("p (a b d) -> p a b d", a=2, b=2)
            lt = area("rot")[:, 0:128].rearrange("p (a d) -> p a d", a=2)
            link(v.tensor_tensor(lt, lp[:, :, 0, :], lp[:, :, 1, :], ALU.mult))
            v.tensor_reduce(lam[:, 0:2], lt, AX, ALU.add).then_inc(s["lambda_products"], 1)
            dve.wait_ge(s["lambda_exp"], 2)
            link(v.tensor_tensor(lam[:, 4:5], lam[:, 3:4], lam[:, 2:3], ALU.subtract))
            link(v.tensor_scalar(lam[:, 5:6], lam[:, 4:5], -LAMBDA_INIT, None, ALU.add))
            later, earlier = const("later"), const("earlier")

            def decay_arg(h):
                dh = decay[:, h, :, :].rearrange("p j i -> p (j i)")
                link(v.tensor_scalar(dh, earlier, log_g[:, 4 + h:5 + h], -1.0, ALU.mult, ALU.mult))
                link(v.tensor_scalar(area("p_ret")[:, 0:512], later, log_g[:, h:h + 1], -1.0, ALU.mult, ALU.mult))
                v.tensor_tensor(dh, dh, area("p_ret")[:, 0:512], ALU.add).then_inc(s["decay_arg"], 1)
                dve.wait_ge(s["decay_arg"], h + 1)

            def rotate_block(t, first, half, cos, sin):
                x = proj[:, t, first:first + 512].rearrange("p (g d) -> p g d", d=64)
                w = lambda c: const(c)[:, t * half:(t + 1) * half].unsqueeze(1).broadcast_to([P, 8, half])
                rotate(x[:, :, 0:half], x[:, :, half:2 * half], w(cos), w(sin),
                       lambda i: area("rot")[:, i * 256:i * 256 + 8 * half].rearrange("p (g d) -> p g d", d=half))

            for c in range(6):
                if c < HD:
                    decay_arg(c)
                dve.wait_ge(s["spent"], SLOT["w_in"] + 4 * (c + 1))
                v.tensor_copy(proj[:, 1, c * 512:(c + 1) * 512], bank[:, 2 * (c % 2) + 1, :]).then_inc(s["copied_dve"], 1)
                if c in (0, 1, 3):
                    dve.wait_ge(s["copied_dve"], c + 1)
                    dve.wait_ge(s["copied_act"], c + 1)
                    for t in range(TT):
                        if c < 2:
                            rotate_block(t, c * 512, 8, "cos_d", "sin_d")
                        else:
                            rotate_block(t, c * 512, 32, "cos_r", "sin_r")
            end(dve)
            begin(dve, 2)
            end(dve)
            begin(dve, 3)
            turned_out("qk", qk_t, 12)
            end(dve)
            begin(dve, 4)

            def diff_shift(u):
                dve.wait_ge(s["diff_scores"], u + 1)
                if u >= 2:
                    dve.wait_ge(s["diff_exp"], u - 1)
                link(v.tensor_reduce(sm[:, u % 2, 4:6], bank[:, 2 * (u % 2):2 * (u % 2) + 2, 0:T], AX, ALU.max))
                v.tensor_scalar(sm[:, u % 2, 0:2], sm[:, u % 2, 4:6], -0.125, None, ALU.mult).then_inc(s["diff_shift"], 1)

            def diff_mixed(u):
                dve.wait_ge(s["diff_exp"], u + 1)
                if u >= 2:
                    dve.wait_ge(s["diff_turned"], u - 1)
                link(v.reciprocal(sm[:, u % 2, 6:8], sm[:, u % 2, 2:4]))
                link(v.tensor_scalar(sm[:, u % 2, 8:9], sm[:, u % 2, 7:8], lam[:, 5:6], None, ALU.mult))
                link(v.tensor_scalar(e_diff[:, u % 2, 1, :], e_diff[:, u % 2, 1, :], sm[:, u % 2, 8:9], None, ALU.mult))
                v.scalar_tensor_tensor(out=a_diff[:, u % 2, :], in0=e_diff[:, u % 2, 0, :], scalar=sm[:, u % 2, 6:7],
                                       in1=e_diff[:, u % 2, 1, :], op0=ALU.mult, op1=ALU.add).then_inc(s["diff_mixed"], 1)

            diff_shift(0)
            diff_shift(1)
            diff_mixed(0)
            for u in range(8):
                h, t = u // 2, u % 2
                if u + 2 < 8:
                    diff_shift(u + 2)
                if u + 1 < 8:
                    diff_mixed(u + 1)
                dve.wait_ge(s["diff_out"], u + 1)
                v.tensor_copy(o_diff[:, t, h * P:(h + 1) * P], bank[:, 6 + u % 2, 0:P]).then_inc(s["diff_out_copied"], 1)
            end(dve)
            begin(dve, 5)
            for h in range(HD):
                dve.wait_ge(s["ret_scores"], h + 1)
                v.scalar_tensor_tensor(out=p_ret[:, h, :, :].rearrange("p j i -> p (j i)"), in0=bank[:, h % 2, :],
                                       scalar=0.125, in1=decay[:, h, :, :].rearrange("p j i -> p (j i)"),
                                       op0=ALU.mult, op1=ALU.mult).then_inc(s["ret_decayed"], 1)
            dve.wait_ge(s["ret_out"], HD)
            for t in range(TT):
                v.tensor_copy(o_ret[:, t, :], bank[:, 2 + t, :])
            end(dve)
            begin(dve, 6)
            stat = area("stat")
            by_head = lambda a: a.rearrange("p t (h c) -> p (t h) c", c=P)
            sq = area("rot", "p (g c) -> p g c", c=P)[:, 0:8, :]
            od, orr = by_head(o_diff), by_head(o_ret)
            link(v.tensor_tensor(sq, od, od, ALU.mult))
            link(v.tensor_reduce(stat[:, 0:8], sq, AX, ALU.add))
            v.tensor_scalar(stat[:, 8:16], stat[:, 0:8], 1.0 / P, EPS, ALU.mult, ALU.add).then_inc(s["head_mean"], 1)
            link(v.tensor_reduce(stat[:, 64:72], orr, AX, ALU.add))
            link(v.tensor_scalar(stat[:, 72:80], stat[:, 64:72], 1.0 / P, None, ALU.mult))
            link(v.tensor_tensor(orr, orr, stat[:, 72:80].unsqueeze(2).broadcast_to([P, 8, P]), ALU.subtract))
            link(v.tensor_tensor(sq, orr, orr, ALU.mult))
            link(v.tensor_reduce(stat[:, 32:40], sq, AX, ALU.add))
            v.tensor_scalar(stat[:, 40:48], stat[:, 32:40], 1.0 / P, EPS, ALU.mult, ALU.add).then_inc(s["head_mean"], 1)
            dve.wait_ge(s["head_root"], 1)
            link(v.reciprocal(stat[:, 24:32], stat[:, 16:24]))
            link(v.tensor_scalar(stat[:, 24:32], stat[:, 24:32], 1.0 - LAMBDA_INIT, None, ALU.mult))
            link(v.tensor_tensor(od, od, stat[:, 24:32].unsqueeze(2).broadcast_to([P, 8, P]), ALU.mult))
            for t in range(TT):
                v.tensor_tensor(mix[:, t, 0:512].rearrange("p (h c) -> p h c", c=P), od[:, 4 * t:4 * t + 4, :],
                                row("diff_g").unsqueeze(1).broadcast_to([P, HD, P]), ALU.mult)
            dve.wait_ge(s["head_root"], 2)
            link(v.reciprocal(stat[:, 56:64], stat[:, 48:56]))
            link(v.tensor_tensor(orr, orr, stat[:, 56:64].unsqueeze(2).broadcast_to([P, 8, P]), ALU.mult))
            for t in range(TT):
                link(v.tensor_tensor(o_ret[:, t, :], o_ret[:, t, :], row("ret_g"), ALU.mult))
                v.tensor_tensor(mix[:, t, 512:1024], o_ret[:, t, :], gate_r[:, t, :], ALU.mult)
            end(dve)
            begin(dve, 7)
            turned_lo("mix", h_t, KD)
            end(dve)
            begin(dve, 8)
            into_residual(SLOT["w_out"] + 8)
            end(dve)
            begin(dve, 9)
            norm(NORMS["ffn"], xres)
            turned_lo("ffn_norm", h_t, KD, lambda b: col("ffn_g", b))
            dve.wait_ge(s["mem_loaded"], 16)
            norm(NORMS["mem"], mem)
            turned_lo("norm_mem", mem_t, KD, lambda b: col("mem_g", b), bank0=4)
            end(dve)
            begin(dve, 10)
            vals = area("vals", "p (g c) -> p g c", c=TOPK)
            idx = area("idx", "p (g c) -> p g c", c=TOPK).bitcast(U32)
            spare = area("spare")
            sets = keys.rearrange("p t b (i c) -> p (t b i) c", c=NK)
            cand = area("cand", "p (g i j) -> p g i j", i=TOPK, j=TOPK)
            pairs = vals.rearrange("p (g s) c -> p g s c", s=2)
            best = area("best", "p (g c) -> p g c", c=TOPK)
            pos = area("pos", "p (g c) -> p g c", c=TOPK).bitcast(U32)

            def top16(values, top, index, rest):
                link(v.max(top[:, 0:8], values))
                v.max_index(index[:, 0:8], top[:, 0:8], values)
                link(v.match_replace(rest, top[:, 0:8], values, -3.0e38))
                link(v.max(top[:, 8:16], rest))
                v.max_index(index[:, 8:16], top[:, 8:16], rest)

            def choose(t, h):
                dve.wait_ge(s["keys_copied"], 2 * (h // 2) + t + 1)
                for i in range(2):
                    g = t * 2 * PH + 2 * h + i
                    top16(sets[:, g, :], vals[:, g, :], idx[:, g, :], spare[:, i * NK:(i + 1) * NK])
                g = t * PH + h
                link(v.tensor_tensor(cand[:, g, :, :], pairs[:, g, 0, :].unsqueeze(2).broadcast_to([P, TOPK, TOPK]),
                                     pairs[:, g, 1, :].unsqueeze(1).broadcast_to([P, TOPK, TOPK]), ALU.add))
                top16(cand[:, g, :, :].rearrange("p i j -> p (i j)"), best[:, g, :], pos[:, g, :], spare[:, 256:512])

            for b in range(4):
                for i in range(4):
                    j = 4 * b + i
                    if b:
                        choose(i // 2, 2 * (b - 1) + i % 2)
                    dve.wait_ge(s["split_act"], SPLIT["w_query"] + j + 1)
                    v.tensor_tensor(pq_t[1][:, j, :], bank[:, i, 0:T], pq_t[0][:, j, :].bitcast(F32), ALU.subtract)\
                        .then_inc(s["split_dve"], 1)
            end(dve)
            begin(dve, 11)
            for i in range(4):
                choose(i // 2, 6 + i % 2)
            dve.drain().then_inc(s["chosen_all"], 1)
            dve.wait_ge(s["chosen_all"], 1)
            link(v.tensor_copy(area("idxf"), area("idx").bitcast(U32)))
            hi_i, lo_i = area("hi").bitcast(U32), area("lo").bitcast(U32)
            posv = area("pos").bitcast(U32)
            link(v.tensor_scalar(hi_i, posv, 4, None, ALU.logical_shift_right))
            link(v.tensor_scalar(lo_i, posv, 15, None, ALU.bitwise_and))
            link(v.tensor_copy(area("hi"), hi_i))
            link(v.tensor_copy(area("lo"), lo_i))
            chosen = area("chosen", "p (f c) -> p f c", f=6)
            eq = area("eq", "p (k a) -> p k a", a=TOPK)
            idxf = area("idxf", "p (t h s a) -> p t h s a", t=TT, s=2, a=TOPK)
            iota16 = const("iota")[:, 0:TOPK].unsqueeze(1).broadcast_to([P, P, TOPK])
            for t in range(TT):
                for f, ch in enumerate(("hi", "lo")):
                    pick = area(ch)[:, t * P:(t + 1) * P].unsqueeze(2).broadcast_to([P, P, TOPK])
                    link(v.tensor_tensor(eq, pick, iota16, ALU.is_equal))
                    e4 = eq.rearrange("p (h k) a -> p h k a", h=PH)
                    link(v.tensor_tensor(e4, e4, idxf[:, t, :, f, :].unsqueeze(2).broadcast_to([P, PH, TOPK, TOPK]), ALU.mult))
                    link(v.tensor_reduce(chosen[:, 2 * f + t, :], eq, AX, ALU.add))
            gst = area("gst")
            for t in range(TT):
                bt = best[:, 8 * t:8 * t + 8, :]
                link(v.tensor_copy(gst[:, t * 8:t * 8 + 8], bt[:, :, 0:1].rearrange("p h o -> p (h o)")))
                v.tensor_tensor(bt, bt, gst[:, t * 8:t * 8 + 8].unsqueeze(2).broadcast_to([P, PH, TOPK]), ALU.subtract)\
                    .then_inc(s["gate_shifted"], 1)
            for t in range(TT):
                bt = best[:, 8 * t:8 * t + 8, :]
                dve.wait_ge(s["gate_exp"], t + 1)
                link(v.tensor_reduce(gst[:, 16 + t * 8:24 + t * 8], bt, AX, ALU.add))
                link(v.reciprocal(gst[:, 32 + t * 8:40 + t * 8], gst[:, 16 + t * 8:24 + t * 8]))
                link(v.tensor_tensor(chosen[:, 4 + t, :].rearrange("p (h k) -> p h k", h=PH), bt,
                                     gst[:, 32 + t * 8:40 + t * 8].unsqueeze(2).broadcast_to([P, PH, TOPK]), ALU.mult))
            signal("choice_made")
            turned_out("chosen", chosen_t, 3)
            end(dve)
            begin(dve, 12)
            iota4 = const("iota").unsqueeze(1).broadcast_to([P, 4, NK])
            one_hots = lambda b: work[:, b * 512:(b + 1) * 512].rearrange("p (t k) -> p t k", t=4)

            def compared(g, u):
                keys4 = chosen_t[:, 1, bass.ds(g * 4, 4)].unsqueeze(2).broadcast_to([P, 4, NK])
                v.tensor_tensor(one_hots(2 + u), iota4, keys4, ALU.is_equal).then_inc(s["one_hot_2"], 1)
                for i in range(4):
                    of = lambda f: chosen_t[:, f, bass.ds(g * 4 + i, 1)]
                    v.tensor_scalar(one_hots(u)[:, i, :], const("iota"), of(0), of(2), ALU.is_equal, ALU.mult)\
                        .then_inc(s["one_hot_1"], 1)

            compared(0, 0)
            compared(1, 1)
            with dve.Fori(1, T // 8) as r:
                for u in range(2):
                    dve.wait_ge(s["spread"], r * 2 + (u - 1))
                    compared(r * 2 + u, u)
            end(dve)
            begin(dve, 13)
            X = SLOT["experts"]
            U3 = 3

            def weigh(k, u, before, spent=None):
                dve.wait_ge(s["gelu_done"], k + 1)
                g = gates[:, bass.ds(k, 1), :].rearrange("p a t -> p (a t)")
                a = work[:, u * T:(u + 1) * T]
                v.tensor_tensor(a, a, g, ALU.mult).then_inc(s["act_product"], 1)
                dve.wait_ge(s["act_product"], before + 1)
                if spent is not None:
                    dve.wait_ge(s["spent"], spent)
                v.tensor_copy(act_t[0][:, u, :], a).then_inc(s["act_hi_made"], 1)
                dve.wait_ge(s["act_hi_made"], before + 1)
                v.tensor_tensor(act_t[1][:, u, :], a, act_t[0][:, u, :].bitcast(F32), ALU.subtract).then_inc(s["weighed"], 1)

            for k in range(3):
                weigh(k, k, k)
            with dve.Fori(1, NK // U3) as r:
                for u in range(U3):
                    weigh(r * U3 + u, u, r * U3 + u, r * (2 * U3) + (X + 2 * u - 3))
            for k in range(NK // U3 * U3, NK):
                weigh(k, k % U3, k, X + 2 * k - 3)
            end(dve)
            begin(dve, 14)
            into_residual(X + 2 * NK)
            signal("residual_ready")
            norm(NORMS["final1"], xres)
            dve.wait_ge(s["norm_scaled"], 2 * NORMS["final1"] + 2)
            dve.wait_ge(s["gain_loaded"], 16)
            for t in range(TT):
                v.tensor_tensor(xres[:, t, :], x_scaled[:, t, :], area("final_g"), ALU.mult)
            end(dve)
            begin(dve, 15)
            norm(NORMS["mix"], xres)
            turned_lo("norm_mix", h_t, KD, lambda b: col("mix_g", b))
            end(dve)
            begin(dve, 16)
            by_tokens("z", KD, [512, 512], z)
            by_tokens("dt_q", KD, [DTQ], lat)
            end(dve)
            begin(dve, 17)
            dve.wait_ge(s["spent"], SLOT["kv_rope"] + 4)
            v.tensor_copy(lat[:, 1, 512:512 + KVR], bank[:, 1, 0:KVR]).then_inc(s["copied_dve"], 1)
            end(dve)
            begin(dve, 18)
            for j in range(16):
                dve.wait_ge(s["spent"], SLOT["xbc"] + j + 1)
                b = bank[:, j % 4, :]
                v.tensor_scalar(xc[:, j, :], b[:, 0:T], col("xw", 4 * j + 3), col("xb", j), ALU.mult, ALU.add)\
                    .then_inc(s["conv_done"], 1)
                for d in range(1, 4):
                    dve.wait_ge(s["conv_done"], 4 * j + d)
                    v.scalar_tensor_tensor(out=xc[:, j, d:T], in0=b[:, 0:T - d], scalar=col("xw", 4 * j + 3 - d),
                                           in1=xc[:, j, d:T], op0=ALU.mult, op1=ALU.add).then_inc(s["conv_done"], 1)
            end(dve)
            begin(dve, 19)
            dts = area("dts")
            t2 = lambda a: dts[:, a:a + 32].rearrange("p (t h) -> p t h", t=TT)
            wide = lambda r_: row(r_).unsqueeze(1).broadcast_to([P, TT, 16])
            link(v.tensor_tensor(t2(32), lat[:, :, 0:16], wide("dt_bias"), ALU.add))
            link(v.scalar_tensor_tensor(out=dts[:, 64:96], in0=dts[:, 32:64], scalar=-1.0, in1=dts[:, 32:64],
                                        op0=ALU.mult, op1=ALU.max))
            signal("dt_arg")
            dve.wait_ge(s["dt_l"], 2)
            link(v.scalar_tensor_tensor(out=dts[:, 32:64], in0=dts[:, 32:64], scalar=0.0, in1=dts[:, 128:160],
                                        op0=ALU.max, op1=ALU.add))
            link(v.tensor_scalar(dts[:, 160:176], dts[:, 160:176], -1.0, None, ALU.mult))
            v.tensor_tensor(t2(0), t2(32), dts[:, 160:176].unsqueeze(1).broadcast_to([P, TT, 16]), ALU.mult)\
                .then_inc(s["dt_scaled"], 1)
            for k in range(1, 4, 2):
                dve.wait_ge(s["turned"], TURN["xs"][0] + k + 1)
                t, b = k // 2, k % 2
                v.tensor_copy(xs[:, t, b * 512:(b + 1) * 512], bank[:, k, :]).then_inc(s["turned_out_dve"], 1)
            dve.wait_ge(s["turned_out_act"], TURN["xs"][1] + 2)
            dve.wait_ge(s["turned_out_dve"], TURN["xs"][2] + 2)
            for t in range(TT):
                v.tensor_tensor(xdt[:, t, :].rearrange("p (h c) -> p h c", c=64),
                                xs[:, t, :].rearrange("p (h c) -> p h c", c=64),
                                t2(32)[:, t, :].unsqueeze(2).broadcast_to([P, SH, 64]), ALU.mult)
            dve.wait_ge(s["tri_loaded"], 16)
            for g in range(SG):
                dve.wait_ge(s["cb_done"], g + 1)
                v.tensor_tensor(cb[:, g, :, :].rearrange("p j l -> p (j l)"), bank[:, 4 + g % 2, :], const("tri"), ALU.mult)\
                    .then_inc(s["cb_masked"], 1)
            dve.wait_ge(s["cum_done"], 1)
            v.tensor_copy(dts[:, 64:96], bank[:, 6, 0:32])
            end(dve)
            begin(dve, 20)

            def clip(h):
                dve.wait_ge(s["seg_sum"], h + 1)
                if h >= 4:
                    dve.wait_ge(s["ssd_out"], h - 3)
                for st in range(TT):
                    v.tensor_scalar(seg[:, h % 4, 2 * P * st:2 * P * st + (2 - st) * P], bank[:, h % 4, st * P:T],
                                    dts[:, 64 + st * 16 + h:65 + st * 16 + h], 0.0, ALU.subtract, ALU.min)\
                        .then_inc(s["seg_clipped"], 1)

            clip(0)
            clip(1)
            for h in range(SH):
                if h + 2 < SH:
                    clip(h + 2)
                dve.wait_ge(s["seg_exp"], h + 1)
                g = h // 4
                for st in range(TT):
                    sl = seg[:, h % 4, 2 * P * st:2 * P * st + (2 - st) * P]
                    v.tensor_tensor(sl, sl, cb[:, g, st, st * P:T], ALU.mult).then_inc(s["seg_weighed"], 1)
            end(dve)
            begin(dve, 21)
            for t in range(TT):
                link(v.tensor_tensor(xs[:, t, :].rearrange("p (h c) -> p h c", c=64),
                                     xs[:, t, :].rearrange("p (h c) -> p h c", c=64),
                                     row("d_skip").unsqueeze(2).broadcast_to([P, SH, 64]), ALU.mult))
                link(v.tensor_tensor(y[:, t, 0:512], xs[:, t, 0:512], bank[:, 4 + 2 * t, :], ALU.add))
                link(v.tensor_tensor(y[:, t, 512:1024], xs[:, t, 512:1024], bank[:, 5 + 2 * t, :], ALU.add))
                link(v.tensor_tensor(y[:, t, :], y[:, t, :], z[:, t, :], ALU.mult))
                link(v.tensor_tensor(xs[:, t, :], y[:, t, :], y[:, t, :], ALU.mult))
                link(v.tensor_reduce(dts[:, 192 + 4 * t:196 + 4 * t], xs[:, t, :].rearrange("p (g c) -> p g c", c=256), AX, ALU.add))
            v.tensor_scalar(dts[:, 200:208], dts[:, 192:200], 1.0 / 256, EPS, ALU.mult, ALU.add).then_inc(s["group_mean"], 1)
            dve.wait_ge(s["group_root"], 1)
            link(v.reciprocal(dts[:, 192:200], dts[:, 208:216]))
            for t in range(TT):
                yg = y[:, t, :].rearrange("p (g c) -> p g c", c=256)
                v.tensor_tensor(yg, yg, dts[:, 192 + 4 * t:196 + 4 * t].unsqueeze(2).broadcast_to([P, SG, 256]), ALU.mult)
            end(dve)
            begin(dve, 22)
            turned_lo("ssd", h_t, KD, lambda b: col("ssd_g", b))
            end(dve)
            begin(dve, 23)
            ql, kl = lat[:, :, 16:400], lat[:, :, 512:768]
            sq1 = area("squares")[:, 0:768].rearrange("p (t c) -> p t c", t=TT)
            sq2 = area("x_scaled")[:, 0:512].rearrange("p (t c) -> p t c", t=TT)
            v.tensor_tensor(sq1, ql, ql, ALU.mult)
            link(v.tensor_tensor(sq2, kl, kl, ALU.mult))
            v.tensor_reduce(dts[:, 192:194], sq1, AX, ALU.add)
            link(v.tensor_reduce(dts[:, 194:196], sq2, AX, ALU.add))
            link(v.tensor_scalar(dts[:, 200:202], dts[:, 192:194], 1.0 / 384, EPS, ALU.mult, ALU.add))
            v.tensor_scalar(dts[:, 202:204], dts[:, 194:196], 1.0 / 256, EPS, ALU.mult, ALU.add).then_inc(s["group_mean"], 1)
            dve.wait_ge(s["group_root"], 2)
            link(v.reciprocal(dts[:, 192:196], dts[:, 208:212]))
            for t in range(TT):
                link(v.tensor_scalar(ql[:, t, :], ql[:, t, :], dts[:, 192 + t:193 + t], None, ALU.mult))
                link(v.tensor_scalar(kl[:, t, :], kl[:, t, :], dts[:, 194 + t:195 + t], None, ALU.mult))
            signal("latents_scaled")
            rope = area("rope")
            link(v.tensor_copy(rope[:, 0:2], pos_i[:, :]))
            for t in range(TT):
                link(v.tensor_scalar(rope[:, 32 + t * 16:48 + t * 16], const("inv_m"), rope[:, t:t + 1], None, ALU.mult))
            ang = rope[:, 32:64]
            BIG = 12582912.0
            for i, shift in enumerate((0.0, 0.25)):
                turns = rope[:, 64 + 32 * i:96 + 32 * i]
                r_ = rope[:, 128 + 32 * i:160 + 32 * i]
                link(v.tensor_scalar(turns, ang, 0.15915494309189535, shift, ALU.mult, ALU.add))
                link(v.tensor_scalar(turns, turns, BIG, None, ALU.add))
                link(v.tensor_scalar(turns, turns, BIG, None, ALU.subtract))
                link(v.scalar_tensor_tensor(out=r_, in0=turns, scalar=-6.28125, in1=ang, op0=ALU.mult, op1=ALU.add))
                link(v.scalar_tensor_tensor(out=r_, in0=turns, scalar=-0.0019340515136718750, in1=r_, op0=ALU.mult, op1=ALU.add))
                link(v.scalar_tensor_tensor(out=r_, in0=turns, scalar=-1.2556659146e-06, in1=r_, op0=ALU.mult, op1=ALU.add))
                if i:
                    link(v.tensor_scalar(r_, r_, 1.5707963267948966, None, ALU.add))
                link(v.tensor_scalar(r_, r_, 3.1415925, -3.1415925, ALU.min, ALU.max))
            signal("trig_arg")
            turned_lo("latents", lat_t, 5, lambda b: col("q_g", b) if b < 3 else col("kv_g", b - 3))
            end(dve)
            begin(dve, 24)
            by_tokens("q_up", 3, [512] * 3, q)
            by_tokens("kv_up", 2, [512] * 4, kv)
            end(dve)
            begin(dve, 25)
            xsc = area("x_scaled")
            for t in range(TT):
                sin = rope[:, 192 + t * 16:208 + t * 16]
                cos = rope[:, 224 + t * 16:240 + t * 16]
                qh = q[:, t, :].rearrange("p (h c) -> p h c", c=MQ)
                w16 = lambda a: a.unsqueeze(1).broadcast_to([P, MH, 16])
                rotate(qh[:, :, 64:80], qh[:, :, 80:96], w16(cos), w16(sin),
                       lambda i: xsc[:, i * 256:(i + 1) * 256].rearrange("p (h c) -> p h c", c=16))
                rotate(lat[:, t, 768:784], lat[:, t, 784:800], cos, sin, lambda i: xsc[:, 1024 + i * 16:1040 + i * 16])
                kc = kcat[:, t, :].rearrange("p (h c) -> p h c", c=MQ)
                v.tensor_copy(kc[:, :, 0:64], kv[:, t, :].rearrange("p (h c) -> p h c", c=128)[:, :, 0:64])
                v.tensor_copy(kc[:, :, 64:96], lat[:, t, 768:800].unsqueeze(1).broadcast_to([P, MH, 32]))
            end(dve)
            begin(dve, 26)
            turned_out("mla_q", q_t, MH, rows_=MQ)
            end(dve)
            begin(dve, 27)
            turned_out("mla_k", k_t, MH, rows_=MQ)
            end(dve)
            begin(dve, 28)
            dve.wait_ge(s["mask_loaded"], 16)
            mask = const("mask").rearrange("p (t k) -> p t k", t=TT)

            def mla_shift(u):
                t = u % 2
                w = (t + 1) * P
                dve.wait_ge(s["mla_scores"], u + 1)
                if u >= 2:
                    dve.wait_ge(s["mla_exp"], u - 1)
                link(v.scalar_tensor_tensor(out=s_m[:, u % 2, 0:w], in0=bank[:, u % 2, 0:w], scalar=float(MQ) ** -0.5,
                                            in1=mask[:, t, 0:w], op0=ALU.mult, op1=ALU.add))
                v.tensor_reduce(sm[:, u % 2, 0:1], s_m[:, u % 2, 0:w], AX, ALU.max, negate=True).then_inc(s["mla_shift"], 1)

            mla_shift(0)
            mla_shift(1)
            for u in range(2 * MH):
                h, t = u // 2, u % 2
                dve.wait_ge(s["mla_exp"], u + 1)
                link(v.reciprocal(sm[:, u % 2, 2:3], sm[:, u % 2, 1:2]))
                if u + 2 < 2 * MH:
                    mla_shift(u + 2)
                dve.wait_ge(s["mla_out"], u + 1)
                v.tensor_scalar(o_m[:, t, h * 64:(h + 1) * 64], bank[:, 4 + u % 2, 0:MV], sm[:, u % 2, 2:3], None, ALU.mult)\
                    .then_inc(s["mla_out_copied"], 1)
            end(dve)
            begin(dve, 29)
            turned_lo("mla_out", m_t, KD)
            end(dve)
            begin(dve, 30)
            into_residual(SLOT["w_out_2"] + 16)
            end(dve)
            begin(dve, 31)
            norm(NORMS["memx"], xres)
            turned_lo("norm_memx", h_t, KD, lambda b: col("memx_g", b))
            end(dve)
            begin(dve, 32)
            by_channels("mem_q", 8, mq_t)
            end(dve)
            begin(dve, 33)

            def mem_shift(u):
                dve.wait_ge(s["mem_scores"], u + 1)
                if u >= 2:
                    dve.wait_ge(s["mem_exp"], u - 1)
                link(v.tensor_reduce(sm[:, u % 2, 3:4], bank[:, u % 2, 0:T], AX, ALU.max))
                v.tensor_scalar(sm[:, u % 2, 0:1], sm[:, u % 2, 3:4], -0.0625, None, ALU.mult).then_inc(s["mem_shift"], 1)

            def mem_scaled(u):
                dve.wait_ge(s["mem_exp"], u + 1)
                link(v.reciprocal(sm[:, u % 2, 2:3], sm[:, u % 2, 1:2]))
                v.tensor_scalar(e_x[:, u % 2, :], e_x[:, u % 2, :], sm[:, u % 2, 2:3], None, ALU.mult).then_inc(s["mem_scaled"], 1)

            mem_shift(0)
            mem_shift(1)
            mem_scaled(0)
            for u in range(8):
                h, t = u // 2, u % 2
                if u + 2 < 8:
                    mem_shift(u + 2)
                if u + 1 < 8:
                    mem_scaled(u + 1)
                if t == 1:
                    dve.wait_ge(s["mem_hi_made"], h + 1)
                    v.tensor_tensor(h_t[1][:, 2 * h:2 * h + 2, :], bank[:, 4 + h % 2, :].rearrange("p (e t) -> p e t", e=2),
                                    h_t[0][:, 2 * h:2 * h + 2, :].bitcast(F32), ALU.subtract)\
                        .then_inc(s["mem_out_copied"], 1)
            end(dve)
            begin(dve, 34)
            into_residual(SLOT["mem_o"] + 8)
            end(dve)
            begin(dve, 35)
            norm(NORMS["ffn2"], xres)
            turned_lo("norm_ffn", h_t, KD, lambda b: col("ffn2_g", b))
            end(dve)
            begin(dve, 36)
            F = SLOT["ffn"]

            def ffn_filter(k, u, half, dst, name, count):
                b = bank[:, 4 + 2 * u + half, :]
                c0 = COL["fw"][0] + half * 66
                w = lambda d: cols[:, bass.ds(k * 3 + (c0 + 2 - d), 1)]
                v.tensor_scalar(dst, b[:, 0:T], w(0), cols[:, bass.ds(k + (COL["fb"][0] + half * 22), 1)], ALU.mult, ALU.add)\
                    .then_inc(s["filter_step"], 1)
                dve.wait_ge(s["filter_step"], count)
                v.scalar_tensor_tensor(out=dst[:, 1:T], in0=b[:, 0:T - 1], scalar=w(1), in1=dst[:, 1:T],
                                       op0=ALU.mult, op1=ALU.add).then_inc(s["filter_step"], 1)
                dve.wait_ge(s["filter_step"], count + 1)
                v.scalar_tensor_tensor(out=dst[:, 2:T], in0=b[:, 0:T - 2], scalar=w(2), in1=dst[:, 2:T],
                                       op0=ALU.mult, op1=ALU.add).then_inc(s[name], 1)

            def ffn_block(k, u, spent, r4, down_spent):
                dve.wait_ge(s["spent"], spent)
                ffn_filter(k, u, 0, gate_f[:, u, :], "ffn_conv_g", r4 + 1)
                dve.wait_ge(s["spent"], spent + 1)
                ffn_filter(k, u, 1, value_f[:, u, :], "ffn_conv_v", r4 + 3)
                dve.wait_ge(s["ffn_silu"], k + 1)
                dve.wait_ge(s["ffn_conv_v"], k + 1)
                v.tensor_tensor(gate_f[:, u, :], gate_f[:, u, :], value_f[:, u, :], ALU.mult).then_inc(s["act_product"], 1)
                dve.wait_ge(s["act_product"], k + (NK + 1))
                if down_spent is not None:
                    dve.wait_ge(s["spent"], down_spent)
                v.tensor_copy(act_t[0][:, u, :], gate_f[:, u, :]).then_inc(s["act_hi_made"], 1)
                dve.wait_ge(s["act_hi_made"], k + (NK + 1))
                v.tensor_tensor(act_t[1][:, u, :], gate_f[:, u, :], act_t[0][:, u, :].bitcast(F32), ALU.subtract)\
                    .then_inc(s["ffn_act"], 1)

            gate_f = area("gate_f", "p (b t) -> p b t", t=T)
            value_f = area("value_f", "p (b t) -> p b t", t=T)
            ffn_block(0, 0, F + 1, 0, None)
            ffn_block(1, 1, F + 3, 4, None)
            with dve.Fori(1, FF // 2) as r:
                for u in range(2):
                    k = r * 2 + u
                    ffn_block(k, u, r * 6 + (F + 3 * u), r * 8 + 4 * u, r * 6 + (F + 3 * u - 1))
            end(dve)
            begin(dve, 37)
            into_residual(F + 3 * FF)
            signal("residual_ready")
            norm(NORMS["final2"], xres)
            dve.wait_ge(s["norm_scaled"], 2 * NORMS["final2"] + 2)
            dve.wait_ge(s["gain_loaded"], 32)
            for t in range(TT):
                v.tensor_tensor(out_sb[:, t, :], x_scaled[:, t, :], area("final_g"), ALU.mult).then_inc(s["norm_scaled"], 1)


def lay_out(i):
    a = {k: np.asarray(v) for k, v in i.items()}
    z = lambda *shape: np.zeros(shape, np.float32)

    def panels(w):
        K, C = w.shape
        wide = -(-C // 512) * 512
        if wide > C:
            w = np.concatenate([w, z(K, wide - C)], axis=1)
        p = w.reshape(K // P, P, wide // 512, 512).transpose(2, 0, 1, 3).reshape(-1, P, 512)
        if len(p) % 2:
            p = np.concatenate([p, z(1, P, 512)])
        return p.reshape(-1, 2, P, 512).transpose(0, 2, 1, 3).reshape(-1, P, 1024)

    def channels(w):
        return w.reshape(KD, P, -1, P).transpose(2, 1, 0, 3).reshape(-1, P, 1024)

    def deep(w):
        return w.reshape(-1, P, D)

    def interleave(ahead, *parts):
        n = len(parts[-1])
        out = [p[0:1] for p in parts[:-1]]
        for k in range(n):
            if k + 1 < n:
                out += [p[k + 1:k + 2] for p in parts[:-1]]
            out.append(parts[-1][k:k + 1])
        return np.concatenate(out)

    w2 = a["w_in_2"][0]
    sub = a["peer_sub_keys"][0].transpose(3, 0, 1, 2).reshape(P, 4, 1, 512).transpose(1, 2, 0, 3)
    sub = np.concatenate([sub, z(4, 1, P, 512)], axis=3)
    queries = np.concatenate([channels(a["peer_w_query"][0]).reshape(4, 4, P, 1024), sub], axis=1).reshape(20, P, 1024)
    ffn = channels(a["w_ffn_up_2"][0])
    order = [panels(a["w_in"][0]), deep(a["w_out"][0]), queries,
             channels(a["w_mem_k_2"][0]), panels(a["w_mem_v_2"][0]),
             interleave(1, a["peer_u"][0].reshape(NK, NK, KD, P).transpose(0, 3, 2, 1).reshape(NK, P, 1024),
                        a["peer_v"][0].reshape(NK, P, D)),
             panels(w2[:, 0:1024]), panels(w2[:, 3072:3072 + DTQ]), panels(w2[:, 3072 + DTQ:]),
             channels(w2[:, 1024:3072]), panels(a["mla_w_q_up_2"][0]), panels(a["mla_w_kv_up_2"][0]),
             deep(a["w_out_2"][0]),
             channels(a["w_mem_q_2"][0]), deep(a["w_mem_o_2"][0]),
             interleave(1, ffn[:FF], ffn[FF:], deep(a["w_ffn_down_2"][0]))]
    assert [len(o) for o in order] == [n for _, n in STAGES]
    by_part = lambda v: v.reshape(-1, P).T
    taps = lambda v: v.reshape(v.shape[0], -1, P).transpose(2, 1, 0).reshape(P, -1)
    cols = [by_part(a[n].reshape(-1)) for n in ("attn_norm_g", "ffn_norm_g", "norm_mix_w_2", "norm_mem_w_2", "norm_memx_w_2",
                                                "norm_ffn_w_2", "ssd_norm_w_2", "mla_q_norm_w_2", "mla_kv_norm_w_2")]
    cols += [taps(a["ssd_conv_w_2"][0]), by_part(a["ssd_conv_b_2"].reshape(-1)),
             taps(a["ffn_conv_w_2"][0]), by_part(a["ffn_conv_b_2"].reshape(-1))]
    rows = np.concatenate([a[n].reshape(-1) for n in ("diff_norm_g", "ret_norm_g", "diff_lambda", "ret_log_decay", "ssd_dt_bias_2",
                                                      "ssd_a_log_2", "ssd_d_2", "final_norm_g", "norm_final_w_2")])
    by_token = lambda v: np.ascontiguousarray(v.reshape(TT, P, -1).transpose(1, 0, 2))
    return {
        "weights": np.concatenate(order),
        "consts": CONST,
        "cols": np.ascontiguousarray(np.concatenate(cols, axis=1)),
        "rows": np.ascontiguousarray(np.broadcast_to(rows, (P, len(rows)))),
        "x": by_token(a["x"]),
        "mem": by_token(a["mem_2"]),
        "positions": np.ascontiguousarray(a["positions_2"].reshape(TT, P).T),
    }


def kernel(**inputs):
    import concourse.bacc as bacc
    from concourse.bass_utils import run_bass_kernel_spmd

    arrays = lay_out(inputs)
    nc = bacc.Bacc("TRN2", target_bir_lowering=False, num_devices=1)
    args = [nc.dram_tensor(name + "_in", v.shape, mybir.dt.from_np(v.dtype), kind="ExternalInput").ap()
            for name, v in arrays.items()]
    out = nc.dram_tensor("out", (P, TT, D), F32, kind="ExternalOutput").ap()
    two_blocks(nc, *args, out)
    r = run_bass_kernel_spmd(nc, [{n + "_in": v for n, v in arrays.items()}], core_ids=[0])
    got = r.results[0]["out"]
    return got.transpose(1, 0, 2).reshape(1, T, D)
```
